# Optimizing a Trainium2 kernel written in Bass

```python
import math
import jax, jax.numpy as jnp
from jax import lax
import numpy as np

D_MODEL = 1024
BATCH = 1
SEQ = 512
DEPTH = 2
DEC_BATCH = 1
DEC_SEQ = 64
PAST_LEN = 512

F32 = jnp.float32
CHUNK = 64
N_EVEN = (DEPTH + 1) // 2
N_ODD = DEPTH // 2
EPS = 1e-6
A_HEADS = 4
A_DK = D_MODEL // A_HEADS
A_DV = D_MODEL // A_HEADS
A_QK = A_HEADS * A_DK
A_W = A_HEADS * A_DV
B_HEADS = 4
B_DK = D_MODEL // B_HEADS
B_DV = D_MODEL // B_HEADS
B_QK = B_HEADS * B_DK
B_W = B_HEADS * B_DV
ROPE_BASE = 10000.0
C_HEADS = 4
C_DK = D_MODEL // 2 // C_HEADS
C_DV = D_MODEL // C_HEADS
C_QK = C_HEADS * C_DK
C_W = C_HEADS * C_DV
C_RANK = 16
C_TAU = 16.0
D_DK = 128
D_DV = 128
D_HEADS = D_MODEL // D_DK
D_QK = D_HEADS * D_DK
D_W = D_HEADS * D_DV
CONV_W = 4
CONV_CH = 2 * D_QK + D_W
EVEN_IN = 2 * A_QK + 2 * A_W + 2 * B_QK + B_W + A_W + B_W + 2 * A_HEADS
ODD_IN = 2 * C_QK + C_W + C_RANK + 2 * D_QK + D_W + 2 * D_HEADS + C_W + D_W

kernel_name = 'hybrid_stream_mlstm_ret_gla_gdn'

def _split(t, sizes):
    return jnp.split(t, [int(s) for s in np.cumsum(sizes)[:-1]], axis=-1)

def _heads(t, n_heads):
    return t.astype(F32).reshape(t.shape[0], t.shape[1], n_heads, -1)

def _rmsnorm(x, g):
    xf = x.astype(F32)
    return xf * lax.rsqrt(jnp.mean(xf * xf, axis=-1, keepdims=True) + EPS) * g

def _head_rmsnorm(o):
    o = o * lax.rsqrt(jnp.mean(o * o, axis=-1, keepdims=True) + EPS)
    return o.reshape(o.shape[0], o.shape[1], -1)

def _l2norm(x):
    return x * lax.rsqrt(jnp.sum(x * x, axis=-1, keepdims=True) + EPS)

def _rope(x, pos):
    half = x.shape[-1] // 2
    inv = ROPE_BASE ** (-jnp.arange(half, dtype=F32) / half)
    ang = pos[:, None] * inv[None, :]
    cos = jnp.cos(ang)[None, :, None, :]
    sin = jnp.sin(ang)[None, :, None, :]
    x1, x2 = x[..., :half], x[..., half:]
    return jnp.concatenate([x1 * cos - x2 * sin, x1 * sin + x2 * cos], axis=-1)

def _chunk_len(T):
    if T % CHUNK == 0:
        return CHUNK
    return T if T < CHUNK else math.gcd(T, CHUNK)

def _to_chunks(t, cs):
    b, T, h = t.shape[:3]
    t = t.reshape((b, T // cs, cs, h) + t.shape[3:])
    return jnp.moveaxis(t, (1, 3), (0, 2))

def _from_chunks(o):
    o = jnp.moveaxis(o, (0, 2), (1, 3))
    return o.reshape(o.shape[0], o.shape[1] * o.shape[2], o.shape[3], o.shape[4])

def _mlstm_chunked(q, k, v, i_pre, log_f, C0, n0, m0):
    T = q.shape[1]
    cs = _chunk_len(T)
    causal = jnp.tril(jnp.ones((cs, cs), dtype=bool))
    qc, kc, vc = (_to_chunks(t, cs) for t in (q, k, v))
    ic = _to_chunks(i_pre, cs)
    b = jnp.cumsum(_to_chunks(log_f, cs), axis=-1)
    dmat = jnp.where(causal, b[..., :, None] - b[..., None, :] + ic[..., None, :], -jnp.inf)
    dmax = jnp.max(dmat, axis=-1)
    qk = jnp.einsum('nbhtd,nbhsd->nbhts', qc, kc)
    g_end = b[..., -1:] - b + ic

    def step(carry, inp):
        C, n, m = carry
        q_c, k_c, v_c, b_c, d_c, dmx_c, qk_c, ge_c = inp
        inter = b_c + m[..., None]
        m_t = jnp.maximum(inter, dmx_c)
        s = qk_c * jnp.exp(d_c - m_t[..., None])
        w_inter = jnp.exp(inter - m_t)
        num = jnp.einsum('bhts,bhsv->bhtv', s, v_c) + w_inter[..., None] * jnp.einsum('bhtd,bhdv->bhtv', q_c, C)
        den = jnp.sum(s, axis=-1) + w_inter * jnp.einsum('bhtd,bhd->bht', q_c, n)
        h = num / jnp.maximum(jnp.abs(den), jnp.exp(-m_t))[..., None]
        m_new = m_t[..., -1]
        kw = k_c * jnp.exp(ge_c - m_new[..., None])[..., None]
        dec = jnp.exp(b_c[..., -1] + m - m_new)
        C = dec[..., None, None] * C + jnp.einsum('bhsd,bhsv->bhdv', kw, v_c)
        n = dec[..., None] * n + jnp.sum(kw, axis=2)
        return (C, n, m_new), h

    init = (C0.astype(F32), n0.astype(F32), m0.astype(F32))
    (C, n, m), h = lax.scan(step, init, (qc, kc, vc, b, dmat, dmax, qk, g_end))
    return _from_chunks(h), C, n, m

def _retention_chunked(q, k, v, S0):
    T = q.shape[1]
    cs = _chunk_len(T)
    lg = jnp.log(1.0 - 2.0 ** (-5.0 - jnp.arange(B_HEADS, dtype=F32)))
    t = jnp.arange(cs, dtype=F32)
    causal = jnp.tril(jnp.ones((cs, cs), dtype=bool))
    diff = jnp.maximum(t[:, None] - t[None, :], 0.0)
    dec_intra = jnp.where(causal[None], jnp.exp(diff[None] * lg[:, None, None]), 0.0)
    q_dec = jnp.exp((t + 1.0)[None, :] * lg[:, None])
    k_dec = jnp.exp((cs - 1.0 - t)[None, :] * lg[:, None])
    c_dec = jnp.exp(cs * lg)
    qc, kc, vc = (_to_chunks(x, cs) for x in (q, k, v))
    o_intra = jnp.einsum('nbhts,nbhsv->nbhtv', jnp.einsum('nbhtd,nbhsd->nbhts', qc, kc) * dec_intra, vc)
    qd = qc * q_dec[..., None]
    kd = kc * k_dec[..., None]

    def step(S, inp):
        q_c, k_c, v_c = inp
        o = jnp.einsum('bhtd,bhdv->bhtv', q_c, S)
        S = c_dec[:, None, None] * S + jnp.einsum('bhsd,bhsv->bhdv', k_c, v_c)
        return S, o

    S, o_inter = lax.scan(step, S0.astype(F32), (qd, kd, vc))
    return _from_chunks(o_intra + o_inter), S

def _gla_chunked(q, k, v, log_a, S0):
    T = q.shape[1]
    cs = _chunk_len(T)
    causal = jnp.tril(jnp.ones((cs, cs), dtype=bool))
    qc, kc, vc = (_to_chunks(x, cs) for x in (q, k, v))
    b = jnp.cumsum(_to_chunks(log_a, cs), axis=3)
    q_t = qc * jnp.exp(b)
    k_t = kc * jnp.exp(-b)
    s = jnp.where(causal, jnp.einsum('nbhtd,nbhsd->nbhts', q_t, k_t), 0.0)
    o_intra = jnp.einsum('nbhts,nbhsv->nbhtv', s, vc)
    b_last = b[..., -1:, :]
    k_end = kc * jnp.exp(b_last - b)
    a_end = jnp.exp(b_last[..., 0, :])

    def step(S, inp):
        q_c, k_c, v_c, a_c = inp
        o = jnp.einsum('bhtd,bhdv->bhtv', q_c, S)
        S = a_c[..., None] * S + jnp.einsum('bhsd,bhsv->bhdv', k_c, v_c)
        return S, o

    S, o_inter = lax.scan(step, S0.astype(F32), (q_t, k_end, vc, a_end))
    return _from_chunks(o_intra + o_inter), S

def _gdn_chunked(q, k, v, g, beta, S0):
    T = q.shape[1]
    cs = _chunk_len(T)
    dv = v.shape[-1]
    causal = jnp.tril(jnp.ones((cs, cs), dtype=bool))
    strict = jnp.tril(jnp.ones((cs, cs), dtype=bool), -1)
    qc, kc, vc = (_to_chunks(x, cs) for x in (q, k, v))
    G = jnp.cumsum(_to_chunks(g, cs), axis=-1)
    bc = _to_chunks(beta, cs)[..., None]
    gam = jnp.exp(jnp.where(causal, G[..., :, None] - G[..., None, :], -jnp.inf))
    kb = kc * bc
    a_mat = jnp.where(strict, jnp.einsum('nbhtd,nbhsd->nbhts', kb, kc) * gam, 0.0)
    eye = jnp.eye(cs, dtype=F32)
    rhs = jnp.concatenate([vc * bc, kb * jnp.exp(G)[..., None]], axis=-1)
    sol = lax.linalg.triangular_solve(a_mat + eye, rhs, left_side=True, lower=True, unit_diagonal=True)
    u0, w = sol[..., :dv], sol[..., dv:]
    attn = jnp.einsum('nbhtd,nbhsd->nbhts', qc, kc) * gam
    qg = qc * jnp.exp(G)[..., None]
    kg = kc * jnp.exp(G[..., -1:] - G)[..., None]
    g_last = jnp.exp(G[..., -1])

    def step(S, inp):
        u0_c, w_c, qg_c, at_c, kg_c, gl_c = inp
        u = u0_c - jnp.einsum('bhtd,bhdv->bhtv', w_c, S)
        o = jnp.einsum('bhtd,bhdv->bhtv', qg_c, S) + jnp.einsum('bhts,bhsv->bhtv', at_c, u)
        S = gl_c[..., None, None] * S + jnp.einsum('bhsd,bhsv->bhdv', kg_c, u)
        return S, o

    S, o = lax.scan(step, S0.astype(F32), (u0, w, qg, attn, kg, g_last))
    return _from_chunks(o), S

def _even_mixer(h, pos, w_in, b_if, g_head, w_out, C0, n0, m0, S0):
    sizes = [A_QK, A_QK, A_W, A_W, B_QK, B_QK, B_W, A_W, B_W, 2 * A_HEADS]
    qa, ka, va, oa, qb, kb, vb, za, zb, gif = _split(h @ w_in, sizes)
    gif = gif.astype(F32) + b_if
    i_pre = gif[..., :A_HEADS]
    log_f = jax.nn.log_sigmoid(gif[..., A_HEADS:])
    ha, C, n, m = _mlstm_chunked(_heads(qa, A_HEADS), _heads(ka, A_HEADS) * A_DK ** -0.5,
                                 _heads(va, A_HEADS), i_pre, log_f, C0, n0, m0)
    ha = ha * jax.nn.sigmoid(_heads(oa, A_HEADS))
    qr = _rope(_heads(qb, B_HEADS), pos) * B_DK ** -0.5
    kr = _rope(_heads(kb, B_HEADS), pos)
    hb, S = _retention_chunked(qr, kr, _heads(vb, B_HEADS), S0)
    o = jnp.concatenate([_head_rmsnorm(ha), _head_rmsnorm(hb)], axis=-1) * g_head
    z = jax.nn.silu(jnp.concatenate([za, zb], axis=-1).astype(F32))
    return (o * z) @ w_out, C, n, m, S

def _odd_mixer(h, w_in, w_a2, b_a2, conv_w, a_log, dt_bias, g_head, w_out, Sg0, Sd0, buf0):
    bsz, T, _ = h.shape
    sizes = [C_QK, C_QK, C_W, C_RANK, D_QK, D_QK, D_W, D_HEADS, D_HEADS, C_W, D_W]
    qc, kc, vc, a1, qd, kd, vd, ad, bd, zc, zd = _split(h @ w_in, sizes)
    log_a = jax.nn.log_sigmoid(a1.astype(F32) @ w_a2 + b_a2) / C_TAU
    hc, Sg = _gla_chunked(_heads(qc, C_HEADS) * C_DK ** -0.5, _heads(kc, C_HEADS), _heads(vc, C_HEADS),
                          log_a.reshape(bsz, T, C_HEADS, C_DK), Sg0)
    qkv = jnp.concatenate([qd, kd, vd], axis=-1).astype(F32)
    full = jnp.concatenate([buf0.astype(F32), qkv], axis=1)
    conv = sum(full[:, j:j + T] * conv_w[j] for j in range(CONV_W))
    qd, kd, vd = _split(jax.nn.silu(conv), [D_QK, D_QK, D_W])
    qd = _l2norm(_heads(qd, D_HEADS)) * D_DK ** -0.5
    kd = _l2norm(_heads(kd, D_HEADS))
    g = -jnp.exp(a_log) * jax.nn.softplus(ad.astype(F32) + dt_bias)
    beta = jax.nn.sigmoid(bd.astype(F32))
    hd, Sd = _gdn_chunked(qd, kd, _heads(vd, D_HEADS), g, beta, Sd0)
    o = jnp.concatenate([_head_rmsnorm(hc), _head_rmsnorm(hd)], axis=-1) * g_head
    z = jax.nn.silu(jnp.concatenate([zc, zd], axis=-1).astype(F32))
    return (o * z) @ w_out, Sg, Sd, full[:, T:]

def _trunk(x, c, pos, st_C, st_n, st_m, st_ret, st_gla, st_gdn, st_conv,
           w_ada, b_ada, g_pre, g_post, w_in_even, b_if_even, g_head_even, w_out_even,
           w_in_odd, w_a2, b_a2, conv_w, a_log, dt_bias, g_head_odd, w_out_odd):
    nC, nn_, nm, nret, ngla, ngdn, nconv = [], [], [], [], [], [], []
    cs = jax.nn.silu(c.astype(F32))
    for l in range(DEPTH):
        mod = cs @ w_ada[l] + b_ada[l]
        shift, scale, gate = jnp.split(mod[:, None, :], 3, axis=-1)
        h = _rmsnorm(x, g_pre[l]) * (1.0 + scale) + shift
        j = l // 2
        if l % 2 == 0:
            y, C, n, m, S = _even_mixer(h, pos, w_in_even[j], b_if_even[j], g_head_even[j], w_out_even[j],
                                        st_C[j], st_n[j], st_m[j], st_ret[j])
            nC.append(C); nn_.append(n); nm.append(m); nret.append(S)
        else:
            y, Sg, Sd, buf = _odd_mixer(h, w_in_odd[j], w_a2[j], b_a2[j], conv_w[j], a_log[j], dt_bias[j],
                                        g_head_odd[j], w_out_odd[j], st_gla[j], st_gdn[j], st_conv[j])
            ngla.append(Sg); ngdn.append(Sd); nconv.append(buf)
        x = (x + gate * _rmsnorm(y, g_post[l])).astype(x.dtype)
    return (x, jnp.stack(nC), jnp.stack(nn_), jnp.stack(nm), jnp.stack(nret),
            jnp.stack(ngla), jnp.stack(ngdn), jnp.stack(nconv))

def setup_inputs(seed: int = 0) -> dict:
    key = jax.random.key(seed)
    ks = jax.random.split(key, 32)

    def nrm(i, shape, s):
        return jax.random.normal(ks[i], shape, F32) * s

    dt = jnp.exp(jax.random.uniform(ks[25], (N_ODD, D_HEADS), F32, minval=math.log(1e-3), maxval=math.log(1e-1)))
    return {
        'x_prompt': nrm(0, (BATCH, SEQ, D_MODEL), 1.0),
        'x_sample': nrm(1, (DEC_BATCH, DEC_SEQ, D_MODEL), 1.0),
        'c_prompt': nrm(2, (BATCH, D_MODEL), 1.0),
        'c_sample': nrm(3, (DEC_BATCH, D_MODEL), 1.0),
        'state_mlstm_C': nrm(4, (N_EVEN, DEC_BATCH, A_HEADS, A_DK, A_DV), 0.3),
        'state_mlstm_n': nrm(5, (N_EVEN, DEC_BATCH, A_HEADS, A_DK), 0.3),
        'state_mlstm_m': nrm(6, (N_EVEN, DEC_BATCH, A_HEADS), 1.0),
        'state_ret': nrm(7, (N_EVEN, DEC_BATCH, B_HEADS, B_DK, B_DV), 1.0),
        'state_gla': nrm(8, (N_ODD, DEC_BATCH, C_HEADS, C_DK, C_DV), 1.0),
        'state_gdn': nrm(9, (N_ODD, DEC_BATCH, D_HEADS, D_DK, D_DV), 0.3),
        'cache_gdn_conv': nrm(10, (N_ODD, DEC_BATCH, CONV_W - 1, CONV_CH), 1.0),
        'w_ada': nrm(11, (DEPTH, D_MODEL, 3 * D_MODEL), D_MODEL ** -0.5),
        'b_ada': nrm(12, (DEPTH, 3 * D_MODEL), 0.02),
        'g_pre': 1.0 + nrm(13, (DEPTH, D_MODEL), 0.02),
        'g_post': 1.0 + nrm(14, (DEPTH, D_MODEL), 0.02),
        'w_in_even': nrm(15, (N_EVEN, D_MODEL, EVEN_IN), D_MODEL ** -0.5),
        'b_if_even': jnp.concatenate([nrm(16, (N_EVEN, A_HEADS), 0.1),
                                      jnp.linspace(3.0, 6.0, A_HEADS, dtype=F32)[None, :] + nrm(17, (N_EVEN, A_HEADS), 0.1)], axis=-1),
        'g_head_even': 1.0 + nrm(18, (N_EVEN, A_W + B_W), 0.02),
        'w_out_even': nrm(19, (N_EVEN, A_W + B_W, D_MODEL), (A_W + B_W) ** -0.5),
        'w_in_odd': nrm(20, (N_ODD, D_MODEL, ODD_IN), D_MODEL ** -0.5),
        'w_a2': nrm(21, (N_ODD, C_RANK, C_QK), C_RANK ** -0.5),
        'b_a2': nrm(22, (N_ODD, C_QK), 0.1),
        'conv_w': nrm(23, (N_ODD, CONV_W, CONV_CH), CONV_W ** -0.5),
        'a_log': jnp.log(jax.random.uniform(ks[24], (N_ODD, D_HEADS), F32, minval=1.0, maxval=16.0)),
        'dt_bias': dt + jnp.log(-jnp.expm1(-dt)),
        'g_head_odd': 1.0 + nrm(26, (N_ODD, C_W + D_W), 0.02),
        'w_out_odd': nrm(27, (N_ODD, C_W + D_W, D_MODEL), (C_W + D_W) ** -0.5),
    }

def reference(x_prompt, x_sample, c_prompt, c_sample, state_mlstm_C, state_mlstm_n, state_mlstm_m,
              state_ret, state_gla, state_gdn, cache_gdn_conv, w_ada, b_ada, g_pre, g_post,
              w_in_even, b_if_even, g_head_even, w_out_even, w_in_odd, w_a2, b_a2, conv_w,
              a_log, dt_bias, g_head_odd, w_out_odd):
    bp = x_prompt.shape[0]
    pos_p = jnp.arange(x_prompt.shape[1], dtype=F32)
    pos_s = PAST_LEN + jnp.arange(x_sample.shape[1], dtype=F32)
    z_C = jnp.zeros((N_EVEN, bp, A_HEADS, A_DK, A_DV), F32)
    z_n = jnp.zeros((N_EVEN, bp, A_HEADS, A_DK), F32)
    z_m = jnp.zeros((N_EVEN, bp, A_HEADS), F32)
    z_ret = jnp.zeros((N_EVEN, bp, B_HEADS, B_DK, B_DV), F32)
    z_gla = jnp.zeros((N_ODD, bp, C_HEADS, C_DK, C_DV), F32)
    z_gdn = jnp.zeros((N_ODD, bp, D_HEADS, D_DK, D_DV), F32)
    z_conv = jnp.zeros((N_ODD, bp, CONV_W - 1, CONV_CH), F32)
    y_p, pC, pn, pm, pret, pgla, pgdn, pconv = _trunk(
        x_prompt, c_prompt, pos_p, z_C, z_n, z_m, z_ret, z_gla, z_gdn, z_conv,
        w_ada, b_ada, g_pre, g_post, w_in_even, b_if_even, g_head_even, w_out_even,
        w_in_odd, w_a2, b_a2, conv_w, a_log, dt_bias, g_head_odd, w_out_odd)
    y_s, sC, sn, sm, sret, sgla, sgdn, sconv = _trunk(
        x_sample, c_sample, pos_s, state_mlstm_C, state_mlstm_n, state_mlstm_m, state_ret,
        state_gla, state_gdn, cache_gdn_conv,
        w_ada, b_ada, g_pre, g_post, w_in_even, b_if_even, g_head_even, w_out_even,
        w_in_odd, w_a2, b_a2, conv_w, a_log, dt_bias, g_head_odd, w_out_odd)
    return (y_p, y_s, pC, pn, pm, pret, pgla, pgdn, pconv, sC, sn, sm, sret, sgla, sgdn, sconv)


_drawn_inputs = setup_inputs


def setup_inputs(seed=0):
    import zlib

    import numpy as np

    out = dict(_drawn_inputs(seed))
    spreads = {}
    factors = {'g_post': 3.704, 'g_head_even': 3.633, 'g_head_odd': 6.45}
    for name, (base, spread) in spreads.items():
        noise = np.random.default_rng([zlib.crc32(name.encode()), seed]).standard_normal(out[name].shape)
        drawn = base * np.exp(spread * noise) if base else spread * noise
        out[name] = __import__('jax').numpy.asarray(drawn.astype(out[name].dtype))
    for name, factor in factors.items():
        out[name] = (out[name] * factor).astype(out[name].dtype)
    return out
```

```python
from contextlib import ExitStack

import numpy as np

import concourse.bass as bass
from concourse import mybir

F32 = mybir.dt.float32
U32 = mybir.dt.uint32
ACT = mybir.ActivationFunctionType
ALU = mybir.AluOpType
AX = mybir.AxisListType

P = 128
D = 1024
KT = D // P
SEQ, DEC = 512, 64
TOK = SEQ + DEC
HALF = TOK // 2
PT = SEQ // P
T = PT + 1
EPS = 1e-6
NEG = -1e30
EVEN_H, GLA_H, GDN_H = 4, 4, 8
RANK = 16
LEVELS = (1, 2, 4, 8, 16, 32, 64)
COND = [0] * PT + [1]


def rows(t):
    return P if t < PT else DEC


def cols(t):
    return slice(t * P, t * P + rows(t))


def shape_constants():
    s, t = np.arange(P)[:, None], np.arange(P)[None, :]
    lg = np.log(1.0 - 2.0 ** (-5.0 - np.arange(EVEN_H)))
    parts = {
        "ident": np.eye(P),
        "ones": np.ones((P, P)),
        "mask": (s <= t) * 1.0,
        "neg_causal": np.where(s <= t, 0.0, NEG),
        "neg_strict": np.where(s < t, 0.0, NEG),
        "half": np.full((P, 1), -0.5),
        "levels": np.concatenate([((s // (2 * n) == t // (2 * n)) & (s % (2 * n) < n) & (t % (2 * n) >= n)) * 1.0
                                  for n in LEVELS], axis=1),
        "decay": np.concatenate([np.where(s <= t, np.exp(np.maximum(t - s, 0) * g), 0.0) for g in lg], axis=1),
        "q_decay": np.exp((s + 1.0) * lg[None, :]),
        "k_decay": np.concatenate([np.exp((P - 1.0 - s) * lg), np.exp(np.maximum(DEC - 1.0 - s, 0) * lg)], axis=1),
        "s_decay": np.broadcast_to(np.concatenate([np.exp(P * lg), np.exp(DEC * lg)])[None, :], (P, 2 * EVEN_H)),
    }
    for n, name in ((EVEN_H, "diag4"), (GDN_H, "diag8")):
        parts[name] = np.broadcast_to(np.eye(P, n)[:, None, :], (P, T, n)).reshape(P, T * n)
    inv = 10000.0 ** (-np.arange(P, dtype=np.float64) / P)
    pos = np.concatenate([np.arange(SEQ), 512 + np.arange(DEC)])
    parts["cos"], parts["sin"] = np.cos(inv[:, None] * pos), np.sin(inv[:, None] * pos)
    where, at = {}, 0
    for name, a in parts.items():
        where[name] = (at, at + a.shape[1])
        at += a.shape[1]
    return np.concatenate(list(parts.values()), axis=1).astype(np.float32), where


class Signal:

    def __init__(self, sem, per, first):
        self.sem, self.per, self.first = sem, per, first

    def done(self, turn, k):
        return self.sem, turn * self.per + (self.first + k + 1)

    def before(self, turn, k):
        return self.sem, turn * self.per + (self.first + k)


class Link:

    def __init__(self, eng, step, turn=0):
        self.eng, self.step, self.turn, self.k = eng, step, turn, 0

    def __call__(self, ins, n=1):
        ins.then_inc(self.step.sem, 1)
        self.eng.wait_ge(*self.step.done(self.turn, self.k))
        self.k += 1

    def close(self):
        assert self.k == self.step.per, (self.k, self.step.per)


class Phase:

    def __init__(self, nc, name, first=0):
        self.nc, self.name, self.first, self.ctx, self.counters = nc, name, first, ExitStack(), []

    def __enter__(self):
        return self

    def __exit__(self, *exc):
        if exc[0] is None:
            self.nc.clear_and_free_semaphores([s.sem for s in self.counters])
            self.nc.all_engine_barrier()
        self.ctx.close()
        return False

    def sb(self, name, shape, dt=F32):
        return self.ctx.enter_context(self.nc.sbuf_tensor(f"{self.name}_{name}", shape, dt))

    def counter(self, name, per=1):
        s = Signal(self.nc.alloc_semaphore(f"{self.name}_{name}"), per, self.first)
        if self.first:
            engines = (self.nc.sync, self.nc.gpsimd, self.nc.scalar, self.nc.vector, self.nc.tensor)
            engines[len(self.counters) % 5].sem_inc(s.sem, self.first)
        self.counters.append(s)
        return s


def matmul_chain(pe, out, pairs):
    for n, (a, b) in enumerate(pairs):
        last = pe.matmul(out, a, b, start=(n == 0), stop=(n == len(pairs) - 1))
    return last


def setup(nc, M, IN, OUT):
    with Phase(nc, "setup") as ph:
        vec = ph.sb("vec_rows", [P, P])
        conv_rows = ph.sb("conv_rows", [P, P])
        tc = ph.sb("tanh_c", [P, 16])
        cs = ph.sb("silu_c", [P, KT, 2])
        wada = ph.sb("w_ada", [P, 2, 3 * D])
        bada = ph.sb("b_ada", [2, 2, 3 * D])
        mod = ph.sb("mod_rows", [2, 2, 2 * D])
        loaded = ph.counter("small_loaded", 16 * 11)
        ada_loaded = [ph.counter(f"ada_loaded{i}", 16 * KT) for i in range(2)]
        bada_loaded = ph.counter("b_ada_loaded", 64)
        x_loaded = ph.counter("x_loaded", 32)
        vec_psum = ph.counter("vec_psum")
        vec_copied = ph.counter("vec_copied", 2)
        tanh_done = ph.counter("tanh_done")
        cs_half = ph.counter("silu_c_half")
        cs_ready = ph.counter("silu_c_ready")
        ada_used = ph.counter("ada_used", 2 * KT)
        mod_ready = ph.counter("mod_ready", 2 * 6)
        modT_psum = ph.counter("modT_psum", 2)
        modT_copied = ph.counter("modT_copied", 2)
        scaled = ph.counter("scaled", 4)
        gh_scaled = ph.counter("g_head_scaled", 4)
        PS = M["ps"]
        with nc.Block() as block:

            @block.sync
            def _(sp):
                sp.dma_start(M["const"][:], IN["const"]).then_inc(M.const_loaded, 16)
                rowsof = [(IN["c_prompt"][0], 0, 8), (IN["c_sample"][0], 8, 8),
                          (IN["g_pre"][0], 16, 8), (IN["g_pre"][1], 24, 8),
                          (IN["g_head_even"][0], 32, 16), (IN["g_head_odd"][0], 48, 16), (IN["b_a2"][0], 64, 4)]
                for src, at, n in rowsof:
                    sp.dma_start(vec[at:at + n, :], src.rearrange("(r c) -> r c", c=P)).then_inc(loaded.sem, 16)
                for j in range(4):
                    sp.dma_start(conv_rows[24 * j:24 * j + 24, :],
                                 IN["conv_w"][0, j].rearrange("(r c) -> r c", c=P)).then_inc(loaded.sem, 16)
                for l in range(2):
                    for k in range(KT):
                        i = l * KT + k
                        if i >= 2:
                            sp.wait_ge(*ada_used.done(0, i - 2))
                        sp.dma_start(wada[:, i % 2, :], IN["w_ada"][l, k * P:(k + 1) * P, :]).then_inc(
                            ada_loaded[i % 2].sem, 16)
                        if i == 0:
                            for m in range(2):
                                sp.dma_start(bada[m:m + 1, :, :], IN["b_ada"].rearrange("(a l) n -> a l n", a=1)
                                             ).then_inc(bada_loaded.sem, 32)
                sp.dma_start(M["x"][:, 0:PT, :], IN["x_prompt"][0].rearrange("(t p) d -> p t d", p=P)).then_inc(x_loaded.sem, 16)
                sp.dma_start(M["x"][0:DEC, PT, :], IN["x_sample"][0]).then_inc(x_loaded.sem, 16)
                sp.wait_ge(*x_loaded.done(0, 31))

            @block.tensor
            def _(pe):
                pe.wait_ge(*loaded.done(0, 16 * 11 - 1))
                pe.wait_ge(M.const_loaded, 16)
                pe.transpose(PS[7][:, 0:68], vec[0:68, :], M.c("ident", 68, 68))
                pe.transpose(PS[7][:, 128:224], conv_rows[0:96, :], M.c("ident", 96, 96)).then_inc(vec_psum.sem, 1)
                pe.wait_ge(*cs_ready.done(0, 0))
                for l in range(2):
                    for k in range(KT):
                        i = l * KT + k
                        pe.wait_ge(*ada_loaded[i % 2].done(0, 16 * (i // 2) + 15))
                        if l and k == 0:
                            pe.wait_ge(*mod_ready.done(0, 5))
                        for n in range(6):
                            last = pe.matmul(PS[n][0:2, :], cs[:, k, :], wada[:, i % 2, n * 512:(n + 1) * 512],
                                             start=(k == 0), stop=(k == KT - 1))
                        last.then_inc(ada_used.sem, 1)
                    pe.wait_ge(*mod_ready.done(0, 6 * l + 5))
                    if l:
                        pe.wait_ge(*modT_copied.done(0, 0))
                    for c in range(16):
                        last = pe.transpose(PS[6][:, 2 * c:2 * c + 2], mod[0:2, l, c * P:(c + 1) * P], M.c("ident", 2, 2))
                    last.then_inc(modT_psum.sem, 1)

            @block.scalar
            def _(act):
                act.wait_ge(*vec_copied.done(0, 1))
                act.activation(tc[:], M["vec"][:, 0:16], ACT.Tanh, scale=0.5).then_inc(tanh_done.sem, 1)

            @block.vector
            def _(dve):
                dve.wait_ge(*vec_psum.done(0, 0))
                dve.tensor_copy(M["vec"][:], PS[7][:, 0:68]).then_inc(vec_copied.sem, 1)
                dve.tensor_copy(M["conv"][:], PS[7][:, 128:224]).then_inc(vec_copied.sem, 1)
                dve.wait_ge(*tanh_done.done(0, 0))
                dve.scalar_tensor_tensor(tc[:], tc[:], 1.0, M["vec"][:, 0:16], ALU.add, ALU.mult).then_inc(cs_half.sem, 1)
                dve.wait_ge(*cs_half.done(0, 0))
                dve.tensor_scalar(cs[:].rearrange("p k m -> p m k"), tc[:].rearrange("p (m k) -> p m k", m=2), 0.5, None,
                                  ALU.mult).then_inc(cs_ready.sem, 1)
                for a, b, f in ((32, 40, 0.25), (40, 48, 0.5), (48, 64, 0.5)):
                    dve.tensor_scalar(M["vec"][:, a:b], M["vec"][:, a:b], f, None, ALU.mult).then_inc(gh_scaled.sem, 1)
                dve.memset(M["x"][DEC:P, PT, :], 0.0).then_inc(gh_scaled.sem, 1)
                dve.wait_ge(*bada_loaded.done(0, 63))
                for l in range(2):
                    dve.wait_ge(*ada_used.done(0, l * KT + KT - 1))
                    for n in range(6):
                        out = mod[:, l, n * 512:(n + 1) * 512] if n < 4 else M["gate"][:, l, (n - 4) * 512:(n - 3) * 512]
                        dve.tensor_tensor(out, PS[n][0:2, :], bada[:, l, n * 512:(n + 1) * 512], ALU.add).then_inc(
                            mod_ready.sem, 1)
                    dve.wait_ge(*modT_psum.done(0, l))
                    dve.tensor_copy(M["modT"][:, l, :, :], PS[6][:, 0:32].rearrange("p (c m) -> p c m", m=2)).then_inc(
                        modT_copied.sem, 1)
                    dve.wait_ge(*modT_copied.done(0, l))
                    for m in range(2):
                        dve.scalar_tensor_tensor(M["modT"][:, l, KT:2 * KT, m], M["modT"][:, l, KT:2 * KT, m], 1.0,
                                                 M["vec"][:, 16 + 8 * l:24 + 8 * l], ALU.add, ALU.mult).then_inc(scaled.sem, 1)


def norm_steps(ph, M, l):
    S = {n: ph.counter(n, k) for n, k in (("sq", T), ("mean", T), ("rstd", T), ("xn", T), ("xT_psum", 2 * T),
                                         ("hT_act", T), ("hT_dve", T))}
    PS = M["ps"]
    sqj = ph.sb("squares", [P, D])
    ss, ms, rs = ph.sb("ss", [P, T]), ph.sb("ms", [P, T]), ph.sb("rs", [P, T])
    xn = ph.sb("xn", [P, 2, D])

    def act_steps(act):
        for t in range(T):
            if t:
                act.wait_ge(*S["sq"].done(0, t - 1))
            act.activation(sqj[0:rows(t), :], M["x"][0:rows(t), t, :], ACT.Square, accum_out=ss[0:rows(t), t:t + 1]
                           ).then_inc(S["sq"].sem, 1)
        for t in range(T):
            act.wait_ge(*S["xT_psum"].done(0, 2 * t))
            for k in range(4):
                last = act.activation(M["hT"][:, k, cols(t)], PS[2 * (t % 2)][:, k * P:k * P + rows(t)], ACT.Identity,
                                      bias=M["modT"][:, l, k, COND[t]:COND[t] + 1],
                                      scale=M["modT"][:, l, KT + k, COND[t]:COND[t] + 1])
            last.then_inc(S["hT_act"].sem, 1)

    def pool_steps(pool):
        for t in range(T):
            R = rows(t)
            pool.wait_ge(*S["sq"].done(0, t))
            pool.tensor_scalar(ms[0:R, t:t + 1], ss[0:R, t:t + 1], 1.0 / D, EPS, ALU.mult, ALU.add).then_inc(S["mean"].sem, 1)
            pool.wait_ge(*S["mean"].done(0, t))
            pool.tensor_tensor(rs[0:R, t:t + 1], ms[0:R, t:t + 1], M.c("half", R), ALU.pow).then_inc(S["rstd"].sem, 1)

    def dve_steps(dve):
        def scale(t):
            R = rows(t)
            dve.wait_ge(*S["rstd"].done(0, t))
            if t >= 2:
                dve.wait_ge(*S["xT_psum"].done(0, 2 * (t - 2) + 1))
            dve.tensor_scalar(xn[0:R, t % 2, :], M["x"][0:R, t, :], rs[0:R, t:t + 1], None, ALU.mult).then_inc(S["xn"].sem, 1)
        scale(0)
        for t in range(T):
            if t + 1 < T:
                scale(t + 1)
            dve.wait_ge(*S["xT_psum"].done(0, 2 * t + 1))
            for k in range(4, KT):
                last = dve.tensor_scalar(M["hT"][:, k, cols(t)], PS[2 * (t % 2) + 1][:, (k - 4) * P:(k - 4) * P + rows(t)],
                                         M["modT"][:, l, KT + k, COND[t]:COND[t] + 1],
                                         M["modT"][:, l, k, COND[t]:COND[t] + 1], ALU.mult, ALU.add)
            last.then_inc(S["hT_dve"].sem, 1)

    def pe_steps(pe):
        for t in range(T):
            R = rows(t)
            pe.wait_ge(*S["xn"].done(0, t))
            for half in range(2):
                if t >= 2:
                    pe.wait_ge(*S[("hT_act", "hT_dve")[half]].done(0, t - 2))
                for k in range(4):
                    kk = 4 * half + k
                    last = pe.transpose(PS[2 * (t % 2) + half][:, k * P:k * P + R], xn[0:R, t % 2, kk * P:(kk + 1) * P],
                                        M.c("ident", R, R))
                last.then_inc(S["xT_psum"].sem, 1)
        pe.wait_ge(*S["hT_act"].done(0, T - 1))
        pe.wait_ge(*S["hT_dve"].done(0, T - 1))

    return act_steps, pool_steps, dve_steps, pe_steps


def small_projection(pe, M, w, c0, n, banks):
    for half in range(2):
        last = matmul_chain(pe, M["ps"][banks[half]][0:n, 0:HALF],
                            [(w[:, k, c0:c0 + n], M["hT"][:, k, half * HALF:(half + 1) * HALF]) for k in range(KT)])
    return last


def log_sigmoid(act, dve, x, a, b, out, S, turn=0):
    if dve is not None:
        dve.scalar_tensor_tensor(a, x, -1.0, x, ALU.mult, ALU.max).then_inc(S["abs"].sem, 1)
        dve.wait_ge(*S["exp"].done(turn, 0))
        dve.tensor_scalar(b, b, 1.0, None, ALU.add).then_inc(S["plus"].sem, 1)
        dve.wait_ge(*S["log"].done(turn, 0))
        return dve.scalar_tensor_tensor(out, x, 0.0, a, ALU.min, ALU.subtract)
    act.wait_ge(*S["abs"].done(turn, 0))
    act.activation(b, a, ACT.Exp, scale=-1.0).then_inc(S["exp"].sem, 1)
    act.wait_ge(*S["plus"].done(turn, 0))
    act.activation(a, b, ACT.Ln).then_inc(S["log"].sem, 1)


def even_gates(nc, M, IN, OUT):
    with Phase(nc, "even_gates") as ph:
        act_norm, pool_norm, dve_norm, pe_norm = norm_steps(ph, M, 0)
        H = EVEN_H
        sb, sig = ph.sb, ph.counter
        wg = sb("w_gates", [P, KT, 2 * H])
        bif = sb("b_if", [H, 2])
        mprev = sb("m_prev", [H, T + 2])
        gi, gf, ta, tb, lf = (sb(n, [H, TOK]) for n in ("gate_i", "gate_f", "ls_a", "ls_b", "log_f"))
        b, u, Mx, m = (sb(n, [H, TOK]) for n in ("cum_f", "u_rows", "M_rows", "m_rows"))
        mp_rows, me_rows = sb("mp_rows", [H, T, H]), sb("me_rows", [H, T, H])
        msel = sb("M_selected", [H, H, TOK])
        col = sb("gate_cols", [P, 3, T, H])
        bro = sb("gate_broadcast", [P, 2, T, H])
        arg = sb("gate_args", [P, 4, T, H])
        wl = sig("w_gates_loaded", 16 * 5)
        proj, copied = sig("gates_psum", 2), sig("gates_copied", 4)
        S = {n: sig("ls_" + n) for n in ("abs", "exp", "plus", "log")}
        lk = sig("vector_step")
        rows_ready, colsp, bp, bcopied = sig("rows_ready"), sig("cols_psum"), sig("M_psum", 2 * H), sig("M_copied", 2 * H)
        args_ready, exps = sig("args_ready"), sig("gate_exps")
        cleared = sig("cols_cleared")
        m_stored = sig("m_stored", 32)
        PS = M["ps"]
        with nc.Block() as block:

            @block.sync
            def _(sp):
                sp.dma_start(wg[:], IN["w_in_even"][0, :, 9 * D:9 * D + 2 * H].rearrange("(k p) n -> p k n", p=P)).then_inc(wl.sem, 16)
                for i in range(2):
                    sp.dma_start(bif[:, i:i + 1], IN["b_if_even"][0, i * H:(i + 1) * H].rearrange("(h a) -> h a", a=1)).then_inc(wl.sem, 16)
                sp.dma_start(mprev[:, PT:PT + 1], IN["state_mlstm_m"][0, 0].rearrange("(h a) -> h a", a=1)).then_inc(wl.sem, 32)
                sp.wait_ge(*rows_ready.done(0, 0))
                sp.dma_start(OUT["pm"][0, 0].rearrange("(h a) -> h a", a=1), mprev[:, T:T + 1]).then_inc(m_stored.sem, 16)
                sp.dma_start(OUT["sm"][0, 0].rearrange("(h a) -> h a", a=1), mprev[:, T + 1:T + 2]).then_inc(m_stored.sem, 16)
                sp.wait_ge(*m_stored.done(0, 31))

            @block.gpsimd
            def _(pool):
                pool_norm(pool)

            @block.tensor
            def _(pe):
                pe_norm(pe)
                pe.wait_ge(*wl.done(0, 79))
                small_projection(pe, M, wg, 0, H, (4, 5)).then_inc(proj.sem, 1)
                small_projection(pe, M, wg, H, H, (6, 7)).then_inc(proj.sem, 1)
                pe.wait_ge(*rows_ready.done(0, 0))
                for n, r in enumerate((u, Mx, m)):
                    for t in range(T):
                        at = (n * T + t) * H
                        pe.transpose(PS[0][0:rows(t), at:at + H], r[:, cols(t)], M.c("ident", H, H))
                for n, r in enumerate((mp_rows, me_rows)):
                    last = pe.matmul(PS[1][:, n * T * H:(n + 1) * T * H], M.c("ones", H), r[:].rearrange("p t h -> p (t h)"),
                                     start=True, stop=True)
                last.then_inc(colsp.sem, 1)
                for h in range(H):
                    for half in range(2):
                        n = 2 * h + half
                        if n >= 2:
                            pe.wait_ge(*bcopied.done(0, n - 2))
                        pe.matmul(PS[2 + half][:, 0:HALF], M.c("ones", H), msel[:, h, half * HALF:(half + 1) * HALF],
                                  start=True, stop=True).then_inc(bp.sem, 1)

            @block.scalar
            def _(act):
                act_norm(act)
                for i, g in enumerate((gi, gf)):
                    act.wait_ge(*proj.done(0, i))
                    for half in range(2):
                        act.activation(g[:, half * HALF:(half + 1) * HALF], PS[4 + 2 * i + half][0:H, 0:HALF], ACT.Identity,
                                       bias=bif[:, i:i + 1]).then_inc(copied.sem, 1)
                log_sigmoid(act, None, gf[:], ta[:], tb[:], lf[:], S)
                act.wait_ge(*args_ready.done(0, 0))
                act.activation(M["mcols"][:], arg[:], ACT.Exp).then_inc(exps.sem, 1)
                for n in range(2 * H):
                    act.wait_ge(*bp.done(0, n))
                    act.activation(M["negM"][:, n // 2, (n % 2) * HALF:(n % 2 + 1) * HALF], PS[2 + n % 2][:, 0:HALF],
                                   ACT.Copy).then_inc(bcopied.sem, 1)

            @block.vector
            def _(dve):
                link = Link(dve, lk)
                dve.memset(mprev[:, 0:1], 0.0)
                dve.memset(col[:], 0.0).then_inc(cleared.sem, 1)
                dve_norm(dve)
                dve.wait_ge(*copied.done(0, 3))
                link(log_sigmoid(None, dve, gf[:], ta[:], tb[:], lf[:], S))
                for t in range(T):
                    last = dve.tensor_tensor_scan(b[:, cols(t)], M.c("ones", H, rows(t)), lf[:, cols(t)], 0.0, ALU.mult, ALU.add)
                link(last)
                link(dve.tensor_tensor(u[:], gi[:], b[:], ALU.subtract))
                dve.wait_ge(*wl.done(0, 79))
                for t in range(T):
                    end = t * P + rows(t) - 1
                    link(dve.tensor_tensor_scan(Mx[:, cols(t)], u[:, cols(t)], u[:, cols(t)], mprev[:, t:t + 1], ALU.max, ALU.max))
                    to = t + 1 if t < PT - 1 else (T if t == PT - 1 else T + 1)
                    link(dve.tensor_tensor(mprev[:, to:to + 1], b[:, end:end + 1], Mx[:, end:end + 1], ALU.add))
                dve.tensor_tensor(m[:], b[:], Mx[:], ALU.add)
                for h in range(H):
                    dve.tensor_scalar(msel[:, h, :], Mx[:], M.c("diag4", H)[:, h:h + 1], -1.0, ALU.mult, ALU.mult)
                for t in range(T):
                    end = t * P + rows(t) - 1
                    dve.tensor_scalar(mp_rows[:, t, :], M.c("diag4", H)[:, 0:H], mprev[:, t:t + 1], None, ALU.mult)
                    last = dve.tensor_scalar(me_rows[:, t, :], M.c("diag4", H)[:, 0:H], Mx[:, end:end + 1], None, ALU.mult)
                last.then_inc(rows_ready.sem, 1)
                dve.wait_ge(*colsp.done(0, 0))
                src = PS[0][:, 0:3 * T * H].rearrange("p (n t h) -> p n t h", n=3, t=T)
                dve.tensor_copy(col[:, :, 0:PT, :], src[:, :, 0:PT, :])
                dve.tensor_copy(col[0:DEC, :, PT, :], src[0:DEC, :, PT, :])
                link(dve.tensor_copy(bro[:].rearrange("p n t h -> p (n t h)"), PS[1][:, 0:2 * T * H]))
                dve.tensor_copy(M["ucol"][:], col[:, 0])
                dve.tensor_tensor(arg[:, 0], bro[:, 0], col[:, 1], ALU.subtract)
                dve.tensor_tensor(arg[:, 1], col[:, 0], bro[:, 1], ALU.subtract)
                dve.tensor_tensor(arg[:, 2], bro[:, 0], bro[:, 1], ALU.subtract)
                dve.tensor_scalar(arg[:, 3], col[:, 2], -1.0, None, ALU.mult).then_inc(args_ready.sem, 1)


def heads(nc, M, IN, OUT, kind):
    H, DV = 4, 256
    DT = {"A": 2, "B": 2, "C": 1}[kind]
    NV = DV + 1 if kind == "A" else DV
    NG = 2 * DV if kind == "A" else DV
    CT = 2 * DT
    NP = 2 * CT + (2 if kind == "C" else 0)
    w_in = IN["w_in_odd" if kind == "C" else "w_in_even"][0].rearrange("(k p) n -> p k n", p=P)
    q0, k0, v0 = {"A": (0, D, 2 * D), "B": (4 * D, 5 * D, 6 * D), "C": (0, 512, D)}[kind]
    gates0 = {"A": [3 * D, 7 * D], "B": [8 * D], "C": [5 * D + 32]}[kind]
    S_in = IN[{"A": "state_mlstm_C", "B": "state_ret", "C": "state_gla"}[kind]][0, 0]
    pS = OUT[{"A": "pC", "B": "pret", "C": "pgla"}[kind]][0, 0]
    sS = OUT[{"A": "sC", "B": "sret", "C": "sgla"}[kind]][0, 0]
    g_col = {"A": 32, "B": 40, "C": 48}[kind]
    g_row = {"A": 0, "B": 8, "C": 0}[kind]
    ms_scale = 1.0 / (4 * DV) if kind == "A" else 1.0 / DV
    QS = (P if kind == "C" else DV) ** -0.5
    PS = M["ps"]
    with Phase(nc, {"A": "mlstm", "B": "retention", "C": "gla"}[kind], first=1) as ph:
        sb, sig = ph.sb, ph.counter
        wqk = sb("w_qk", [P, KT, CT * P])
        wv = sb("w_gates_v", [P, KT, NG + DV])
        qk = sb("qkT", [P, CT, TOK])
        v = sb("v", [P, NV])
        th = sb("tanh", [P, NG])
        zs = sb("z_silu", [P, DV])
        sT = sb("scores", [P, P])
        kw = sb("k_weighted", [P, DT * P])
        num_a, num, hg, g = sb("intra", [P, NV]), sb("num", [P, NV]), sb("h_gated", [P, DV]), sb("g", [P, DV])
        sq = sb("squares", [P, DV])
        sm = sb("small", [P, 8])
        St = [sb("state_prompt", [P, DT, NV]), sb("state_sample", [P, DT, NV])]
        if kind == "A":
            E, arg = sb("E", [P, P]), sb("E_arg", [P, P])
            logit_ready, decay_ready = sig("logit_ready", T), sig("decay_ready", T)
        if kind in "BC":
            raw = sb("qkT_raw", [P, CT, TOK])
        if kind == "B":
            ra, rb = sb("rope_a", [P, TOK]), sb("rope_b", [P, TOK])
        if kind == "C":
            wa = sb("w_a2", [RANK, P])
            la, lb, lc, bT = (sb(n, [P, TOK]) for n in ("ls_x", "ls_a", "ls_b", "cum_a"))
            ends = sb("block_ends", [P, 3, T])
            eend = sb("block_exps", [P, 3, T])
            Sc = sb("state_scaled", [P, DV])
            nS = sb("state_new", [P, DV])
            wal = sig("w_a2_loaded", 16)
            Lg = {n: sig("ls_" + n) for n in ("abs", "exp", "plus", "log")}
            shifted, exps, b_ready = sig("b_shifted"), sig("b_exps", 3), sig("b_ready")
            sc_ready, nS_ready = sig("state_scaled_ready", PT), sig("state_new_ready", T)
        wql, wvl = sig("w_qk_loaded", 16), sig("w_v_loaded", 16 * (3 if kind == "A" else 2))
        wql2 = sig("w_qk_loaded2", 16)
        sl = sig("state_loaded", 32 if kind == "A" else 16)
        p_st, s_st = sig("prompt_state_stored", 32 if kind == "A" else 16), sig("sample_state_stored", 32 if kind == "A" else 16)
        qk_psum, qk_copied, qk_ready = sig("qk_psum", NP), sig("qk_copied", NP), sig("qk_ready")
        filled = sig("filled")
        (gates_psum, tanh_done, gates_used, v_psum, v_copied, scores_psum, scores_ready, kw_ready,
         nums_psum, intra_copied, state_psum, state_ready, squared, mean_ready, rstd_ready, g_ready, gT_psum,
         gT_copied) = (sig(n, T) for n in (
             "gates_psum", "tanh_done", "gates_used", "v_psum", "v_copied", "scores_psum",
             "scores_ready", "kw_ready", "nums_psum", "intra_copied", "state_psum", "state_ready", "squared",
             "mean_ready", "rstd_ready", "g_ready", "gT_psum", "gT_copied"))
        num_ready = sig("num_ready", PT)
        if kind == "A":
            den, hg_ready = sig("den_step", 4 * T), sig("h_gated_ready", T)
        NL = {"A": 0, "B": 11, "C": 6}[kind]
        lk = sig("vector_step", NL)

        def q_side(t):
            return slice(0, DT), cols(t)

        nc.all_engine_barrier()
        with nc.Block() as block:

            @block.sync
            def _(sp):
                with sp.Fori(0, H) as h:
                    sp.wait_ge(*qk_psum.before(h, 0))
                    sp.dma_start(wqk[:, :, 0:DT * P], w_in[:, :, bass.ds(h * (DT * P) + q0, DT * P)]).then_inc(wql.sem, 16)
                    sp.dma_start(wqk[:, :, DT * P:CT * P], w_in[:, :, bass.ds(h * (DT * P) + k0, DT * P)]).then_inc(wql2.sem, 16)
                    if kind == "C":
                        sp.dma_start(wa[:], IN["w_a2"][0][:, bass.ds(h * P, P)]).then_inc(wal.sem, 16)
                    sp.wait_ge(*v_psum.before(h, 0))
                    for n, c0 in enumerate(gates0 + [v0]):
                        sp.dma_start(wv[:, :, n * DV:(n + 1) * DV], w_in[:, :, bass.ds(h * DV + c0, DV)]).then_inc(wvl.sem, 16)
                sp.wait_ge(*p_st.before(H, 0))
                sp.wait_ge(*s_st.before(H, 0))

            @block.gpsimd
            def _(pool):
                with pool.Fori(0, H) as h:
                    for t in range(T):
                        R = rows(t)
                        pool.wait_ge(*squared.done(h, t))
                        pool.sem_inc(M.passed, 1)
                        pool.tensor_scalar(sm[0:R, 4:5], sm[0:R, 3:4], ms_scale, EPS, ALU.mult, ALU.add).then_inc(mean_ready.sem, 1)
                        pool.wait_ge(*mean_ready.done(h, t))
                        pool.tensor_tensor(sm[0:R, 5:6], sm[0:R, 4:5], M.c("half", R), ALU.pow).then_inc(rstd_ready.sem, 1)

            @block.tensor
            def _(pe):
                with pe.Fori(0, H) as h:
                    pe.wait_ge(*state_ready.before(h, 0))
                    for ct in range(CT):
                        if ct == 0:
                            pe.wait_ge(*wql.done(h, 15))
                        if ct == DT:
                            pe.wait_ge(*wql2.done(h, 15))
                        for half in range(2):
                            n = 2 * ct + half
                            pe.wait_ge(*(qk_copied.done(h, n - 2) if n >= 2 else qk_copied.before(h, 0)))
                            matmul_chain(pe, PS[half][:, 0:HALF],
                                         [(wqk[:, k, ct * P:(ct + 1) * P], M["hT"][:, k, half * HALF:(half + 1) * HALF])
                                          for k in range(KT)]).then_inc(qk_psum.sem, 1)
                    if kind == "C":
                        pe.wait_ge(*wal.done(h, 15))
                        for half in range(2):
                            pe.wait_ge(*qk_copied.done(h, 2 * CT + half - 2))
                            pe.matmul(PS[half][:, 0:HALF], wa[:], M["a1T"][:, half * HALF:(half + 1) * HALF],
                                      start=True, stop=True).then_inc(qk_psum.sem, 1)

                    def project(t, c0, n, out):
                        return matmul_chain(pe, out, [(M["hT"][:, k, cols(t)], wv[:, k, c0:c0 + n]) for k in range(KT)])

                    def turn_g(t):
                        pe.wait_ge(*g_ready.done(h, t))
                        pe.wait_ge(*gT_copied.before(h, t))
                        pe.sem_inc(M.passed, 1)
                        R = rows(t)
                        for d in range(2):
                            last = pe.transpose(PS[7][:, d * P:d * P + R], g[0:R, d * P:(d + 1) * P], M.c("ident", R, R))
                        last.then_inc(gT_psum.sem, 1)

                    for t in range(T):
                        R, cs = rows(t), cols(t)
                        if t == 0:
                            pe.wait_ge(*wvl.done(h, wvl.per - 1))
                        pe.wait_ge(*gates_used.before(h, t))
                        project(t, 0, NG, PS[2][0:R, 0:NG]).then_inc(gates_psum.sem, 1)
                        if t == 0:
                            pe.wait_ge(*(qk_copied.done(h, NP - 1) if kind == "A" else qk_ready.done(h, 0)))
                        pe.wait_ge(*kw_ready.before(h, t))
                        matmul_chain(pe, PS[4][0:R, 0:R], [(qk[:, DT + d, cs], qk[:, d, cs]) for d in range(DT)])
                        for d in range(DT):
                            last = pe.transpose(PS[4][0:R, (d + 1) * P:(d + 2) * P], qk[:, DT + d, cs], M.c("ident", P, P))
                        last.then_inc(scores_psum.sem, 1)
                        pe.wait_ge(*v_copied.before(h, t))
                        project(t, NG, DV, PS[3][0:R, 0:DV]).then_inc(v_psum.sem, 1)
                        if t and kind != "C":
                            pe.wait_ge(*num_ready.before(h, t - 1))
                            pe.wait_ge(*(sl.done(h, sl.per - 1) if t == PT else state_ready.before(h, t)))
                            matmul_chain(pe, PS[5][0:R, 0:NV], [(qk[:, d, cs], St[t // PT][:, d, :]) for d in range(DT)])
                        pe.wait_ge(*scores_ready.done(h, t))
                        pe.wait_ge(*v_copied.done(h, t))
                        pe.wait_ge(*intra_copied.before(h, t))
                        pairs = [(sT[0:R, 0:R], v[0:R, :])]
                        if t and kind == "C":
                            pe.wait_ge(*sc_ready.done(h, t - 1))
                            pairs.append((qk[:, 0, cs], Sc[:]))
                        pe.sem_inc(M.passed, 1)
                        matmul_chain(pe, PS[6][0:R, 0:NV], pairs).then_inc(nums_psum.sem, 1)
                        pe.wait_ge(*kw_ready.done(h, t))
                        pe.wait_ge(*(nS_ready if kind == "C" else state_ready).before(h, t))
                        pe.sem_inc(M.passed, 1)
                        for d in range(DT):
                            last = pe.matmul(PS[d][:, 0:NV], kw[0:R, d * P:(d + 1) * P], v[0:R, :], start=True, stop=True)
                        last.then_inc(state_psum.sem, 1)
                        if t:
                            turn_g(t - 1)
                    turn_g(T - 1)

            @block.scalar
            def _(act):
                with act.Fori(0, H) as h:
                    act.wait_ge(*s_st.before(h, 0))
                    src = S_in[bass.ds(h, 1)].rearrange("a (d p) v -> p (a d) v", p=P)
                    act.dma_start(St[1][:, :, 0:DV], src).then_inc(sl.sem, 16)
                    if kind == "A":
                        n_in = IN["state_mlstm_n"][0, 0][bass.ds(h, 1)].rearrange("a (d p b) -> p (a d) b", p=P, b=1)
                        act.dma_start(St[1][:, :, DV:NV], n_in, allow_slow_non_contiguous=True).then_inc(sl.sem, 16)
                    for n in range(NP):
                        ct, half = n // 2, n % 2
                        act.wait_ge(*qk_psum.done(h, n))
                        to = slice(half * HALF, (half + 1) * HALF)
                        if ct == CT:
                            act.activation(la[:, to], PS[half][:, 0:HALF], ACT.Copy).then_inc(qk_copied.sem, 1)
                            continue
                        scale = QS if (ct >= DT) == (kind == "A") else 1.0
                        act.activation((qk if kind == "A" else raw)[:, ct, to], PS[half][:, 0:HALF], ACT.Copy,
                                       scale=scale).then_inc(qk_copied.sem, 1)
                    if kind == "C":
                        log_sigmoid(act, None, None, lb[:], lc[:], None, Lg, h)
                        act.wait_ge(*shifted.done(h, 0))
                        act.activation(eend[:], ends[:], ACT.Exp).then_inc(exps.sem, 1)
                        act.activation(lb[:], la[:], ACT.Exp).then_inc(exps.sem, 1)
                        act.activation(lc[:], la[:], ACT.Exp, scale=-1.0).then_inc(exps.sem, 1)
                    for t in range(T):
                        R = rows(t)
                        if kind == "A":
                            act.wait_ge(*logit_ready.done(h, t))
                            act.activation(E[0:R, 0:R], arg[0:R, 0:R], ACT.Exp).then_inc(decay_ready.sem, 1)
                        act.wait_ge(*gates_psum.done(h, t))
                        act.wait_ge(*(hg_ready if kind == "A" else gates_used).before(h, t))
                        act.activation(th[0:R, :], PS[2][0:R, 0:NG], ACT.Tanh, scale=0.5).then_inc(tanh_done.sem, 1)
                        act.wait_ge(*v_psum.done(h, t))
                        act.wait_ge(*state_psum.before(h, t))
                        act.activation(v[0:R, 0:DV], PS[3][0:R, 0:DV], ACT.Copy).then_inc(v_copied.sem, 1)
                        act.wait_ge(*nums_psum.done(h, t))
                        act.wait_ge(*g_ready.before(h, t))
                        act.activation(num_a[0:R, :], PS[6][0:R, 0:NV], ACT.Copy).then_inc(intra_copied.sem, 1)
                        if kind == "A":
                            act.wait_ge(*hg_ready.done(h, t))
                        elif kind == "B" and t:
                            act.wait_ge(*num_ready.done(h, t - 1))
                        else:
                            act.wait_ge(*intra_copied.done(h, t))
                        src = hg if kind == "A" else (num if kind == "B" and t else num_a)
                        act.activation(sq[0:R, :], src[0:R, 0:DV], ACT.Square, accum_out=sm[0:R, 3:4]).then_inc(squared.sem, 1)
                        if t >= PT - 1:
                            i = t - PT + 1
                            act.wait_ge(*state_ready.done(h, t))
                            st = (p_st, s_st)[i]
                            act.dma_start((pS, sS)[i][bass.ds(h, 1)].rearrange("a (d p) v -> p (a d) v", p=P),
                                           St[i][:, :, 0:DV]).then_inc(st.sem, 16)
                            if kind == "A":
                                n_out = OUT[("pn", "sn")[i]][0, 0][bass.ds(h, 1)].rearrange("a (d p b) -> p (a d) b", p=P, b=1)
                                act.dma_start(n_out, St[i][:, :, DV:NV], allow_slow_non_contiguous=True).then_inc(st.sem, 16)

            @block.vector
            def _(dve):
                if kind == "A":
                    dve.memset(v[:, DV:NV], 1.0).then_inc(filled.sem, 1)
                if kind == "C":
                    dve.memset(sT[:], 0.0).then_inc(filled.sem, 1)
                    dve.wait_ge(*filled.done(0, 0))
                with dve.Fori(0, H) as h:
                    link = Link(dve, lk, h)
                    if kind == "B":
                        for i in range(2):
                            dve.wait_ge(*qk_copied.done(h, 4 * i + 3))
                            x1, x2 = raw[:, 2 * i, :], raw[:, 2 * i + 1, :]
                            for a, b, out, op in ((x1, x2, 0, ALU.subtract), (x2, x1, 1, ALU.add)):
                                link(dve.tensor_tensor(ra[:], a, M.c("cos"), ALU.mult))
                                link(dve.tensor_tensor(rb[:], b, M.c("sin"), ALU.mult))
                                last = dve.tensor_tensor(qk[:, 2 * i + out, :], ra[:], rb[:], op)
                                if (i, out) == (1, 1):
                                    last.then_inc(qk_ready.sem, 1)
                                else:
                                    link(last)
                    elif kind == "C":
                        dve.wait_ge(*qk_copied.done(h, NP - 1))
                        link(dve.tensor_scalar(la[:], la[:], M["vec"][:, bass.ds(h + 64, 1)], None, ALU.add))
                        link(log_sigmoid(None, dve, la[:], lb[:], lc[:], la[:], Lg, h))
                        link(dve.tensor_scalar(la[:], la[:], 1.0 / 16.0, None, ALU.mult))
                        for t in range(T):
                            last = dve.tensor_tensor_scan(bT[:, cols(t)], M.c("ones")[:, 0:rows(t)], la[:, cols(t)], 0.0,
                                                          ALU.mult, ALU.add)
                        link(last)
                        for t in range(T):
                            mid = t * P + rows(t) // 2 - 1
                            end = t * P + rows(t) - 1
                            dve.tensor_copy(ends[:, 0, t:t + 1], bT[:, mid:mid + 1])
                            dve.tensor_copy(ends[:, 2, t:t + 1], bT[:, end:end + 1])
                            last = dve.tensor_scalar(ends[:, 1, t:t + 1], bT[:, end:end + 1], bT[:, mid:mid + 1], None, ALU.subtract)
                        link(last)
                        for t in range(T):
                            last = dve.tensor_scalar(la[:, cols(t)], bT[:, cols(t)], ends[:, 0, t:t + 1], None, ALU.subtract)
                        last.then_inc(shifted.sem, 1)
                        dve.wait_ge(*exps.done(h, 2))
                        link(dve.tensor_tensor(qk[:, 0, :], raw[:, 0, :], lb[:], ALU.mult))
                        dve.tensor_tensor(qk[:, 1, :], raw[:, 1, :], lc[:], ALU.mult).then_inc(qk_ready.sem, 1)
                    for t in range(T):
                        R, cs = rows(t), cols(t)
                        S = St[t // PT]
                        u = h + t * H
                        if kind == "A":
                            dve.scalar_tensor_tensor(arg[0:R, 0:R], M["negM"][0:R, bass.ds(h, 1), cs].rearrange("p a t -> p (a t)"),
                                                     M["ucol"][0:R, t, bass.ds(h, 1)], M.c("neg_causal", R)[:, 0:R],
                                                     ALU.add, ALU.add).then_inc(logit_ready.sem, 1)
                            dve.wait_ge(*decay_ready.done(h, t))
                        dve.wait_ge(*scores_psum.done(h, t))
                        if kind == "C":
                            dve.sem_inc(M.passed, 1)
                            dve.copy_predicated(sT[0:R, 0:R], M.c("mask", R)[:, 0:R].bitcast(U32), PS[4][0:R, 0:R]).then_inc(scores_ready.sem, 1)
                            dve.tensor_copy(kw[0:R, :], PS[4][0:R, P:2 * P]).then_inc(kw_ready.sem, 1)
                        else:
                            if kind == "A":
                                by, kc = E[0:R, 0:R], M["mcols"][0:R, 1, t, bass.ds(h, 1)]
                            else:
                                by = M["const"][0:R, bass.ds(h * P + M.at["decay"][0], R)]
                                kc = M["const"][0:R, bass.ds(h + M.at["k_decay"][0] + H * (t // PT), 1)]
                            dve.tensor_tensor(sT[0:R, 0:R], PS[4][0:R, 0:R], by, ALU.mult).then_inc(scores_ready.sem, 1)
                            dve.tensor_scalar(kw[0:R, :], PS[4][0:R, P:(1 + DT) * P], kc, None, ALU.mult).then_inc(kw_ready.sem, 1)
                        if t == PT:
                            dve.wait_ge(*sl.done(h, sl.per - 1))
                        if t == 0:
                            dve.wait_ge(*p_st.before(h, 0))
                        if t:
                            dve.wait_ge(*state_ready.before(h, t))
                        if kind == "C" and t:
                            dve.tensor_scalar(Sc[:], S[:, 0, :], eend[:, 0, t:t + 1], None, ALU.mult).then_inc(sc_ready.sem, 1)
                        dve.wait_ge(*tanh_done.done(h, t))
                        dve.wait_ge(*g_ready.before(h, t))
                        dve.scalar_tensor_tensor(zs[0:R, :], th[0:R, NG - DV:NG], 1.0, PS[2][0:R, NG - DV:NG], ALU.add, ALU.mult
                                                 ).then_inc(gates_used.sem, 1)
                        dve.wait_ge(*state_psum.done(h, t))
                        if kind == "C":
                            dve.tensor_scalar(nS[:], PS[0][:, 0:NV], eend[:, 1, t:t + 1], None, ALU.mult).then_inc(nS_ready.sem, 1)
                            dve.wait_ge(*nS_ready.done(h, t))
                            if t == 0:
                                dve.tensor_copy(S[:, 0, :], nS[:]).then_inc(state_ready.sem, 1)
                            else:
                                dve.scalar_tensor_tensor(S[:, 0, :], S[:, 0, :], eend[:, 2, t:t + 1], nS[:], ALU.mult, ALU.add
                                                         ).then_inc(state_ready.sem, 1)
                        else:
                            dec = (M["mcols"][:, 2, t, bass.ds(h, 1)] if kind == "A" else
                                   M["const"][:, bass.ds(h + M.at["s_decay"][0] + H * (t // PT), 1)])
                            for d in range(DT):
                                if t == 0:
                                    last = dve.tensor_copy(S[:, d, :], PS[d][:, 0:NV])
                                else:
                                    last = dve.scalar_tensor_tensor(S[:, d, :], S[:, d, :], dec, PS[d][:, 0:NV], ALU.mult, ALU.add)
                            last.then_inc(state_ready.sem, 1)
                        dve.wait_ge(*intra_copied.done(h, t))
                        n_src = num_a
                        if t and kind != "C":
                            w = (M["mcols"][0:R, 0, t, bass.ds(h, 1)] if kind == "A" else
                                 M["const"][0:R, bass.ds(h + M.at["q_decay"][0], 1)])
                            dve.scalar_tensor_tensor(num[0:R, :], PS[5][0:R, 0:NV], w, num_a[0:R, :], ALU.mult, ALU.add
                                                     ).then_inc(num_ready.sem, 1)
                            dve.wait_ge(*num_ready.done(h, t - 1))
                            n_src = num
                        if kind == "A":
                            dcol = n_src[0:R, DV:NV]
                            dve.scalar_tensor_tensor(sm[0:R, 0:1], dcol, -1.0, dcol, ALU.mult, ALU.max).then_inc(den.sem, 1)
                            dve.wait_ge(*den.done(h, 4 * t))
                            dve.tensor_tensor(sm[0:R, 1:2], sm[0:R, 0:1], M["mcols"][0:R, 3, t, bass.ds(h, 1)], ALU.max).then_inc(den.sem, 1)
                            dve.wait_ge(*den.done(h, 4 * t + 1))
                            dve.reciprocal(sm[0:R, 2:3], sm[0:R, 1:2]).then_inc(den.sem, 1)
                            dve.wait_ge(*den.done(h, 4 * t + 2))
                            dve.tensor_scalar(hg[0:R, :], n_src[0:R, 0:DV], sm[0:R, 2:3], None, ALU.mult).then_inc(den.sem, 1)
                            dve.wait_ge(*den.done(h, 4 * t + 3))
                            dve.scalar_tensor_tensor(hg[0:R, :], th[0:R, 0:DV], 1.0, hg[0:R, :], ALU.add, ALU.mult).then_inc(hg_ready.sem, 1)
                            fin = hg
                        else:
                            fin = n_src
                        dve.wait_ge(*rstd_ready.done(h, t))
                        dve.wait_ge(*gates_used.done(h, t))
                        dve.wait_ge(*gT_psum.before(h, t))
                        dve.scalar_tensor_tensor(g[0:R, :], fin[0:R, 0:DV], sm[0:R, 5:6], zs[0:R, :], ALU.mult, ALU.mult
                                                 ).then_inc(g_ready.sem, 1)
                        for tt in ([t - 1] if t else []) + ([t] if t == T - 1 else []):
                            dve.wait_ge(*gT_psum.done(h, tt))
                            for d in range(2):
                                last = dve.tensor_scalar(M["gT"][:, bass.ds(h * 2 + (g_row + d), 1), cols(tt)].rearrange("p a t -> p (a t)"),
                                                         PS[7][:, d * P:d * P + rows(tt)], M["vec"][:, bass.ds(h * 2 + (g_col + d), 1)],
                                                         None, ALU.mult)
                            last.then_inc(gT_copied.sem, 1)
                    link.close()


def odd_gates(nc, M, IN, OUT):
    with Phase(nc, "odd_gates") as ph:
        act_norm, pool_norm, dve_norm, pe_norm = norm_steps(ph, M, 1)
        H = GDN_H
        sb, sig = ph.sb, ph.counter
        wg = sb("w_gates", [P, KT, RANK + 2 * H])
        dt_b, a_l = sb("dt_bias", [H, 1]), sb("a_log", [H, 1])
        ndt, ea = sb("minus_dt", [H, 1]), sb("exp_a", [H, 1])
        cache = sb("cache_rows", [72, P])
        gi, ta, tb = (sb(n, [H, 2, TOK]) for n in ("gate_in", "ls_a", "ls_b"))
        ge_rows = sb("ge_rows", [H, T, H])
        col, bro = sb("gate_cols", [P, 2, T, H]), sb("gate_broadcast", [P, T, H])
        arg = sb("gate_args", [P, 5, T, H])
        wl = sig("w_gates_loaded", 16 * 5)
        proj, copied = sig("gates_psum", 3), sig("gates_copied", 6)
        S = {n: sig("ls_" + n) for n in ("abs", "exp", "plus", "log")}
        lk = sig("vector_step")
        exp_a, rows_ready, colsp, args_ready, exps = (sig(n) for n in ("exp_a_ready", "rows_ready", "cols_psum", "args_ready", "gate_exps"))
        signs, beta = sig("minus_dt_ready"), sig("beta_halved")
        cachep, cachec = sig("cache_psum"), sig("cache_copied")
        PS = M["ps"]
        rows_g = M["grow"]
        with nc.Block() as block:

            @block.sync
            def _(sp):
                w_in = IN["w_in_odd"][0].rearrange("(k p) n -> p k n", p=P)
                sp.dma_start(wg[:, :, 0:RANK], w_in[:, :, 2 * D:2 * D + RANK]).then_inc(wl.sem, 16)
                sp.dma_start(wg[:, :, RANK:], w_in[:, :, 5 * D + RANK:5 * D + RANK + 2 * H]).then_inc(wl.sem, 16)
                sp.dma_start(dt_b[:], IN["dt_bias"][0].rearrange("(h a) -> h a", a=1)).then_inc(wl.sem, 16)
                sp.dma_start(a_l[:], IN["a_log"][0].rearrange("(h a) -> h a", a=1)).then_inc(wl.sem, 16)
                sp.dma_start(cache[:], IN["cache_gdn_conv"][0, 0].rearrange("r (c p) -> (r c) p", p=P)).then_inc(wl.sem, 16)

            @block.gpsimd
            def _(pool):
                pool_norm(pool)

            @block.tensor
            def _(pe):
                pe_norm(pe)
                pe.wait_ge(*wl.done(0, 79))
                small_projection(pe, M, wg, 0, RANK, (4, 5)).then_inc(proj.sem, 1)
                small_projection(pe, M, wg, RANK, H, (6, 7)).then_inc(proj.sem, 1)
                pe.transpose(PS[1][:, 0:72], cache[:], M.c("ident", 72, 72)).then_inc(cachep.sem, 1)
                pe.wait_ge(*copied.done(0, 1))
                small_projection(pe, M, wg, RANK + H, H, (4, 5)).then_inc(proj.sem, 1)
                pe.wait_ge(*rows_ready.done(0, 0))
                for n, r in enumerate((rows_g[:, 0, :], gi[:, 1, :])):
                    for t in range(T):
                        at = (n * T + t) * H
                        pe.transpose(PS[0][0:rows(t), at:at + H], r[:, cols(t)], M.c("ident", H, H))
                pe.matmul(PS[2][:, 0:T * H], M.c("ones", H), ge_rows[:].rearrange("p t h -> p (t h)"),
                          start=True, stop=True).then_inc(colsp.sem, 1)

            @block.scalar
            def _(act):
                act_norm(act)
                act.wait_ge(*wl.done(0, 79))
                act.activation(ea[:], a_l[:], ACT.Exp).then_inc(exp_a.sem, 1)
                act.wait_ge(*signs.done(0, 0))
                for i in range(3):
                    act.wait_ge(*proj.done(0, i))
                    for half in range(2):
                        to = slice(half * HALF, (half + 1) * HALF)
                        src = PS[(4, 6, 4)[i] + half]
                        if i == 1:
                            act.activation(gi[:, 0, to], src[0:H, 0:HALF], ACT.Identity, bias=ndt[:], scale=-1.0).then_inc(copied.sem, 1)
                        else:
                            n = (RANK, 0, H)[i]
                            out = M["a1T"][:, to] if i == 0 else gi[:, 1, to]
                            act.activation(out, src[0:n, 0:HALF], ACT.Copy).then_inc(copied.sem, 1)
                log_sigmoid(act, None, None, ta[:], tb[:], None, S)
                act.wait_ge(*args_ready.done(0, 0))
                act.activation(M["gcols"][:], arg[:], ACT.Exp).then_inc(exps.sem, 1)

            @block.vector
            def _(dve):
                link = Link(dve, lk)
                dve.memset(col[:], 0.0)
                dve.wait_ge(*wl.done(0, 79))
                dve.tensor_scalar(ndt[:], dt_b[:], -1.0, None, ALU.mult).then_inc(signs.sem, 1)
                dve_norm(dve)
                dve.wait_ge(*cachep.done(0, 0))
                dve.tensor_copy(M["cacheT"][:], PS[1][:, 0:72]).then_inc(cachec.sem, 1)
                dve.wait_ge(*copied.done(0, 5))
                link(log_sigmoid(None, dve, gi[:], ta[:], tb[:], gi[:], S))
                dve.wait_ge(*exp_a.done(0, 0))
                link(dve.tensor_scalar(gi[:, 0, :], gi[:, 0, :], ea[:], None, ALU.mult))
                for t in range(T):
                    last = dve.tensor_tensor_scan(rows_g[:, 0, cols(t)], M.c("ones", H, rows(t)), gi[:, 0, cols(t)], 0.0, ALU.mult, ALU.add)
                link(last)
                dve.tensor_tensor(rows_g[:, 1, :], rows_g[:, 0, :], gi[:, 1, :], ALU.add)
                for t in range(T):
                    end = t * P + rows(t) - 1
                    last = dve.tensor_scalar(ge_rows[:, t, :], M.c("diag8", H)[:, 0:H], rows_g[:, 0, end:end + 1], None, ALU.mult)
                last.then_inc(rows_ready.sem, 1)
                dve.wait_ge(*colsp.done(0, 0))
                src = PS[0][:, 0:2 * T * H].rearrange("p (n t h) -> p n t h", n=2, t=T)
                dve.tensor_copy(col[:, :, 0:PT, :], src[:, :, 0:PT, :])
                dve.tensor_copy(col[0:DEC, :, PT, :], src[0:DEC, :, PT, :])
                link(dve.tensor_copy(bro[:].rearrange("p t h -> p (t h)"), PS[2][:, 0:T * H]))
                dve.tensor_copy(M["Gcol"][:], col[:, 0])
                dve.tensor_copy(arg[:, 0], col[:, 0])
                dve.tensor_tensor(arg[:, 1], col[:, 0], col[:, 1], ALU.add)
                dve.tensor_copy(arg[:, 2], col[:, 1])
                dve.tensor_tensor(arg[:, 3], bro[:], col[:, 0], ALU.subtract)
                dve.tensor_copy(arg[:, 4], bro[:]).then_inc(args_ready.sem, 1)
                dve.wait_ge(*exps.done(0, 0))
                dve.tensor_scalar(M["gcols"][:, 2], M["gcols"][:, 2], 0.5, None, ALU.mult).then_inc(beta.sem, 1)


def gdn_heads(nc, M, IN, OUT):
    H = GDN_H
    NL = len(LEVELS) - 1
    W = 3 + SEQ + 3 + DEC
    C = W - 3
    S0 = SEQ + 3
    PS = M["ps"]
    w_in = IN["w_in_odd"][0].rearrange("(k p) n -> p k n", p=P)
    sec = [2 * D + RANK + i * D for i in range(3)]
    z0 = 6 * D + RANK + 2 * H

    def conv_cols(t):
        return slice(t * P, (t + 1) * P) if t < PT else slice(S0, S0 + DEC)

    with Phase(nc, "gdn", first=1) as ph:
        sb, sig = ph.sb, ph.counter
        wT, wz = sb("w_qkv", [P, KT, 3 * P]), sb("w_z", [P, KT, P])
        pj, cv, thc = sb("pre_conv", [P, 3, W]), sb("conv", [P, 3, C]), sb("tanh_conv", [P, 3, C])
        tk = sb("qkv_tokens", [P, T, 3, P])
        sqs = thc[:].rearrange("p a b -> p (a b)")[:, 0:T * 2 * P].rearrange("p (t a d) -> p t a d", t=T, a=2)
        kn, qn, kbe, kg, bv = (sb(n, [P, T, P]) for n in ("k_norm", "q_norm", "k_beta_decay", "k_end", "v_beta"))
        ss, ms, rn, mh = (sb(n, [P, T, 2]) for n in ("ss2", "ms2", "rn2", "minus_half"))
        sc = sb("scales", [P, 4, T])
        kT, qT = sb("kT", [P, TOK]), sb("qT", [P, TOK])
        gsel = sb("G_selected", [H, 2, TOK])
        E = sb("E", [P, 2, TOK])
        AT, atT = sb("AT", [P, TOK]), sb("attnT", [P, TOK])
        X, XT, Q = sb("X", [P, TOK]), sb("XT", [P, TOK]), sb("Q", [P, TOK])
        ML = sb("A_level", [P, 2, TOK])
        wN = sb("w_minus_T", [P, TOK])
        u, o_a, o, g, sqj = (sb(n, [P, P]) for n in ("u", "o_intra", "o", "g", "squares"))
        zs, tz = sb("z_silu", [P, T, P]), sb("tanh_z", [P, T, P])
        sm = sb("small", [P, 4])
        St = [sb("state_prompt", [P, P]), sb("state_sample", [P, P])]
        newc = sb("new_cache", [P, 2, 72])
        cr = sb("new_cache_rows", [72, 2, P])

        names = {"w_loaded": 48, "wz_loaded": 16, "state_loaded": 16, "prompt_stored": 16, "sample_stored": 16,
                 "gsel_ready": 1, "G_psum": 1, "arg_ready": 1, "E_ready": 2, "proj_psum": 6, "proj_copied": 6, "cache_put": 1,
                 "conv_step": 9, "conv_ready": 3, "tanh_conv": 3, "silu_ready": 3, "cache_saved": 1, "z_psum": 1, "tanh_z": 1, "z_used": 1,
                 "tok_psum": T, "tok_copied": T, "tok_squared": 1, "ss_ready": 1, "ms_ready": 1, "rn_ready": 1, "scale_a": 1, "scale_b": 1,
                 "kq_norm": 1, "kq_psum": 1, "kq_copied": 1, "kk_psum": 1, "A_ready": 1, "attn_ready": 1, "level_ready": NL,
                 "A1_ready": 1, "XT1_ready": 1, "X1_psum": 1, "X1_copied": 1,
                 "Q_psum": NL, "Q_copied": NL, "XX_psum": NL, "X_ready": NL, "w_psum": 1, "w_copied": 1, "kv_scaled": 1,
                 "u_psum": T, "u_copied": T, "o_psum": T, "o_copied": T, "o_ready": PT, "squared": T, "mean_ready": T, "rstd_ready": T,
                 "state_psum": T, "state_ready": T, "g_ready": T, "gT_psum": T, "gT_copied": T}
        s = {n: sig(n, k) for n, k in names.items()}
        cleared = sig("cleared")
        cacheT_psum, cacheT_copied, cache_stored = sig("cache_psum", 2), sig("cache_copied", 2), sig("cache_stored", 32)

        def tiles(x, t):
            return x[0:rows(t), t * P:t * P + rows(t)]

        def bank(n, t):
            return PS[n[0]][:, t * P:(t + 1) * P] if t < PT else PS[5][0:DEC, n[1]:n[1] + DEC]

        nc.all_engine_barrier()
        with nc.Block() as block:

            @block.sync
            def _(sp):
                with sp.Fori(0, H) as h:
                    sp.wait_ge(*s["proj_psum"].before(h, 0))
                    for i in range(3):
                        sp.dma_start(wT[:, :, i * P:(i + 1) * P], w_in[:, :, bass.ds(h * P + sec[i], P)]).then_inc(s["w_loaded"].sem, 16)
                    sp.wait_ge(*s["z_psum"].before(h, 0))
                    sp.dma_start(wz[:], w_in[:, :, bass.ds(h * P + z0, P)]).then_inc(s["wz_loaded"].sem, 16)
                sp.wait_ge(*s["prompt_stored"].before(H, 0))
                sp.wait_ge(*s["sample_stored"].before(H, 0))
                for i, name in enumerate(("pconv", "sconv")):
                    sp.wait_ge(*cacheT_copied.done(0, i))
                    sp.dma_start(OUT[name][0, 0].rearrange("r (c p) -> (r c) p", p=P), cr[:, i, :]).then_inc(cache_stored.sem, 16)
                sp.wait_ge(*cache_stored.done(0, 31))

            @block.gpsimd
            def _(pool):
                pool.memset(mh[:], -0.5)
                with pool.Fori(0, H) as h:
                    pool.wait_ge(*s["ss_ready"].done(h, 0))
                    pool.sem_inc(M.passed, 1)
                    pool.tensor_scalar(ms[:], ss[:], 0.25, EPS, ALU.mult, ALU.add).then_inc(s["ms_ready"].sem, 1)
                    pool.wait_ge(*s["ms_ready"].done(h, 0))
                    pool.tensor_tensor(rn[:], ms[:], mh[:], ALU.pow).then_inc(s["rn_ready"].sem, 1)
                    pool.wait_ge(*s["A_ready"].done(h, 0))
                    for n in range(NL):
                        if n >= 2:
                            pool.wait_ge(*s["Q_psum"].done(h, n - 2))
                        lev = M.c("levels")[:, (n + 1) * P:(n + 2) * P]
                        for t in range(T if n < NL - 1 else PT):
                            R = rows(t)
                            last = pool.tensor_tensor(tiles(ML[:, n % 2, :], t), tiles(AT, t), lev[0:R, 0:R], ALU.mult)
                        last.then_inc(s["level_ready"].sem, 1)
                    for t in range(T):
                        R = rows(t)
                        pool.wait_ge(*s["squared"].done(h, t))
                        pool.sem_inc(M.passed, 1)
                        pool.tensor_scalar(sm[0:R, 1:2], sm[0:R, 0:1], 1.0 / P, EPS, ALU.mult, ALU.add).then_inc(s["mean_ready"].sem, 1)
                        pool.wait_ge(*s["mean_ready"].done(h, t))
                        pool.tensor_tensor(sm[0:R, 2:3], sm[0:R, 1:2], M.c("half", R), ALU.pow).then_inc(s["rstd_ready"].sem, 1)

            @block.tensor
            def _(pe):
                with pe.Fori(0, H) as h:
                    pe.wait_ge(*s["gsel_ready"].done(h, 0))
                    pe.wait_ge(*s["state_ready"].before(h, 0))
                    pe.wait_ge(*s["o_ready"].before(h, 0))
                    pe.wait_ge(*s["o_copied"].before(h, 0))
                    pe.wait_ge(*s["u_copied"].before(h, 0))
                    for i in range(2):
                        pe.matmul(PS[6 + i][:, 0:SEQ], M.c("ones", H), gsel[:, i, 0:SEQ], start=True, stop=True)
                        last = pe.matmul(PS[4][:, i * DEC:(i + 1) * DEC], M.c("ones", H), gsel[:, i, SEQ:TOK], start=True, stop=True)
                    last.then_inc(s["G_psum"].sem, 1)
                    pe.wait_ge(*s["w_loaded"].done(h, 47))
                    for n in range(6):
                        ct, half = n // 2, n % 2
                        pe.wait_ge(*(s["proj_copied"].done(h, n - 2) if n >= 2 else s["proj_copied"].before(h, 0)))
                        matmul_chain(pe, PS[half][:, 0:HALF], [(wT[:, k, ct * P:(ct + 1) * P], M["hT"][:, k, half * HALF:(half + 1) * HALF])
                                                               for k in range(KT)]).then_inc(s["proj_psum"].sem, 1)
                    pe.wait_ge(*s["wz_loaded"].done(h, 15))
                    for t in range(T):
                        out = PS[2][:, t * P:(t + 1) * P] if t < PT else PS[3][0:DEC, 0:P]
                        last = matmul_chain(pe, out, [(M["hT"][:, k, cols(t)], wz[:, k, :]) for k in range(KT)])
                    last.then_inc(s["z_psum"].sem, 1)
                    pe.wait_ge(*s["arg_ready"].done(h, 0))
                    pe.wait_ge(*s["silu_ready"].done(h, 2))
                    for t in range(T):
                        R = rows(t)
                        pe.wait_ge(*(s["tok_copied"].done(h, t - 2) if t >= 2 else s["gT_copied"].before(h, 0)))
                        pe.sem_inc(M.passed, 1)
                        for i in range(3):
                            last = pe.transpose(PS[4 + t % 2][0:R, i * P:(i + 1) * P], cv[:, i, conv_cols(t)], M.c("ident", P, P))
                        last.then_inc(s["tok_psum"].sem, 1)
                    pe.wait_ge(*s["kq_norm"].done(h, 0))
                    for i, x in enumerate((kn, qn)):
                        for t in range(T):
                            R = rows(t)
                            out = PS[6 + i][:, t * P:(t + 1) * P] if t < PT else PS[4][:, i * DEC:(i + 1) * DEC]
                            last = pe.transpose(out, x[0:R, t, :], M.c("ident", R, R))
                    last.then_inc(s["kq_psum"].sem, 1)
                    pe.wait_ge(*s["kq_copied"].done(h, 0))
                    pe.wait_ge(*s["z_used"].done(h, 0))
                    for i, x in enumerate((kT, qT)):
                        for t in range(T):
                            last = pe.matmul(bank((2 + i, i * DEC), t), kT[:, cols(t)], x[:, cols(t)], start=True, stop=True)
                    last.then_inc(s["kk_psum"].sem, 1)
                    pe.wait_ge(*s["XT1_ready"].done(h, 0))
                    pe.wait_ge(*s["attn_ready"].done(h, 0))
                    for t in range(T):
                        last = pe.transpose(bank((4, 0), t), tiles(XT, t), M.c("ident", rows(t), rows(t)))
                    last.then_inc(s["X1_psum"].sem, 1)
                    pe.wait_ge(*s["X1_copied"].done(h, 0))
                    for n in range(NL):
                        n_t = T if n < NL - 1 else PT
                        pe.wait_ge(*s["level_ready"].done(h, n))
                        if n:
                            pe.wait_ge(*s["X_ready"].done(h, n - 1))
                        for t in range(n_t):
                            last = pe.matmul(bank((2, 2 * DEC), t), tiles(ML[:, n % 2, :], t), tiles(X, t), start=True, stop=True)
                        last.then_inc(s["Q_psum"].sem, 1)
                        pe.wait_ge(*s["Q_copied"].done(h, n))
                        for t in range(n_t):
                            if n < NL - 1:
                                pe.matmul(bank((3, 0), t), tiles(XT, t), tiles(Q, t), start=True, stop=True)
                            last = pe.matmul(bank((4, DEC), t), tiles(Q, t), tiles(XT, t), start=True, stop=True)
                        last.then_inc(s["XX_psum"].sem, 1)
                    pe.wait_ge(*s["X_ready"].done(h, NL - 1))
                    pe.wait_ge(*s["kv_scaled"].done(h, 0))
                    for t in range(T):
                        R = rows(t)
                        out = PS[2][:, t * P:t * P + R] if t < PT else PS[5][:, 0:DEC]
                        last = pe.matmul(out, kbe[0:R, t, :], tiles(XT, t), start=True, stop=True)
                    last.then_inc(s["w_psum"].sem, 1)
                    pe.wait_ge(*s["w_copied"].done(h, 0))

                    def turn_g(t):
                        pe.wait_ge(*s["g_ready"].done(h, t))
                        pe.wait_ge(*s["gT_copied"].before(h, t))
                        pe.sem_inc(M.passed, 1)
                        pe.transpose(PS[5][:, 0:rows(t)], g[0:rows(t), :], M.c("ident", rows(t), rows(t))).then_inc(s["gT_psum"].sem, 1)

                    for t in range(T):
                        R, S = rows(t), St[t // PT]
                        if t:
                            pe.wait_ge(*s["state_ready"].before(h, t))
                        if t == PT:
                            pe.wait_ge(*s["state_loaded"].done(h, 15))
                        pe.wait_ge(*s["u_copied"].before(h, t))
                        pairs = [(tiles(XT, t), bv[0:R, t, :])] + ([(wN[:, cols(t)], S[:])] if t else [])
                        pe.sem_inc(M.passed, 1)
                        matmul_chain(pe, PS[6][0:R, 0:P], pairs).then_inc(s["u_psum"].sem, 1)
                        pe.wait_ge(*s["o_copied"].before(h, t))
                        if t:
                            pe.wait_ge(*s["o_ready"].before(h, t - 1))
                            pe.matmul(PS[7][0:R, 0:P], qT[:, cols(t)], S[:], start=True, stop=True)
                        pe.wait_ge(*s["u_copied"].done(h, t))
                        pe.sem_inc(M.passed, 1)
                        pe.matmul(PS[7][0:R, P:2 * P], tiles(atT, t), u[0:R, :], start=True, stop=True).then_inc(s["o_psum"].sem, 1)
                        pe.matmul(PS[4][:, 0:P], kg[0:R, t, :], u[0:R, :], start=True, stop=True).then_inc(s["state_psum"].sem, 1)
                        if t:
                            turn_g(t - 1)
                    turn_g(T - 1)
                pe.wait_ge(*s["cache_saved"].before(H, 0))
                pe.wait_ge(*s["gT_copied"].before(H, 0))
                for i in range(2):
                    pe.transpose(PS[i][0:72, 0:P], newc[:, i, :], M.c("ident", P, P)).then_inc(cacheT_psum.sem, 1)

            @block.scalar
            def _(act):
                with act.Fori(0, H) as h:
                    act.wait_ge(*s["sample_stored"].before(h, 0))
                    act.dma_start(St[1][:], IN["state_gdn"][0, 0][bass.ds(h, 1)].rearrange("a p v -> p (a v)")).then_inc(s["state_loaded"].sem, 16)
                    act.wait_ge(*s["arg_ready"].done(h, 0))
                    act.activation(E[:, :, 0:SEQ], E[:, :, 0:SEQ], ACT.Exp).then_inc(s["E_ready"].sem, 1)
                    act.activation(E[0:DEC, :, SEQ:TOK], E[0:DEC, :, SEQ:TOK], ACT.Exp).then_inc(s["E_ready"].sem, 1)
                    for n in range(6):
                        ct, half = n // 2, n % 2
                        act.wait_ge(*s["proj_psum"].done(h, n))
                        if n == 0:
                            act.wait_ge(*s["cache_saved"].before(h, 0))
                        if half == 0:
                            act.activation(pj[:, ct, 3:3 + HALF], PS[0][:, 0:HALF], ACT.Copy).then_inc(s["proj_copied"].sem, 1)
                        else:
                            act.activation(pj[:, ct, 3 + HALF:3 + SEQ], PS[1][:, 0:SEQ - HALF], ACT.Copy)
                            act.activation(pj[:, ct, 6 + SEQ:W], PS[1][:, SEQ - HALF:HALF], ACT.Copy).then_inc(s["proj_copied"].sem, 1)
                    for ct in range(3):
                        act.wait_ge(*s["conv_ready"].done(h, ct))
                        act.activation(thc[:, ct, :], cv[:, ct, :], ACT.Tanh, scale=0.5).then_inc(s["tanh_conv"].sem, 1)
                    act.wait_ge(*s["z_psum"].done(h, 0))
                    act.wait_ge(*s["z_used"].before(h, 0))
                    act.activation(tz[:, 0:PT, :], PS[2][:, :].rearrange("p (t d) -> p t d", t=PT), ACT.Tanh, scale=0.5)
                    act.activation(tz[0:DEC, PT, :], PS[3][0:DEC, 0:P], ACT.Tanh, scale=0.5).then_inc(s["tanh_z"].sem, 1)
                    for t in range(T):
                        R = rows(t)
                        act.wait_ge(*s["tok_psum"].done(h, t))
                        act.activation(tk[0:R, t, :, :], PS[4 + t % 2][0:R, 0:3 * P].rearrange("p (a d) -> p a d", a=3), ACT.Copy
                                       ).then_inc(s["tok_copied"].sem, 1)
                    act.wait_ge(*s["tok_copied"].done(h, T - 1))
                    act.wait_ge(*s["silu_ready"].done(h, 2))
                    act.activation(sqs, tk[:, :, 0:2, :], ACT.Square).then_inc(s["tok_squared"].sem, 1)
                    act.wait_ge(*s["kq_psum"].done(h, 0))
                    for i, x in enumerate((kT, qT)):
                        act.activation(x[:, 0:SEQ], PS[6 + i][:, 0:SEQ], ACT.Copy)
                        last = act.activation(x[:, SEQ:TOK], PS[4][:, i * DEC:(i + 1) * DEC], ACT.Copy)
                    last.then_inc(s["kq_copied"].sem, 1)
                    act.wait_ge(*s["X1_psum"].done(h, 0))
                    act.activation(X[:, 0:SEQ], PS[4][:, :], ACT.Copy)
                    act.activation(X[0:DEC, SEQ:TOK], PS[5][0:DEC, 0:DEC], ACT.Copy).then_inc(s["X1_copied"].sem, 1)
                    for n in range(NL):
                        act.wait_ge(*s["Q_psum"].done(h, n))
                        last = act.activation(Q[:, 0:SEQ], PS[2][:, :], ACT.Copy)
                        if n < NL - 1:
                            last = act.activation(Q[0:DEC, SEQ:TOK], PS[5][0:DEC, 2 * DEC:3 * DEC], ACT.Copy)
                        last.then_inc(s["Q_copied"].sem, 1)
                    act.wait_ge(*s["w_psum"].done(h, 0))
                    act.activation(wN[:, 0:SEQ], PS[2][:, :], ACT.Copy, scale=-1.0)
                    act.activation(wN[:, SEQ:TOK], PS[5][:, 0:DEC], ACT.Copy, scale=-1.0).then_inc(s["w_copied"].sem, 1)
                    for t in range(T):
                        R = rows(t)
                        act.wait_ge(*s["u_psum"].done(h, t))
                        act.wait_ge(*s["state_psum"].before(h, t))
                        act.activation(u[0:R, :], PS[6][0:R, 0:P], ACT.Copy).then_inc(s["u_copied"].sem, 1)
                        act.wait_ge(*s["o_psum"].done(h, t))
                        act.wait_ge(*s["g_ready"].before(h, t))
                        act.activation(o_a[0:R, :], PS[7][0:R, P:2 * P], ACT.Copy).then_inc(s["o_copied"].sem, 1)
                        act.wait_ge(*(s["o_ready"].done(h, t - 1) if t else s["o_copied"].done(h, t)))
                        act.activation(sqj[0:R, :], (o if t else o_a)[0:R, :], ACT.Square, accum_out=sm[0:R, 0:1]).then_inc(s["squared"].sem, 1)
                        if t >= PT - 1:
                            i = t - PT + 1
                            act.wait_ge(*s["state_ready"].done(h, t))
                            act.dma_start(OUT[("pgdn", "sgdn")[i]][0, 0][bass.ds(h, 1)].rearrange("a p v -> p (a v)"), St[i][:]
                                           ).then_inc(s[("prompt_stored", "sample_stored")[i]].sem, 16)

            @block.vector
            def _(dve):
                dve.memset(tk[:], 0.0)
                dve.memset(pj[:, :, 0:3], 0.0).then_inc(cleared.sem, 1)
                with dve.Fori(0, H) as h:
                    dve.wait_ge(*s["G_psum"].before(h, 0))
                    dve.tensor_scalar(gsel[:], M["grow"][:], M["const"][0:H, bass.ds(h + M.at["diag8"][0], 1)], None, ALU.mult
                                      ).then_inc(s["gsel_ready"].sem, 1)
                    dve.wait_ge(*s["G_psum"].done(h, 0))
                    dve.wait_ge(*s["attn_ready"].before(h, 0))
                    for i, name in ((1, "neg_strict"), (0, "neg_causal")):
                        for t in range(T):
                            R = rows(t)
                            src = PS[6 + i][0:R, t * P:t * P + R] if t < PT else PS[4][0:R, i * DEC:(i + 1) * DEC]
                            last = dve.scalar_tensor_tensor(E[0:R, i, t * P:t * P + R], src, M["Gcol"][0:R, t, bass.ds(h, 1)],
                                                            M.c(name, R)[:, 0:R], ALU.subtract, ALU.add)
                    last.then_inc(s["arg_ready"].sem, 1)
                    for ct in range(3):
                        if ct == 0:
                            dve.wait_ge(*s["cache_saved"].before(h, 0))
                            dve.wait_ge(*s["tok_psum"].before(h, 0))
                            for c in range(3):
                                last = dve.tensor_copy(pj[:, c, S0:S0 + 3], cacheT_of(M, h, c))
                            last.then_inc(s["cache_put"].sem, 1)
                            dve.wait_ge(*s["cache_put"].done(h, 0))
                        dve.wait_ge(*s["proj_copied"].done(h, 2 * ct + 1))
                        for j in range(4):
                            wj = M["conv"][:, bass.ds(h + (24 * j + 8 * ct), 1)]
                            if j == 0:
                                ins = dve.tensor_scalar(cv[:, ct, :], pj[:, ct, 0:C], wj, None, ALU.mult)
                            else:
                                ins = dve.scalar_tensor_tensor(cv[:, ct, :], pj[:, ct, j:j + C], wj, cv[:, ct, :], ALU.mult, ALU.add)
                            if j < 3:
                                ins.then_inc(s["conv_step"].sem, 1)
                                dve.wait_ge(*s["conv_step"].done(h, 3 * ct + j))
                            else:
                                ins.then_inc(s["conv_ready"].sem, 1)
                    for ct in range(3):
                        for i, c0 in enumerate((SEQ, W - 3)):
                            last = dve.tensor_copy(new_cache_of(newc, i, h, ct), pj[:, ct, c0:c0 + 3])
                    last.then_inc(s["cache_saved"].sem, 1)
                    for ct in range(3):
                        dve.wait_ge(*s["tanh_conv"].done(h, ct))
                        dve.scalar_tensor_tensor(cv[:, ct, :], thc[:, ct, :], 1.0, cv[:, ct, :], ALU.add, ALU.mult).then_inc(s["silu_ready"].sem, 1)
                    dve.wait_ge(*s["tanh_z"].done(h, 0))
                    dve.wait_ge(*s["g_ready"].before(h, 0))
                    dve.scalar_tensor_tensor(zs[:, 0:PT, :], tz[:, 0:PT, :], 1.0, PS[2][:, :].rearrange("p (t d) -> p t d", t=PT), ALU.add, ALU.mult)
                    dve.scalar_tensor_tensor(zs[0:DEC, PT, :], tz[0:DEC, PT, :], 1.0, PS[3][0:DEC, 0:P], ALU.add, ALU.mult).then_inc(s["z_used"].sem, 1)
                    dve.wait_ge(*s["tok_squared"].done(h, 0))
                    dve.tensor_reduce(ss[:], sqs, AX.X, ALU.add).then_inc(s["ss_ready"].sem, 1)
                    dve.wait_ge(*s["rn_ready"].done(h, 0))
                    dve.wait_ge(*s["kv_scaled"].before(h, 0))
                    dve.tensor_scalar(sc[:, 0, :], rn[:, :, 1], 0.5, None, ALU.mult)
                    dve.tensor_scalar(sc[:, 1, :], rn[:, :, 0], 0.5 * P ** -0.5, None, ALU.mult).then_inc(s["scale_a"].sem, 1)
                    dve.wait_ge(*s["scale_a"].done(h, 0))

                    def gcol(i):
                        return M["gcols"][:, i, :, bass.ds(h, 1)].rearrange("p t a -> p (t a)")

                    def spread(x):
                        return x.rearrange("p (t a) -> p t a", a=1).broadcast_to([P, T, P])

                    dve.tensor_tensor(kn[:], tk[:, :, 1, :], spread(sc[:, 0, :]), ALU.mult)
                    dve.tensor_tensor(qn[:], tk[:, :, 0, :], spread(sc[:, 1, :]), ALU.mult).then_inc(s["kq_norm"].sem, 1)
                    dve.tensor_tensor(sc[:, 2, :], sc[:, 0, :], gcol(1), ALU.mult)
                    dve.tensor_tensor(sc[:, 3, :], sc[:, 0, :], gcol(3), ALU.mult).then_inc(s["scale_b"].sem, 1)
                    dve.wait_ge(*s["scale_b"].done(h, 0))
                    dve.tensor_tensor(kbe[:], tk[:, :, 1, :], spread(sc[:, 2, :]), ALU.mult)
                    dve.tensor_tensor(kg[:], tk[:, :, 1, :], spread(sc[:, 3, :]), ALU.mult)
                    for t in range(T):
                        last = dve.tensor_scalar(bv[:, t, :], tk[:, t, 2, :], M["gcols"][:, 2, t, bass.ds(h, 1)], None, ALU.mult)
                    last.then_inc(s["kv_scaled"].sem, 1)
                    dve.wait_ge(*s["kk_psum"].done(h, 0))
                    dve.wait_ge(*s["E_ready"].done(h, 1))
                    dve.tensor_tensor(AT[:, 0:SEQ], PS[2][:, :], E[:, 1, 0:SEQ], ALU.mult)
                    dve.tensor_tensor(AT[0:DEC, SEQ:TOK], PS[5][0:DEC, 0:DEC], E[0:DEC, 1, SEQ:TOK], ALU.mult).then_inc(s["A_ready"].sem, 1)
                    dve.wait_ge(*s["A_ready"].done(h, 0))
                    for t in range(T):
                        R = rows(t)
                        last = dve.tensor_tensor(tiles(Q, t), tiles(AT, t), M.c("levels", R)[:, 0:R], ALU.mult)
                    last.then_inc(s["A1_ready"].sem, 1)
                    dve.wait_ge(*s["A1_ready"].done(h, 0))
                    for t in range(T):
                        R = rows(t)
                        last = dve.tensor_tensor(tiles(XT, t), M.c("ident", R, R), tiles(Q, t), ALU.subtract)
                    last.then_inc(s["XT1_ready"].sem, 1)
                    dve.tensor_tensor(atT[:, 0:SEQ], PS[3][:, :], E[:, 0, 0:SEQ], ALU.mult)
                    dve.tensor_tensor(atT[0:DEC, SEQ:TOK], PS[5][0:DEC, DEC:2 * DEC], E[0:DEC, 0, SEQ:TOK], ALU.mult).then_inc(s["attn_ready"].sem, 1)
                    dve.wait_ge(*s["X1_copied"].done(h, 0))
                    for n in range(NL):
                        dve.wait_ge(*s["XX_psum"].done(h, n))
                        if n < NL - 1:
                            dve.tensor_tensor(X[:, 0:SEQ], X[:, 0:SEQ], PS[3][:, :], ALU.subtract)
                            dve.tensor_tensor(X[0:DEC, SEQ:TOK], X[0:DEC, SEQ:TOK], PS[5][0:DEC, 0:DEC], ALU.subtract)
                            dve.tensor_tensor(XT[0:DEC, SEQ:TOK], XT[0:DEC, SEQ:TOK], PS[5][0:DEC, DEC:2 * DEC], ALU.subtract)
                        dve.tensor_tensor(XT[:, 0:SEQ], XT[:, 0:SEQ], PS[4][:, :], ALU.subtract).then_inc(s["X_ready"].sem, 1)
                        dve.wait_ge(*s["X_ready"].done(h, n))
                    for t in range(T):
                        R, S = rows(t), St[t // PT]
                        if t == 0:
                            dve.wait_ge(*s["prompt_stored"].before(h, 0))
                        if t == PT:
                            dve.wait_ge(*s["state_loaded"].done(h, 15))
                        dve.wait_ge(*s["state_psum"].done(h, t))
                        if t == 0:
                            dve.tensor_copy(S[:], PS[4][:, 0:P]).then_inc(s["state_ready"].sem, 1)
                        else:
                            dve.wait_ge(*s["state_ready"].before(h, t))
                            dve.scalar_tensor_tensor(S[:], S[:], M["gcols"][:, 4, t, bass.ds(h, 1)], PS[4][:, 0:P], ALU.mult, ALU.add
                                                     ).then_inc(s["state_ready"].sem, 1)
                        dve.wait_ge(*s["o_copied"].done(h, t))
                        if t:
                            dve.wait_ge(*s["g_ready"].before(h, t))
                            dve.scalar_tensor_tensor(o[0:R, :], PS[7][0:R, 0:P], M["gcols"][0:R, 0, t, bass.ds(h, 1)], o_a[0:R, :],
                                                     ALU.mult, ALU.add).then_inc(s["o_ready"].sem, 1)
                        dve.wait_ge(*s["rstd_ready"].done(h, t))
                        dve.wait_ge(*s["gT_psum"].before(h, t))
                        dve.scalar_tensor_tensor(g[0:R, :], (o if t else o_a)[0:R, :], sm[0:R, 2:3], zs[0:R, t, :], ALU.mult, ALU.mult
                                                 ).then_inc(s["g_ready"].sem, 1)
                        for tt in ([t - 1] if t else []) + ([t] if t == T - 1 else []):
                            dve.wait_ge(*s["gT_psum"].done(h, tt))
                            dve.tensor_scalar(M["gT"][:, bass.ds(h + 8, 1), cols(tt)].rearrange("p a t -> p (a t)"), PS[5][:, 0:rows(tt)],
                                              M["vec"][:, bass.ds(h + 56, 1)], None, ALU.mult).then_inc(s["gT_copied"].sem, 1)
                for i in range(2):
                    dve.wait_ge(*cacheT_psum.done(0, i))
                    dve.tensor_copy(cr[:, i, :], PS[i][0:72, 0:P]).then_inc(cacheT_copied.sem, 1)


def cacheT_of(M, h, ct):
    return M["cacheT"][:].rearrange("p (r c) -> p r c", r=3)[:, :, bass.ds(h + 8 * ct, 1)].rearrange("p r a -> p (r a)")


def new_cache_of(newc, i, h, ct):
    return newc[:, i, :].rearrange("p (r c) -> p r c", r=3)[:, :, bass.ds(h + 8 * ct, 1)].rearrange("p r a -> p (r a)")


def output(nc, M, IN, OUT, l):
    with Phase(nc, f"output{l}") as ph:
        sb, sig = ph.sb, ph.counter
        K = 16
        wo = sb("w_out", [P, K, D])
        y, yn = sb("y", [P, 2, D]), sb("squares", [P, D])
        gp, gate = sb("g_post_rows", [2, D]), sb("gate_rows", [P, 2, D])
        sel = sb("cond_select", [2, 2, P])
        ss, ms, rs = sb("ss", [P, T]), sb("ms", [P, T]), sb("rs", [P, T])
        loaded, gpl = [sig(f"w_out_loaded{i}", 64) for i in range(4)], sig("g_post_loaded", 32)
        sel_ready, gate_psum, gate_ready = sig("gates_scaled", 2), sig("gate_psum", 4), sig("gate_copied", 4)
        (y_psum, y_copied, squared, mean_ready, rstd_ready, y_norm, y_gated, x_ready) = (sig(n, T) for n in (
            "y_psum", "y_copied", "squared", "mean_ready", "rstd_ready", "y_norm", "y_gated", "x_ready"))
        stored = sig("x_stored", 16 * T)
        PS = M["ps"]
        with nc.Block() as block:

            @block.sync
            def _(sp):
                w = IN[("w_out_even", "w_out_odd")[l]][0].rearrange("(k p) n -> p k n", p=P)
                for i in range(2):
                    sp.dma_start(gp[i:i + 1, :], IN["g_post"][l:l + 1, :]).then_inc(gpl.sem, 16)
                for k in range(K):
                    sp.dma_start(wo[:, k, :], w[:, k, :]).then_inc(loaded[k // 4].sem, 16)
                if l == 1:
                    for t in range(T):
                        sp.wait_ge(*x_ready.done(0, t))
                        out = OUT["y_p"][0, cols(t), :] if t < PT else OUT["y_s"][0]
                        sp.dma_start(out, M["x"][0:rows(t), t, :]).then_inc(stored.sem, 16)
                    sp.wait_ge(*stored.done(0, 16 * T - 1))

            @block.gpsimd
            def _(pool):
                for t in range(T):
                    R = rows(t)
                    pool.wait_ge(*squared.done(0, t))
                    pool.tensor_scalar(ms[0:R, t:t + 1], ss[0:R, t:t + 1], 1.0 / D, EPS, ALU.mult, ALU.add).then_inc(mean_ready.sem, 1)
                    pool.wait_ge(*mean_ready.done(0, t))
                    pool.tensor_tensor(rs[0:R, t:t + 1], ms[0:R, t:t + 1], M.c("half", R), ALU.pow).then_inc(rstd_ready.sem, 1)

            @block.tensor
            def _(pe):
                pe.wait_ge(*sel_ready.done(0, 1))
                for m in range(2):
                    for half in range(2):
                        pe.matmul(PS[4 + 2 * m + half][:, :], sel[:, m, :], M["gate"][:, l, half * 512:(half + 1) * 512],
                                  start=True, stop=True).then_inc(gate_psum.sem, 1)
                for t in range(T):
                    R = rows(t)
                    if t >= 2:
                        pe.wait_ge(*y_copied.done(0, t - 2))
                    for half in range(2):
                        for k in range(K):
                            if t == 0 and half == 0 and k % 4 == 0:
                                pe.wait_ge(*loaded[k // 4].done(0, 63))
                            last = pe.matmul(PS[2 * (t % 2) + half][0:R, :], M["gT"][:, k, cols(t)], wo[:, k, half * 512:(half + 1) * 512],
                                             start=(k == 0), stop=(k == K - 1))
                    last.then_inc(y_psum.sem, 1)

            @block.scalar
            def _(act):
                for n in range(4):
                    act.wait_ge(*gate_psum.done(0, n))
                    act.activation(gate[:, n // 2, (n % 2) * 512:(n % 2 + 1) * 512], PS[4 + n][:, :], ACT.Copy).then_inc(gate_ready.sem, 1)
                for t in range(T):
                    R = rows(t)
                    act.wait_ge(*y_psum.done(0, t))
                    if t >= 2:
                        act.wait_ge(*x_ready.done(0, t - 2))
                    act.activation(y[0:R, t % 2, 0:512], PS[2 * (t % 2)][0:R, :], ACT.Copy)
                    act.activation(y[0:R, t % 2, 512:D], PS[2 * (t % 2) + 1][0:R, :], ACT.Copy).then_inc(y_copied.sem, 1)
                    act.wait_ge(*y_copied.done(0, t))
                    act.activation(yn[0:R, :], y[0:R, t % 2, :], ACT.Square, accum_out=ss[0:R, t:t + 1]).then_inc(squared.sem, 1)

            @block.vector
            def _(dve):
                dve.wait_ge(*gpl.done(0, 31))
                dve.tensor_tensor(M["gate"][:, l, :], M["gate"][:, l, :], gp[:], ALU.mult).then_inc(sel_ready.sem, 1)
                for m in range(2):
                    last = dve.tensor_scalar(sel[:, m, :], M.c("ones", 2), M.c("ident", 2)[:, m:m + 1], None, ALU.mult)
                last.then_inc(sel_ready.sem, 1)
                dve.wait_ge(*gate_ready.done(0, 3))
                for t in range(T):
                    R = rows(t)
                    yt = y[0:R, t % 2, :]
                    dve.wait_ge(*rstd_ready.done(0, t))
                    dve.scalar_tensor_tensor(yt, yt, rs[0:R, t:t + 1], gate[0:R, COND[t], :], ALU.mult, ALU.mult).then_inc(y_gated.sem, 1)
                    dve.wait_ge(*y_gated.done(0, t))
                    dve.tensor_tensor(M["x"][0:R, t, :], M["x"][0:R, t, :], yt, ALU.add).then_inc(x_ready.sem, 1)


class Memory(dict):

    def c(self, name, n=P, m=None):
        a, b = self.at[name]
        return self["const"][0:n, a:(b if m is None else a + m)]


def build(nc, IN, OUT, at):
    with ExitStack() as ctx:
        def sb(name, shape):
            return ctx.enter_context(nc.sbuf_tensor(name, shape, F32))

        M = Memory()
        M.at = at
        M.passed = ctx.enter_context(nc.semaphore("passed"))
        M.const_loaded = ctx.enter_context(nc.semaphore("const_loaded"))
        M["const"] = sb("const", [P, max(b for _, b in at.values())])
        M["x"] = sb("x", [P, T, D])
        M["hT"] = sb("hT", [P, KT, TOK])
        M["gT"] = sb("gT", [P, 16, TOK])
        M["vec"], M["conv"] = sb("vectors", [P, 68]), sb("conv_taps", [P, 96])
        M["modT"], M["gate"] = sb("modT", [P, 2, 16, 2]), sb("gate", [2, 2, D])
        M["ps"] = [ctx.enter_context(nc.psum_tensor(f"bank{i}", [P, 512], F32)) for i in range(8)]
        setup(nc, M, IN, OUT)
        with ExitStack() as layer:
            for name, shape in (("negM", [P, EVEN_H, TOK]), ("ucol", [P, T, EVEN_H]), ("mcols", [P, 4, T, EVEN_H])):
                M[name] = layer.enter_context(nc.sbuf_tensor(name, shape, F32))
            even_gates(nc, M, IN, OUT)
            heads(nc, M, IN, OUT, "A")
            heads(nc, M, IN, OUT, "B")
        output(nc, M, IN, OUT, 0)
        with ExitStack() as layer:
            for name, shape in (("a1T", [RANK, TOK]), ("grow", [GDN_H, 2, TOK]), ("Gcol", [P, T, GDN_H]), ("gcols", [P, 5, T, GDN_H]),
                                ("cacheT", [P, 72])):
                M[name] = layer.enter_context(nc.sbuf_tensor(name, shape, F32))
            odd_gates(nc, M, IN, OUT)
            heads(nc, M, IN, OUT, "C")
            gdn_heads(nc, M, IN, OUT)
        output(nc, M, IN, OUT, 1)


_OUTS = [("y_p", (1, SEQ, D)), ("y_s", (1, DEC, D))] + [
    (side + n, (1, 1) + shape) for side in "ps" for n, shape in (
        ("C", (4, 256, 256)), ("n", (4, 256)), ("m", (4,)), ("ret", (4, 256, 256)), ("gla", (4, 128, 256)),
        ("gdn", (8, 128, 128)), ("conv", (3, 3072)))]
_INS = ["x_prompt", "x_sample", "c_prompt", "c_sample", "state_mlstm_C", "state_mlstm_n", "state_mlstm_m", "state_ret",
        "state_gla", "state_gdn", "cache_gdn_conv", "w_ada", "b_ada", "g_pre", "g_post", "w_in_even", "b_if_even",
        "g_head_even", "w_out_even", "w_in_odd", "w_a2", "b_a2", "conv_w", "a_log", "dt_bias", "g_head_odd", "w_out_odd"]


def kernel(**inputs):
    import concourse.bacc as bacc
    from concourse.bass_utils import run_bass_kernel_spmd

    nc = bacc.Bacc("TRN2", target_bir_lowering=False, num_devices=1)
    const, at = shape_constants()
    arrays, IN, OUT = {"in_const": const}, {}, {}
    for name in _INS:
        arrays["in_" + name] = np.ascontiguousarray(inputs[name])
    for name, a in arrays.items():
        IN[name[3:]] = nc.dram_tensor(name, a.shape, F32, kind="ExternalInput").ap()
    for name, shape in _OUTS:
        OUT[name] = nc.dram_tensor("out_" + name, shape, F32, kind="ExternalOutput").ap()
    build(nc, IN, OUT, at)
    r = run_bass_kernel_spmd(nc, [arrays], core_ids=[0])
    return tuple(r.results[0]["out_" + name] for name, _ in _OUTS)
```

```python
from contextlib import ExitStack

import numpy as np

import concourse.bass as bass
from concourse import mybir

F32 = mybir.dt.float32
U32 = mybir.dt.uint32
ACT = mybir.ActivationFunctionType
ALU = mybir.AluOpType
AX = mybir.AxisListType

P = 128
D = 1024
KT = D // P
SEQ, DEC = 512, 64
TOK = SEQ + DEC
HALF = TOK // 2
PT = SEQ // P
T = PT + 1
EPS = 1e-6
NEG = -1e30
EVEN_H, GLA_H, GDN_H = 4, 4, 8
RANK = 16
LEVELS = (1, 2, 4, 8, 16, 32, 64)
COND = [0] * PT + [1]


def rows(t):
    return P if t < PT else DEC


def cols(t):
    return slice(t * P, t * P + rows(t))


def shape_constants():
    s, t = np.arange(P)[:, None], np.arange(P)[None, :]
    lg = np.log(1.0 - 2.0 ** (-5.0 - np.arange(EVEN_H)))
    parts = {
        "ident": np.eye(P),
        "ones": np.ones((P, P)),
        "mask": (s <= t) * 1.0,
        "neg_causal": np.where(s <= t, 0.0, NEG),
        "neg_strict": np.where(s < t, 0.0, NEG),
        "half": np.full((P, 1), -0.5),
        "levels": np.concatenate([((s // (2 * n) == t // (2 * n)) & (s % (2 * n) < n) & (t % (2 * n) >= n)) * 1.0
                                  for n in LEVELS], axis=1),
        "decay": np.concatenate([np.where(s <= t, np.exp(np.maximum(t - s, 0) * g), 0.0) for g in lg], axis=1),
        "q_decay": np.exp((s + 1.0) * lg[None, :]),
        "k_decay": np.concatenate([np.exp((P - 1.0 - s) * lg), np.exp(np.maximum(DEC - 1.0 - s, 0) * lg)], axis=1),
        "s_decay": np.broadcast_to(np.concatenate([np.exp(P * lg), np.exp(DEC * lg)])[None, :], (P, 2 * EVEN_H)),
    }
    for n, name in ((EVEN_H, "diag4"), (GDN_H, "diag8")):
        parts[name] = np.broadcast_to(np.eye(P, n)[:, None, :], (P, T, n)).reshape(P, T * n)
    inv = 10000.0 ** (-np.arange(P, dtype=np.float64) / P)
    pos = np.concatenate([np.arange(SEQ), 512 + np.arange(DEC)])
    parts["cos"], parts["sin"] = np.cos(inv[:, None] * pos), np.sin(inv[:, None] * pos)
    where, at = {}, 0
    for name, a in parts.items():
        where[name] = (at, at + a.shape[1])
        at += a.shape[1]
    return np.concatenate(list(parts.values()), axis=1).astype(np.float32), where


class Signal:

    def __init__(self, sem, per, first):
        self.sem, self.per, self.first = sem, per, first

    def done(self, turn, k):
        return self.sem, turn * self.per + (self.first + k + 1)

    def before(self, turn, k):
        return self.sem, turn * self.per + (self.first + k)


class Link:

    def __init__(self, eng, step, turn=0):
        self.eng, self.step, self.turn, self.k = eng, step, turn, 0

    def __call__(self, ins, n=1):
        ins.then_inc(self.step.sem, 1)
        self.eng.wait_ge(*self.step.done(self.turn, self.k))
        self.k += 1

    def close(self):
        assert self.k == self.step.per, (self.k, self.step.per)


class Phase:

    def __init__(self, nc, name, first=0):
        self.nc, self.name, self.first, self.ctx, self.counters = nc, name, first, ExitStack(), []

    def __enter__(self):
        return self

    def __exit__(self, *exc):
        if exc[0] is None:
            self.nc.clear_and_free_semaphores([s.sem for s in self.counters])
            self.nc.all_engine_barrier()
        self.ctx.close()
        return False

    def sb(self, name, shape, dt=F32):
        return self.ctx.enter_context(self.nc.sbuf_tensor(f"{self.name}_{name}", shape, dt))

    def counter(self, name, per=1):
        s = Signal(self.nc.alloc_semaphore(f"{self.name}_{name}"), per, self.first)
        if self.first:
            engines = (self.nc.sync, self.nc.gpsimd, self.nc.scalar, self.nc.vector, self.nc.tensor)
            engines[len(self.counters) % 5].sem_inc(s.sem, self.first)
        self.counters.append(s)
        return s


def matmul_chain(pe, out, pairs):
    for n, (a, b) in enumerate(pairs):
        last = pe.matmul(out, a, b, start=(n == 0), stop=(n == len(pairs) - 1))
    return last


def setup(nc, M, IN, OUT):
    with Phase(nc, "setup") as ph:
        vec = ph.sb("vec_rows", [P, P])
        conv_rows = ph.sb("conv_rows", [P, P])
        tc = ph.sb("tanh_c", [P, 16])
        cs = ph.sb("silu_c", [P, KT, 2])
        wada = ph.sb("w_ada", [P, 2, 3 * D])
        bada = ph.sb("b_ada", [2, 2, 3 * D])
        mod = ph.sb("mod_rows", [2, 2, 2 * D])
        loaded = ph.counter("small_loaded", 16 * 11)
        ada_loaded = [ph.counter(f"ada_loaded{i}", 16 * KT) for i in range(2)]
        bada_loaded = ph.counter("b_ada_loaded", 64)
        x_loaded = ph.counter("x_loaded", 32)
        vec_psum = ph.counter("vec_psum")
        vec_copied = ph.counter("vec_copied", 2)
        tanh_done = ph.counter("tanh_done")
        cs_half = ph.counter("silu_c_half")
        cs_ready = ph.counter("silu_c_ready")
        ada_used = ph.counter("ada_used", 2 * KT)
        mod_ready = ph.counter("mod_ready", 2 * 6)
        modT_psum = ph.counter("modT_psum", 2)
        modT_copied = ph.counter("modT_copied", 2)
        scaled = ph.counter("scaled", 4)
        gh_scaled = ph.counter("g_head_scaled", 4)
        PS = M["ps"]
        with nc.Block() as block:

            @block.sync
            def _(sp):
                sp.dma_start(M["const"][:], IN["const"]).then_inc(M.const_loaded, 16)
                rowsof = [(IN["c_prompt"][0], 0, 8), (IN["c_sample"][0], 8, 8),
                          (IN["g_pre"][0], 16, 8), (IN["g_pre"][1], 24, 8),
                          (IN["g_head_even"][0], 32, 16), (IN["g_head_odd"][0], 48, 16), (IN["b_a2"][0], 64, 4)]
                for src, at, n in rowsof:
                    sp.dma_start(vec[at:at + n, :], src.rearrange("(r c) -> r c", c=P)).then_inc(loaded.sem, 16)
                for j in range(4):
                    sp.dma_start(conv_rows[24 * j:24 * j + 24, :],
                                 IN["conv_w"][0, j].rearrange("(r c) -> r c", c=P)).then_inc(loaded.sem, 16)
                for l in range(2):
                    for k in range(KT):
                        i = l * KT + k
                        if i >= 2:
                            sp.wait_ge(*ada_used.done(0, i - 2))
                        sp.dma_start(wada[:, i % 2, :], IN["w_ada"][l, k * P:(k + 1) * P, :]).then_inc(
                            ada_loaded[i % 2].sem, 16)
                        if i == 0:
                            for m in range(2):
                                sp.dma_start(bada[m:m + 1, :, :], IN["b_ada"].rearrange("(a l) n -> a l n", a=1)
                                             ).then_inc(bada_loaded.sem, 32)
                sp.dma_start(M["x"][:, 0:PT, :], IN["x_prompt"][0].rearrange("(t p) d -> p t d", p=P)).then_inc(x_loaded.sem, 16)
                sp.dma_start(M["x"][0:DEC, PT, :], IN["x_sample"][0]).then_inc(x_loaded.sem, 16)
                sp.wait_ge(*x_loaded.done(0, 31))

            @block.tensor
            def _(pe):
                pe.wait_ge(*loaded.done(0, 16 * 11 - 1))
                pe.wait_ge(M.const_loaded, 16)
                pe.transpose(PS[7][:, 0:68], vec[0:68, :], M.c("ident", 68, 68))
                pe.transpose(PS[7][:, 128:224], conv_rows[0:96, :], M.c("ident", 96, 96)).then_inc(vec_psum.sem, 1)
                pe.wait_ge(*cs_ready.done(0, 0))
                for l in range(2):
                    for k in range(KT):
                        i = l * KT + k
                        pe.wait_ge(*ada_loaded[i % 2].done(0, 16 * (i // 2) + 15))
                        if l and k == 0:
                            pe.wait_ge(*mod_ready.done(0, 5))
                        for n in range(6):
                            last = pe.matmul(PS[n][0:2, :], cs[:, k, :], wada[:, i % 2, n * 512:(n + 1) * 512],
                                             start=(k == 0), stop=(k == KT - 1))
                        last.then_inc(ada_used.sem, 1)
                    pe.wait_ge(*mod_ready.done(0, 6 * l + 5))
                    if l:
                        pe.wait_ge(*modT_copied.done(0, 0))
                    for c in range(16):
                        last = pe.transpose(PS[6][:, 2 * c:2 * c + 2], mod[0:2, l, c * P:(c + 1) * P], M.c("ident", 2, 2))
                    last.then_inc(modT_psum.sem, 1)

            @block.scalar
            def _(act):
                act.wait_ge(*vec_copied.done(0, 1))
                act.activation(tc[:], M["vec"][:, 0:16], ACT.Tanh, scale=0.5).then_inc(tanh_done.sem, 1)

            @block.vector
            def _(dve):
                dve.wait_ge(*vec_psum.done(0, 0))
                dve.tensor_copy(M["vec"][:], PS[7][:, 0:68]).then_inc(vec_copied.sem, 1)
                dve.tensor_copy(M["conv"][:], PS[7][:, 128:224]).then_inc(vec_copied.sem, 1)
                dve.wait_ge(*tanh_done.done(0, 0))
                dve.scalar_tensor_tensor(tc[:], tc[:], 1.0, M["vec"][:, 0:16], ALU.add, ALU.mult).then_inc(cs_half.sem, 1)
                dve.wait_ge(*cs_half.done(0, 0))
                dve.tensor_scalar(cs[:].rearrange("p k m -> p m k"), tc[:].rearrange("p (m k) -> p m k", m=2), 0.5, None,
                                  ALU.mult).then_inc(cs_ready.sem, 1)
                for a, b, f in ((32, 40, 0.25), (40, 48, 0.5), (48, 64, 0.5)):
                    dve.tensor_scalar(M["vec"][:, a:b], M["vec"][:, a:b], f, None, ALU.mult).then_inc(gh_scaled.sem, 1)
                dve.memset(M["x"][DEC:P, PT, :], 0.0).then_inc(gh_scaled.sem, 1)
                dve.wait_ge(*bada_loaded.done(0, 63))
                for l in range(2):
                    dve.wait_ge(*ada_used.done(0, l * KT + KT - 1))
                    for n in range(6):
                        out = mod[:, l, n * 512:(n + 1) * 512] if n < 4 else M["gate"][:, l, (n - 4) * 512:(n - 3) * 512]
                        dve.tensor_tensor(out, PS[n][0:2, :], bada[:, l, n * 512:(n + 1) * 512], ALU.add).then_inc(
                            mod_ready.sem, 1)
                    dve.wait_ge(*modT_psum.done(0, l))
                    dve.tensor_copy(M["modT"][:, l, :, :], PS[6][:, 0:32].rearrange("p (c m) -> p c m", m=2)).then_inc(
                        modT_copied.sem, 1)
                    dve.wait_ge(*modT_copied.done(0, l))
                    for m in range(2):
                        dve.scalar_tensor_tensor(M["modT"][:, l, KT:2 * KT, m], M["modT"][:, l, KT:2 * KT, m], 1.0,
                                                 M["vec"][:, 16 + 8 * l:24 + 8 * l], ALU.add, ALU.mult).then_inc(scaled.sem, 1)


def norm_steps(ph, M, l):
    S = {n: ph.counter(n, k) for n, k in (("sq", T), ("mean", T), ("rstd", T), ("xn", T), ("xT_psum", 2 * T),
                                         ("hT_act", T), ("hT_dve", T))}
    PS = M["ps"]
    sqj = ph.sb("squares", [P, D])
    ss, ms, rs = ph.sb("ss", [P, T]), ph.sb("ms", [P, T]), ph.sb("rs", [P, T])
    xn = ph.sb("xn", [P, 2, D])

    def act_steps(act):
        for t in range(T):
            if t:
                act.wait_ge(*S["sq"].done(0, t - 1))
            act.activation(sqj[0:rows(t), :], M["x"][0:rows(t), t, :], ACT.Square, accum_out=ss[0:rows(t), t:t + 1]
                           ).then_inc(S["sq"].sem, 1)
        for t in range(T):
            act.wait_ge(*S["xT_psum"].done(0, 2 * t))
            for k in range(4):
                last = act.activation(M["hT"][:, k, cols(t)], PS[2 * (t % 2)][:, k * P:k * P + rows(t)], ACT.Identity,
                                      bias=M["modT"][:, l, k, COND[t]:COND[t] + 1],
                                      scale=M["modT"][:, l, KT + k, COND[t]:COND[t] + 1])
            last.then_inc(S["hT_act"].sem, 1)

    def pool_steps(pool):
        for t in range(T):
            R = rows(t)
            pool.wait_ge(*S["sq"].done(0, t))
            pool.tensor_scalar(ms[0:R, t:t + 1], ss[0:R, t:t + 1], 1.0 / D, EPS, ALU.mult, ALU.add).then_inc(S["mean"].sem, 1)
            pool.wait_ge(*S["mean"].done(0, t))
            pool.tensor_tensor(rs[0:R, t:t + 1], ms[0:R, t:t + 1], M.c("half", R), ALU.pow).then_inc(S["rstd"].sem, 1)

    def dve_steps(dve):
        def scale(t):
            R = rows(t)
            dve.wait_ge(*S["rstd"].done(0, t))
            if t >= 2:
                dve.wait_ge(*S["xT_psum"].done(0, 2 * (t - 2) + 1))
            dve.tensor_scalar(xn[0:R, t % 2, :], M["x"][0:R, t, :], rs[0:R, t:t + 1], None, ALU.mult).then_inc(S["xn"].sem, 1)
        scale(0)
        for t in range(T):
            if t + 1 < T:
                scale(t + 1)
            dve.wait_ge(*S["xT_psum"].done(0, 2 * t + 1))
            for k in range(4, KT):
                last = dve.tensor_scalar(M["hT"][:, k, cols(t)], PS[2 * (t % 2) + 1][:, (k - 4) * P:(k - 4) * P + rows(t)],
                                         M["modT"][:, l, KT + k, COND[t]:COND[t] + 1],
                                         M["modT"][:, l, k, COND[t]:COND[t] + 1], ALU.mult, ALU.add)
            last.then_inc(S["hT_dve"].sem, 1)

    def pe_steps(pe):
        for t in range(T):
            R = rows(t)
            pe.wait_ge(*S["xn"].done(0, t))
            for half in range(2):
                if t >= 2:
                    pe.wait_ge(*S[("hT_act", "hT_dve")[half]].done(0, t - 2))
                for k in range(4):
                    kk = 4 * half + k
                    last = pe.transpose(PS[2 * (t % 2) + half][:, k * P:k * P + R], xn[0:R, t % 2, kk * P:(kk + 1) * P],
                                        M.c("ident", R, R))
                last.then_inc(S["xT_psum"].sem, 1)
        pe.wait_ge(*S["hT_act"].done(0, T - 1))
        pe.wait_ge(*S["hT_dve"].done(0, T - 1))

    return act_steps, pool_steps, dve_steps, pe_steps


def small_projection(pe, M, w, c0, n, banks):
    for half in range(2):
        last = matmul_chain(pe, M["ps"][banks[half]][0:n, 0:HALF],
                            [(w[:, k, c0:c0 + n], M["hT"][:, k, half * HALF:(half + 1) * HALF]) for k in range(KT)])
    return last


def log_sigmoid(act, dve, x, a, b, out, S, turn=0):
    if dve is not None:
        dve.scalar_tensor_tensor(a, x, -1.0, x, ALU.mult, ALU.max).then_inc(S["abs"].sem, 1)
        dve.wait_ge(*S["exp"].done(turn, 0))
        dve.tensor_scalar(b, b, 1.0, None, ALU.add).then_inc(S["plus"].sem, 1)
        dve.wait_ge(*S["log"].done(turn, 0))
        return dve.scalar_tensor_tensor(out, x, 0.0, a, ALU.min, ALU.subtract)
    act.wait_ge(*S["abs"].done(turn, 0))
    act.activation(b, a, ACT.Exp, scale=-1.0).then_inc(S["exp"].sem, 1)
    act.wait_ge(*S["plus"].done(turn, 0))
    act.activation(a, b, ACT.Ln).then_inc(S["log"].sem, 1)


def even_gates(nc, M, IN, OUT):
    with Phase(nc, "even_gates") as ph:
        act_norm, pool_norm, dve_norm, pe_norm = norm_steps(ph, M, 0)
        H = EVEN_H
        sb, sig = ph.sb, ph.counter
        wg = sb("w_gates", [P, KT, 64])
        bif = sb("b_if", [H, 2])
        mprev = sb("m_prev", [H, T + 2])
        gi, gf, ta, tb, lf = (sb(n, [H, TOK]) for n in ("gate_i", "gate_f", "ls_a", "ls_b", "log_f"))
        b, u, Mx, m = (sb(n, [H, TOK]) for n in ("cum_f", "u_rows", "M_rows", "m_rows"))
        mp_rows, me_rows = sb("mp_rows", [H, T, H]), sb("me_rows", [H, T, H])
        msel = sb("M_selected", [H, H, TOK])
        col = sb("gate_cols", [P, 3, T, H])
        bro = sb("gate_broadcast", [P, 2, T, H])
        arg = sb("gate_args", [P, 4, T, H])
        wl = sig("w_gates_loaded", 16 * 6)
        proj, copied = sig("gates_psum", 2), sig("gates_copied", 4)
        S = {n: sig("ls_" + n) for n in ("abs", "exp", "plus", "log")}
        lk = sig("vector_step")
        rows_ready, colsp, bp, bcopied = sig("rows_ready"), sig("cols_psum"), sig("M_psum", 2 * H), sig("M_copied", 2 * H)
        args_ready, exps = sig("args_ready"), sig("gate_exps")
        cleared = sig("cols_cleared")
        m_stored = sig("m_stored", 32)
        PS = M["ps"]
        with nc.Block() as block:

            @block.sync
            def _(sp):
                sp.wait_ge(*cleared.done(0, 0))
                for i in range(2):
                    sp.dma_start(wg[:, :, 32 * i:32 * i + H], IN["w_in_even"][0, :, 9 * D + i * H:9 * D + (i + 1) * H].rearrange(
                        "(k p) n -> p k n", p=P)).then_inc(wl.sem, 16)
                for i in range(2):
                    sp.dma_start(bif[:, i:i + 1], IN["b_if_even"][0, i * H:(i + 1) * H].rearrange("(h a) -> h a", a=1)).then_inc(wl.sem, 16)
                sp.dma_start(mprev[:, PT:PT + 1], IN["state_mlstm_m"][0, 0].rearrange("(h a) -> h a", a=1)).then_inc(wl.sem, 32)
                sp.wait_ge(*rows_ready.done(0, 0))
                sp.dma_start(OUT["pm"][0, 0].rearrange("(h a) -> h a", a=1), mprev[:, T:T + 1]).then_inc(m_stored.sem, 16)
                sp.dma_start(OUT["sm"][0, 0].rearrange("(h a) -> h a", a=1), mprev[:, T + 1:T + 2]).then_inc(m_stored.sem, 16)
                sp.wait_ge(*m_stored.done(0, 31))

            @block.gpsimd
            def _(pool):
                pool_norm(pool)

            @block.tensor
            def _(pe):
                pe_norm(pe)
                pe.wait_ge(*wl.done(0, 95))
                small_projection(pe, M, wg, 0, 32 + H, (4, 5)).then_inc(proj.sem, 1)
                pe.wait_ge(*rows_ready.done(0, 0))
                for n, r in enumerate((u, Mx, m)):
                    for t in range(T):
                        at = (n * T + t) * H
                        pe.transpose(PS[0][0:rows(t), at:at + H], r[:, cols(t)], M.c("ident", H, H))
                for n, r in enumerate((mp_rows, me_rows)):
                    last = pe.matmul(PS[1][:, n * T * H:(n + 1) * T * H], M.c("ones", H), r[:].rearrange("p t h -> p (t h)"),
                                     start=True, stop=True)
                last.then_inc(colsp.sem, 1)
                for h in range(H):
                    for half in range(2):
                        n = 2 * h + half
                        if n >= 2:
                            pe.wait_ge(*bcopied.done(0, n - 2))
                        pe.matmul(PS[2 + half][:, 0:HALF], M.c("ones", H), msel[:, h, half * HALF:(half + 1) * HALF],
                                  start=True, stop=True).then_inc(bp.sem, 1)

            @block.scalar
            def _(act):
                act_norm(act)
                for i, g in enumerate((gi, gf)):
                    act.wait_ge(*proj.done(0, 0))
                    for half in range(2):
                        act.activation(g[:, half * HALF:(half + 1) * HALF], PS[4 + half][32 * i:32 * i + H, 0:HALF], ACT.Identity,
                                       bias=bif[:, i:i + 1]).then_inc(copied.sem, 1)
                log_sigmoid(act, None, gf[:], ta[:], tb[:], lf[:], S)
                act.wait_ge(*args_ready.done(0, 0))
                act.activation(M["mcols"][:], arg[:], ACT.Exp).then_inc(exps.sem, 1)
                for n in range(2 * H):
                    act.wait_ge(*bp.done(0, n))
                    act.activation(M["negM"][:, n // 2, (n % 2) * HALF:(n % 2 + 1) * HALF], PS[2 + n % 2][:, 0:HALF],
                                   ACT.Copy).then_inc(bcopied.sem, 1)

            @block.vector
            def _(dve):
                link = Link(dve, lk)
                dve.memset(wg[:], 0.0).then_inc(cleared.sem, 1)
                dve.memset(mprev[:, 0:1], 0.0)
                dve.memset(col[:], 0.0)
                dve_norm(dve)
                dve.wait_ge(*copied.done(0, 3))
                link(log_sigmoid(None, dve, gf[:], ta[:], tb[:], lf[:], S))
                for t in range(T):
                    last = dve.tensor_tensor_scan(b[:, cols(t)], M.c("ones", H, rows(t)), lf[:, cols(t)], 0.0, ALU.mult, ALU.add)
                link(last)
                link(dve.tensor_tensor(u[:], gi[:], b[:], ALU.subtract))
                dve.wait_ge(*wl.done(0, 95))
                for t in range(T):
                    end = t * P + rows(t) - 1
                    link(dve.tensor_tensor_scan(Mx[:, cols(t)], u[:, cols(t)], u[:, cols(t)], mprev[:, t:t + 1], ALU.max, ALU.max))
                    to = t + 1 if t < PT - 1 else (T if t == PT - 1 else T + 1)
                    link(dve.tensor_tensor(mprev[:, to:to + 1], b[:, end:end + 1], Mx[:, end:end + 1], ALU.add))
                dve.tensor_tensor(m[:], b[:], Mx[:], ALU.add)
                for h in range(H):
                    dve.tensor_scalar(msel[:, h, :], Mx[:], M.c("diag4", H)[:, h:h + 1], -1.0, ALU.mult, ALU.mult)
                for t in range(T):
                    end = t * P + rows(t) - 1
                    dve.tensor_scalar(mp_rows[:, t, :], M.c("diag4", H)[:, 0:H], mprev[:, t:t + 1], None, ALU.mult)
                    last = dve.tensor_scalar(me_rows[:, t, :], M.c("diag4", H)[:, 0:H], Mx[:, end:end + 1], None, ALU.mult)
                last.then_inc(rows_ready.sem, 1)
                dve.wait_ge(*colsp.done(0, 0))
                src = PS[0][:, 0:3 * T * H].rearrange("p (n t h) -> p n t h", n=3, t=T)
                dve.tensor_copy(col[:, :, 0:PT, :], src[:, :, 0:PT, :])
                dve.tensor_copy(col[0:DEC, :, PT, :], src[0:DEC, :, PT, :])
                link(dve.tensor_copy(bro[:].rearrange("p n t h -> p (n t h)"), PS[1][:, 0:2 * T * H]))
                dve.tensor_copy(M["ucol"][:], col[:, 0])
                dve.tensor_tensor(arg[:, 0], bro[:, 0], col[:, 1], ALU.subtract)
                dve.tensor_tensor(arg[:, 1], col[:, 0], bro[:, 1], ALU.subtract)
                dve.tensor_tensor(arg[:, 2], bro[:, 0], bro[:, 1], ALU.subtract)
                dve.tensor_scalar(arg[:, 3], col[:, 2], -1.0, None, ALU.mult).then_inc(args_ready.sem, 1)


def heads(nc, M, IN, OUT, kind):
    H, DV = 4, 256
    DT = {"A": 2, "B": 2, "C": 1}[kind]
    NV = DV + 1 if kind == "A" else DV
    NG = 2 * DV if kind == "A" else DV
    CT = 2 * DT
    NA = 2 if kind == "C" else 0
    NP = NA + 2 * CT
    w_in = IN["w_in_odd" if kind == "C" else "w_in_even"][0].rearrange("(k p) n -> p k n", p=P)
    q0, k0, v0 = {"A": (0, D, 2 * D), "B": (4 * D, 5 * D, 6 * D), "C": (0, 512, D)}[kind]
    gates0 = {"A": [3 * D, 7 * D], "B": [8 * D], "C": [5 * D + 32]}[kind]
    S_in = IN[{"A": "state_mlstm_C", "B": "state_ret", "C": "state_gla"}[kind]][0, 0]
    pS = OUT[{"A": "pC", "B": "pret", "C": "pgla"}[kind]][0, 0]
    sS = OUT[{"A": "sC", "B": "sret", "C": "sgla"}[kind]][0, 0]
    g_col = {"A": 32, "B": 40, "C": 48}[kind]
    g_row = {"A": 0, "B": 8, "C": 0}[kind]
    ms_scale = 1.0 / (4 * DV) if kind == "A" else 1.0 / DV
    QS = (P if kind == "C" else DV) ** -0.5
    PS = M["ps"]
    with Phase(nc, {"A": "mlstm", "B": "retention", "C": "gla"}[kind], first=1) as ph:
        sb, sig = ph.sb, ph.counter
        wqk = sb("w_qk", [P, KT, CT * P])
        wv = sb("w_gates_v", [P, KT, NG + DV])
        qk = sb("qkT", [P, CT, TOK])
        v = sb("v", [P, NV])
        th = sb("tanh", [P, NG])
        zs = sb("z_silu", [P, DV])
        sT = sb("scores", [P, P])
        kw = sb("k_weighted", [P, DT * P])
        num_a, num, hg, g = sb("intra", [P, NV]), sb("num", [P, NV]), sb("h_gated", [P, DV]), sb("g", [P, DV])
        sq = sb("squares", [P, DV])
        sm = sb("small", [P, 8])
        St = [sb("state_prompt", [P, DT, NV]), sb("state_sample", [P, DT, NV])]
        if kind == "A":
            E, arg = sb("E", [P, P]), sb("E_arg", [P, P])
            logit_ready, decay_ready = sig("logit_ready", T), sig("decay_ready", T)
        if kind in "BC":
            raw = sb("qkT_raw", [P, CT, TOK])
        if kind == "B":
            ra, rb = sb("rope_a", [P, TOK]), sb("rope_b", [P, TOK])
        if kind == "C":
            wa = sb("w_a2", [RANK, P])
            la, lb, lc, bT = (sb(n, [P, TOK]) for n in ("ls_x", "ls_a", "ls_b", "cum_a"))
            ends = sb("block_ends", [P, 3, T])
            eend = sb("block_exps", [P, 3, T])
            Sc = sb("state_scaled", [P, DV])
            nS = sb("state_new", [P, DV])
            wal = sig("w_a2_loaded", 16)
            Lg = {n: sig("ls_" + n) for n in ("abs", "exp", "plus", "log")}
            shifted, exps, b_ready = sig("b_shifted"), sig("b_exps", 3), sig("b_ready")
            sc_ready, nS_ready = sig("state_scaled_ready", PT), sig("state_new_ready", T)
        wql, wvl = sig("w_qk_loaded", 16), sig("w_v_loaded", 16 * (3 if kind == "A" else 2))
        wql2 = sig("w_qk_loaded2", 16)
        sl = sig("state_loaded", 32 if kind == "A" else 16)
        p_st, s_st = sig("prompt_state_stored", 32 if kind == "A" else 16), sig("sample_state_stored", 32 if kind == "A" else 16)
        qk_psum, qk_copied, qk_ready = sig("qk_psum", NP), sig("qk_copied", NP), sig("qk_ready")
        filled = sig("filled")
        (gates_psum, tanh_done, gates_used, v_psum, v_copied, scores_psum, scores_ready, kw_ready,
         nums_psum, intra_copied, state_psum, state_ready, squared, mean_ready, rstd_ready, g_ready, gT_psum,
         gT_copied) = (sig(n, T) for n in (
             "gates_psum", "tanh_done", "gates_used", "v_psum", "v_copied", "scores_psum",
             "scores_ready", "kw_ready", "nums_psum", "intra_copied", "state_psum", "state_ready", "squared",
             "mean_ready", "rstd_ready", "g_ready", "gT_psum", "gT_copied"))
        num_ready = sig("num_ready", PT)
        if kind == "A":
            den, hg_ready = sig("den_step", 4 * T), sig("h_gated_ready", T)
        NL = {"A": 0, "B": 11, "C": 5}[kind]
        lk = sig("vector_step", NL)

        def q_side(t):
            return slice(0, DT), cols(t)

        nc.all_engine_barrier()
        with nc.Block() as block:

            @block.sync
            def _(sp):
                with sp.Fori(0, H) as h:
                    sp.wait_ge(*qk_psum.before(h, 0))
                    sp.dma_start(wqk[:, :, 0:DT * P], w_in[:, :, bass.ds(h * (DT * P) + q0, DT * P)]).then_inc(wql.sem, 16)
                    sp.dma_start(wqk[:, :, DT * P:CT * P], w_in[:, :, bass.ds(h * (DT * P) + k0, DT * P)]).then_inc(wql2.sem, 16)
                    if kind == "C":
                        sp.dma_start(wa[:], IN["w_a2"][0][:, bass.ds(h * P, P)]).then_inc(wal.sem, 16)
                    sp.wait_ge(*v_psum.before(h, 0))
                    for n, c0 in enumerate(gates0 + [v0]):
                        sp.dma_start(wv[:, :, n * DV:(n + 1) * DV], w_in[:, :, bass.ds(h * DV + c0, DV)]).then_inc(wvl.sem, 16)
                sp.wait_ge(*p_st.before(H, 0))
                sp.wait_ge(*s_st.before(H, 0))

            @block.gpsimd
            def _(pool):
                with pool.Fori(0, H) as h:
                    for t in range(T):
                        R = rows(t)
                        pool.wait_ge(*squared.done(h, t))
                        pool.sem_inc(M.passed, 1)
                        pool.tensor_scalar(sm[0:R, 4:5], sm[0:R, 3:4], ms_scale, EPS, ALU.mult, ALU.add).then_inc(mean_ready.sem, 1)
                        pool.wait_ge(*mean_ready.done(h, t))
                        pool.tensor_tensor(sm[0:R, 5:6], sm[0:R, 4:5], M.c("half", R), ALU.pow).then_inc(rstd_ready.sem, 1)

            @block.tensor
            def _(pe):
                with pe.Fori(0, H) as h:
                    pe.wait_ge(*state_ready.before(h, 0))
                    if kind == "C":
                        pe.wait_ge(*wal.done(h, 15))
                        for n in range(2):
                            pe.wait_ge(*qk_copied.before(h, 0))
                            pe.matmul(PS[n][:, 0:HALF], wa[:], M["a1T"][:, n * HALF:(n + 1) * HALF],
                                      start=True, stop=True).then_inc(qk_psum.sem, 1)
                    for ct in range(CT):
                        if ct == 0:
                            pe.wait_ge(*wql.done(h, 15))
                        if ct == DT:
                            pe.wait_ge(*wql2.done(h, 15))
                        for half in range(2):
                            n = NA + 2 * ct + half
                            pe.wait_ge(*(qk_copied.done(h, n - 2) if n >= 2 else qk_copied.before(h, 0)))
                            matmul_chain(pe, PS[half][:, 0:HALF],
                                         [(wqk[:, k, ct * P:(ct + 1) * P], M["hT"][:, k, half * HALF:(half + 1) * HALF])
                                          for k in range(KT)]).then_inc(qk_psum.sem, 1)

                    def project(t, c0, n, out):
                        return matmul_chain(pe, out, [(M["hT"][:, k, cols(t)], wv[:, k, c0:c0 + n]) for k in range(KT)])

                    def turn_g(t):
                        pe.wait_ge(*g_ready.done(h, t))
                        pe.wait_ge(*gT_copied.before(h, t))
                        pe.sem_inc(M.passed, 1)
                        R = rows(t)
                        for d in range(2):
                            last = pe.transpose(PS[7][:, d * P:d * P + R], g[0:R, d * P:(d + 1) * P], M.c("ident", R, R))
                        last.then_inc(gT_psum.sem, 1)

                    for t in range(T):
                        R, cs = rows(t), cols(t)
                        if t == 0:
                            pe.wait_ge(*wvl.done(h, wvl.per - 1))
                        pe.wait_ge(*gates_used.before(h, t))
                        project(t, 0, NG, PS[2][0:R, 0:NG]).then_inc(gates_psum.sem, 1)
                        if t == 0:
                            pe.wait_ge(*(qk_copied.done(h, NP - 1) if kind == "A" else qk_ready.done(h, 0)))
                        pe.wait_ge(*kw_ready.before(h, t))
                        matmul_chain(pe, PS[4][0:R, 0:R], [(qk[:, DT + d, cs], qk[:, d, cs]) for d in range(DT)])
                        for d in range(DT):
                            last = pe.transpose(PS[4][0:R, (d + 1) * P:(d + 2) * P], qk[:, DT + d, cs], M.c("ident", P, P))
                        last.then_inc(scores_psum.sem, 1)
                        pe.wait_ge(*v_copied.before(h, t))
                        project(t, NG, DV, PS[3][0:R, 0:DV]).then_inc(v_psum.sem, 1)
                        if t and kind != "C":
                            pe.wait_ge(*num_ready.before(h, t - 1))
                            pe.wait_ge(*(sl.done(h, sl.per - 1) if t == PT else state_ready.before(h, t)))
                            matmul_chain(pe, PS[5][0:R, 0:NV], [(qk[:, d, cs], St[t // PT][:, d, :]) for d in range(DT)])
                        pe.wait_ge(*scores_ready.done(h, t))
                        pe.wait_ge(*v_copied.done(h, t))
                        pe.wait_ge(*intra_copied.before(h, t))
                        pairs = [(sT[0:R, 0:R], v[0:R, :])]
                        if t and kind == "C":
                            pe.wait_ge(*sc_ready.done(h, t - 1))
                            pairs.append((qk[:, 0, cs], Sc[:]))
                        pe.sem_inc(M.passed, 1)
                        matmul_chain(pe, PS[6][0:R, 0:NV], pairs).then_inc(nums_psum.sem, 1)
                        pe.wait_ge(*kw_ready.done(h, t))
                        pe.wait_ge(*(nS_ready if kind == "C" else state_ready).before(h, t))
                        pe.sem_inc(M.passed, 1)
                        for d in range(DT):
                            last = pe.matmul(PS[d][:, 0:NV], kw[0:R, d * P:(d + 1) * P], v[0:R, :], start=True, stop=True)
                        last.then_inc(state_psum.sem, 1)
                        if t:
                            turn_g(t - 1)
                    turn_g(T - 1)

            @block.scalar
            def _(act):
                with act.Fori(0, H) as h:
                    act.wait_ge(*s_st.before(h, 0))
                    src = S_in[bass.ds(h, 1)].rearrange("a (d p) v -> p (a d) v", p=P)
                    act.dma_start(St[1][:, :, 0:DV], src).then_inc(sl.sem, 16)
                    if kind == "A":
                        n_in = IN["state_mlstm_n"][0, 0][bass.ds(h, 1)].rearrange("a (d p b) -> p (a d) b", p=P, b=1)
                        act.dma_start(St[1][:, :, DV:NV], n_in, allow_slow_non_contiguous=True).then_inc(sl.sem, 16)
                    for n in range(NP):
                        ct, half = (n - NA) // 2, n % 2
                        act.wait_ge(*qk_psum.done(h, n))
                        to = slice(half * HALF, (half + 1) * HALF)
                        if n < NA:
                            act.sem_inc(M.passed, 1)
                            act.activation(la[:, to], PS[half][:, 0:HALF], ACT.Identity, bias=M["vec"][:, bass.ds(h + 64, 1)]
                                           ).then_inc(qk_copied.sem, 1)
                            if n == NA - 1:
                                log_sigmoid(act, None, None, lb[:], lc[:], None, Lg, h)
                            continue
                        scale = QS if (ct >= DT) == (kind == "A") else 1.0
                        act.activation((qk if kind == "A" else raw)[:, ct, to], PS[half][:, 0:HALF], ACT.Copy,
                                       scale=scale).then_inc(qk_copied.sem, 1)
                        if kind == "C" and n == NA + 1:
                            act.wait_ge(*shifted.done(h, 0))
                            act.activation(lb[:], la[:], ACT.Exp).then_inc(exps.sem, 1)
                            act.activation(lc[:], la[:], ACT.Exp, scale=-1.0).then_inc(exps.sem, 1)
                            act.activation(eend[:], ends[:], ACT.Exp).then_inc(exps.sem, 1)
                    for t in range(T):
                        R = rows(t)
                        if kind == "A":
                            act.wait_ge(*logit_ready.done(h, t))
                            act.activation(E[0:R, 0:R], arg[0:R, 0:R], ACT.Exp).then_inc(decay_ready.sem, 1)
                        act.wait_ge(*gates_psum.done(h, t))
                        act.wait_ge(*(hg_ready if kind == "A" else gates_used).before(h, t))
                        act.activation(th[0:R, :], PS[2][0:R, 0:NG], ACT.Tanh, scale=0.5).then_inc(tanh_done.sem, 1)
                        act.wait_ge(*v_psum.done(h, t))
                        act.wait_ge(*state_psum.before(h, t))
                        act.activation(v[0:R, 0:DV], PS[3][0:R, 0:DV], ACT.Copy).then_inc(v_copied.sem, 1)
                        act.wait_ge(*nums_psum.done(h, t))
                        act.wait_ge(*g_ready.before(h, t))
                        act.activation(num_a[0:R, :], PS[6][0:R, 0:NV], ACT.Copy).then_inc(intra_copied.sem, 1)
                        if kind == "A":
                            act.wait_ge(*hg_ready.done(h, t))
                        elif kind == "B" and t:
                            act.wait_ge(*num_ready.done(h, t - 1))
                        else:
                            act.wait_ge(*intra_copied.done(h, t))
                        src = hg if kind == "A" else (num if kind == "B" and t else num_a)
                        act.activation(sq[0:R, :], src[0:R, 0:DV], ACT.Square, accum_out=sm[0:R, 3:4]).then_inc(squared.sem, 1)
                        if t >= PT - 1:
                            i = t - PT + 1
                            act.wait_ge(*state_ready.done(h, t))
                            st = (p_st, s_st)[i]
                            act.dma_start((pS, sS)[i][bass.ds(h, 1)].rearrange("a (d p) v -> p (a d) v", p=P),
                                           St[i][:, :, 0:DV]).then_inc(st.sem, 16)
                            if kind == "A":
                                n_out = OUT[("pn", "sn")[i]][0, 0][bass.ds(h, 1)].rearrange("a (d p b) -> p (a d) b", p=P, b=1)
                                act.dma_start(n_out, St[i][:, :, DV:NV], allow_slow_non_contiguous=True).then_inc(st.sem, 16)

            @block.vector
            def _(dve):
                if kind == "A":
                    dve.memset(v[:, DV:NV], 1.0).then_inc(filled.sem, 1)
                if kind == "C":
                    dve.memset(sT[:], 0.0).then_inc(filled.sem, 1)
                    dve.wait_ge(*filled.done(0, 0))
                with dve.Fori(0, H) as h:
                    link = Link(dve, lk, h)
                    if kind == "B":
                        for i in range(2):
                            dve.wait_ge(*qk_copied.done(h, 4 * i + 3))
                            x1, x2 = raw[:, 2 * i, :], raw[:, 2 * i + 1, :]
                            for a, b, out, op in ((x1, x2, 0, ALU.subtract), (x2, x1, 1, ALU.add)):
                                link(dve.tensor_tensor(ra[:], a, M.c("cos"), ALU.mult))
                                link(dve.tensor_tensor(rb[:], b, M.c("sin"), ALU.mult))
                                last = dve.tensor_tensor(qk[:, 2 * i + out, :], ra[:], rb[:], op)
                                if (i, out) == (1, 1):
                                    last.then_inc(qk_ready.sem, 1)
                                else:
                                    link(last)
                    elif kind == "C":
                        dve.wait_ge(*qk_copied.done(h, NA - 1))
                        link(log_sigmoid(None, dve, la[:], lb[:], lc[:], la[:], Lg, h))
                        link(dve.tensor_scalar(la[:], la[:], 1.0 / 16.0, None, ALU.mult))
                        for t in range(T):
                            last = dve.tensor_tensor_scan(bT[:, cols(t)], M.c("ones")[:, 0:rows(t)], la[:, cols(t)], 0.0,
                                                          ALU.mult, ALU.add)
                        link(last)
                        for t in range(T):
                            mid = t * P + rows(t) // 2 - 1
                            end = t * P + rows(t) - 1
                            dve.tensor_copy(ends[:, 0, t:t + 1], bT[:, mid:mid + 1])
                            dve.tensor_copy(ends[:, 2, t:t + 1], bT[:, end:end + 1])
                            last = dve.tensor_scalar(ends[:, 1, t:t + 1], bT[:, end:end + 1], bT[:, mid:mid + 1], None, ALU.subtract)
                        link(last)
                        for t in range(T):
                            last = dve.tensor_scalar(la[:, cols(t)], bT[:, cols(t)], ends[:, 0, t:t + 1], None, ALU.subtract)
                        last.then_inc(shifted.sem, 1)
                        dve.wait_ge(*exps.done(h, 2))
                        dve.wait_ge(*qk_copied.done(h, NA + 1))
                        link(dve.tensor_tensor(qk[:, 0, :], raw[:, 0, :], lb[:], ALU.mult))
                        dve.wait_ge(*qk_copied.done(h, NP - 1))
                        dve.tensor_tensor(qk[:, 1, :], raw[:, 1, :], lc[:], ALU.mult).then_inc(qk_ready.sem, 1)
                    for t in range(T):
                        R, cs = rows(t), cols(t)
                        S = St[t // PT]
                        u = h + t * H
                        if kind == "A":
                            dve.scalar_tensor_tensor(arg[0:R, 0:R], M["negM"][0:R, bass.ds(h, 1), cs].rearrange("p a t -> p (a t)"),
                                                     M["ucol"][0:R, t, bass.ds(h, 1)], M.c("neg_causal", R)[:, 0:R],
                                                     ALU.add, ALU.add).then_inc(logit_ready.sem, 1)
                            dve.wait_ge(*decay_ready.done(h, t))
                        dve.wait_ge(*scores_psum.done(h, t))
                        if kind == "C":
                            dve.sem_inc(M.passed, 1)
                            dve.copy_predicated(sT[0:R, 0:R], M.c("mask", R)[:, 0:R].bitcast(U32), PS[4][0:R, 0:R]).then_inc(scores_ready.sem, 1)
                            dve.tensor_copy(kw[0:R, :], PS[4][0:R, P:2 * P]).then_inc(kw_ready.sem, 1)
                        else:
                            if kind == "A":
                                by, kc = E[0:R, 0:R], M["mcols"][0:R, 1, t, bass.ds(h, 1)]
                            else:
                                by = M["const"][0:R, bass.ds(h * P + M.at["decay"][0], R)]
                                kc = M["const"][0:R, bass.ds(h + M.at["k_decay"][0] + H * (t // PT), 1)]
                            dve.tensor_tensor(sT[0:R, 0:R], PS[4][0:R, 0:R], by, ALU.mult).then_inc(scores_ready.sem, 1)
                            dve.tensor_scalar(kw[0:R, :], PS[4][0:R, P:(1 + DT) * P], kc, None, ALU.mult).then_inc(kw_ready.sem, 1)
                        if t == PT:
                            dve.wait_ge(*sl.done(h, sl.per - 1))
                        if t == 0:
                            dve.wait_ge(*p_st.before(h, 0))
                        if t:
                            dve.wait_ge(*state_ready.before(h, t))
                        if kind == "C" and t:
                            dve.tensor_scalar(Sc[:], S[:, 0, :], eend[:, 0, t:t + 1], None, ALU.mult).then_inc(sc_ready.sem, 1)
                        dve.wait_ge(*tanh_done.done(h, t))
                        dve.wait_ge(*g_ready.before(h, t))
                        dve.scalar_tensor_tensor(zs[0:R, :], th[0:R, NG - DV:NG], 1.0, PS[2][0:R, NG - DV:NG], ALU.add, ALU.mult
                                                 ).then_inc(gates_used.sem, 1)
                        dve.wait_ge(*state_psum.done(h, t))
                        if kind == "C":
                            dve.tensor_scalar(nS[:], PS[0][:, 0:NV], eend[:, 1, t:t + 1], None, ALU.mult).then_inc(nS_ready.sem, 1)
                            dve.wait_ge(*nS_ready.done(h, t))
                            if t == 0:
                                dve.tensor_copy(S[:, 0, :], nS[:]).then_inc(state_ready.sem, 1)
                            else:
                                dve.scalar_tensor_tensor(S[:, 0, :], S[:, 0, :], eend[:, 2, t:t + 1], nS[:], ALU.mult, ALU.add
                                                         ).then_inc(state_ready.sem, 1)
                        else:
                            dec = (M["mcols"][:, 2, t, bass.ds(h, 1)] if kind == "A" else
                                   M["const"][:, bass.ds(h + M.at["s_decay"][0] + H * (t // PT), 1)])
                            for d in range(DT):
                                if t == 0:
                                    last = dve.tensor_copy(S[:, d, :], PS[d][:, 0:NV])
                                else:
                                    last = dve.scalar_tensor_tensor(S[:, d, :], S[:, d, :], dec, PS[d][:, 0:NV], ALU.mult, ALU.add)
                            last.then_inc(state_ready.sem, 1)
                        dve.wait_ge(*intra_copied.done(h, t))
                        n_src = num_a
                        if t and kind != "C":
                            w = (M["mcols"][0:R, 0, t, bass.ds(h, 1)] if kind == "A" else
                                 M["const"][0:R, bass.ds(h + M.at["q_decay"][0], 1)])
                            dve.scalar_tensor_tensor(num[0:R, :], PS[5][0:R, 0:NV], w, num_a[0:R, :], ALU.mult, ALU.add
                                                     ).then_inc(num_ready.sem, 1)
                            dve.wait_ge(*num_ready.done(h, t - 1))
                            n_src = num
                        if kind == "A":
                            dcol = n_src[0:R, DV:NV]
                            dve.scalar_tensor_tensor(sm[0:R, 0:1], dcol, -1.0, dcol, ALU.mult, ALU.max).then_inc(den.sem, 1)
                            dve.wait_ge(*den.done(h, 4 * t))
                            dve.tensor_tensor(sm[0:R, 1:2], sm[0:R, 0:1], M["mcols"][0:R, 3, t, bass.ds(h, 1)], ALU.max).then_inc(den.sem, 1)
                            dve.wait_ge(*den.done(h, 4 * t + 1))
                            dve.reciprocal(sm[0:R, 2:3], sm[0:R, 1:2]).then_inc(den.sem, 1)
                            dve.wait_ge(*den.done(h, 4 * t + 2))
                            dve.tensor_scalar(hg[0:R, :], n_src[0:R, 0:DV], sm[0:R, 2:3], None, ALU.mult).then_inc(den.sem, 1)
                            dve.wait_ge(*den.done(h, 4 * t + 3))
                            dve.scalar_tensor_tensor(hg[0:R, :], th[0:R, 0:DV], 1.0, hg[0:R, :], ALU.add, ALU.mult).then_inc(hg_ready.sem, 1)
                            fin = hg
                        else:
                            fin = n_src
                        dve.wait_ge(*rstd_ready.done(h, t))
                        dve.wait_ge(*gates_used.done(h, t))
                        dve.wait_ge(*gT_psum.before(h, t))
                        dve.scalar_tensor_tensor(g[0:R, :], fin[0:R, 0:DV], sm[0:R, 5:6], zs[0:R, :], ALU.mult, ALU.mult
                                                 ).then_inc(g_ready.sem, 1)
                        for tt in ([t - 1] if t else []) + ([t] if t == T - 1 else []):
                            dve.wait_ge(*gT_psum.done(h, tt))
                            for d in range(2):
                                last = dve.tensor_scalar(M["gT"][:, bass.ds(h * 2 + (g_row + d), 1), cols(tt)].rearrange("p a t -> p (a t)"),
                                                         PS[7][:, d * P:d * P + rows(tt)], M["vec"][:, bass.ds(h * 2 + (g_col + d), 1)],
                                                         None, ALU.mult)
                            last.then_inc(gT_copied.sem, 1)
                    link.close()


def odd_gates(nc, M, IN, OUT):
    with Phase(nc, "odd_gates") as ph:
        act_norm, pool_norm, dve_norm, pe_norm = norm_steps(ph, M, 1)
        H = GDN_H
        sb, sig = ph.sb, ph.counter
        wg = sb("w_gates", [P, KT, 96])
        cleared = sig("w_gates_cleared")
        dt_b, a_l = sb("dt_bias", [H, 1]), sb("a_log", [H, 1])
        ndt, ea = sb("minus_dt", [H, 1]), sb("exp_a", [H, 1])
        cache = sb("cache_rows", [72, P])
        gi, ta, tb = (sb(n, [H, 2, TOK]) for n in ("gate_in", "ls_a", "ls_b"))
        ge_rows = sb("ge_rows", [H, T, H])
        col, bro = sb("gate_cols", [P, 2, T, H]), sb("gate_broadcast", [P, T, H])
        arg = sb("gate_args", [P, 5, T, H])
        wl = sig("w_gates_loaded", 16 * 6)
        proj, copied = sig("gates_psum", 3), sig("gates_copied", 6)
        S = {n: sig("ls_" + n) for n in ("abs", "exp", "plus", "log")}
        lk = sig("vector_step")
        exp_a, rows_ready, colsp, args_ready, exps = (sig(n) for n in ("exp_a_ready", "rows_ready", "cols_psum", "args_ready", "gate_exps"))
        signs, beta = sig("minus_dt_ready"), sig("beta_halved")
        cachep, cachec = sig("cache_psum"), sig("cache_copied")
        PS = M["ps"]
        rows_g = M["grow"]
        with nc.Block() as block:

            @block.sync
            def _(sp):
                w_in = IN["w_in_odd"][0].rearrange("(k p) n -> p k n", p=P)
                sp.wait_ge(*cleared.done(0, 0))
                for i, (c0, n) in enumerate(((2 * D, RANK), (5 * D + RANK, H), (5 * D + RANK + H, H))):
                    sp.dma_start(wg[:, :, 32 * i:32 * i + n], w_in[:, :, c0:c0 + n]).then_inc(wl.sem, 16)
                sp.dma_start(dt_b[:], IN["dt_bias"][0].rearrange("(h a) -> h a", a=1)).then_inc(wl.sem, 16)
                sp.dma_start(a_l[:], IN["a_log"][0].rearrange("(h a) -> h a", a=1)).then_inc(wl.sem, 16)
                sp.dma_start(cache[:], IN["cache_gdn_conv"][0, 0].rearrange("r (c p) -> (r c) p", p=P)).then_inc(wl.sem, 16)

            @block.gpsimd
            def _(pool):
                pool_norm(pool)

            @block.tensor
            def _(pe):
                pe_norm(pe)
                pe.wait_ge(*wl.done(0, 95))
                small_projection(pe, M, wg, 0, 64 + H, (4, 5)).then_inc(proj.sem, 1)
                pe.transpose(PS[1][:, 0:72], cache[:], M.c("ident", 72, 72)).then_inc(cachep.sem, 1)
                pe.wait_ge(*rows_ready.done(0, 0))
                for n, r in enumerate((rows_g[:, 0, :], gi[:, 1, :])):
                    for t in range(T):
                        at = (n * T + t) * H
                        pe.transpose(PS[0][0:rows(t), at:at + H], r[:, cols(t)], M.c("ident", H, H))
                pe.matmul(PS[2][:, 0:T * H], M.c("ones", H), ge_rows[:].rearrange("p t h -> p (t h)"),
                          start=True, stop=True).then_inc(colsp.sem, 1)

            @block.scalar
            def _(act):
                act_norm(act)
                act.wait_ge(*wl.done(0, 95))
                act.activation(ea[:], a_l[:], ACT.Exp).then_inc(exp_a.sem, 1)
                act.wait_ge(*signs.done(0, 0))
                for i in range(3):
                    act.wait_ge(*proj.done(0, 0))
                    for half in range(2):
                        to = slice(half * HALF, (half + 1) * HALF)
                        src = PS[4 + half][32 * i:32 * i + 32]
                        if i == 1:
                            act.activation(gi[:, 0, to], src[0:H, 0:HALF], ACT.Identity, bias=ndt[:], scale=-1.0).then_inc(copied.sem, 1)
                        else:
                            n = (RANK, 0, H)[i]
                            out = M["a1T"][:, to] if i == 0 else gi[:, 1, to]
                            act.activation(out, src[0:n, 0:HALF], ACT.Copy).then_inc(copied.sem, 1)
                log_sigmoid(act, None, None, ta[:], tb[:], None, S)
                act.wait_ge(*args_ready.done(0, 0))
                act.activation(M["gcols"][:], arg[:], ACT.Exp).then_inc(exps.sem, 1)

            @block.vector
            def _(dve):
                link = Link(dve, lk)
                dve.memset(wg[:], 0.0).then_inc(cleared.sem, 1)
                dve.memset(col[:], 0.0)
                dve.wait_ge(*wl.done(0, 95))
                dve.tensor_scalar(ndt[:], dt_b[:], -1.0, None, ALU.mult).then_inc(signs.sem, 1)
                dve_norm(dve)
                dve.wait_ge(*cachep.done(0, 0))
                dve.tensor_copy(M["cacheT"][:], PS[1][:, 0:72]).then_inc(cachec.sem, 1)
                dve.wait_ge(*copied.done(0, 5))
                link(log_sigmoid(None, dve, gi[:], ta[:], tb[:], gi[:], S))
                dve.wait_ge(*exp_a.done(0, 0))
                link(dve.tensor_scalar(gi[:, 0, :], gi[:, 0, :], ea[:], None, ALU.mult))
                for t in range(T):
                    last = dve.tensor_tensor_scan(rows_g[:, 0, cols(t)], M.c("ones", H, rows(t)), gi[:, 0, cols(t)], 0.0, ALU.mult, ALU.add)
                link(last)
                dve.tensor_tensor(rows_g[:, 1, :], rows_g[:, 0, :], gi[:, 1, :], ALU.add)
                for t in range(T):
                    end = t * P + rows(t) - 1
                    last = dve.tensor_scalar(ge_rows[:, t, :], M.c("diag8", H)[:, 0:H], rows_g[:, 0, end:end + 1], None, ALU.mult)
                last.then_inc(rows_ready.sem, 1)
                dve.wait_ge(*colsp.done(0, 0))
                src = PS[0][:, 0:2 * T * H].rearrange("p (n t h) -> p n t h", n=2, t=T)
                dve.tensor_copy(col[:, :, 0:PT, :], src[:, :, 0:PT, :])
                dve.tensor_copy(col[0:DEC, :, PT, :], src[0:DEC, :, PT, :])
                link(dve.tensor_copy(bro[:].rearrange("p t h -> p (t h)"), PS[2][:, 0:T * H]))
                dve.tensor_copy(M["Gcol"][:], col[:, 0])
                dve.tensor_copy(arg[:, 0], col[:, 0])
                dve.tensor_tensor(arg[:, 1], col[:, 0], col[:, 1], ALU.add)
                dve.tensor_copy(arg[:, 2], col[:, 1])
                dve.tensor_tensor(arg[:, 3], bro[:], col[:, 0], ALU.subtract)
                dve.tensor_copy(arg[:, 4], bro[:]).then_inc(args_ready.sem, 1)
                dve.wait_ge(*exps.done(0, 0))
                dve.tensor_scalar(M["gcols"][:, 2], M["gcols"][:, 2], 0.5, None, ALU.mult).then_inc(beta.sem, 1)


def gdn_heads(nc, M, IN, OUT):
    H = GDN_H
    NL = len(LEVELS) - 1
    W = 3 + SEQ + 3 + DEC
    C = W - 3
    S0 = SEQ + 3
    PS = M["ps"]
    w_in = IN["w_in_odd"][0].rearrange("(k p) n -> p k n", p=P)
    sec = [2 * D + RANK + i * D for i in range(3)] + [6 * D + RANK + 2 * H]
    TB = (4, 6, 2, 3, 5)
    GB = (7, 4)

    def conv_cols(t):
        return slice(t * P, (t + 1) * P) if t < PT else slice(S0, S0 + DEC)

    with Phase(nc, "gdn", first=1) as ph:
        sb, sig = ph.sb, ph.counter
        wT = sb("w_qkvz", [P, KT, 4 * P])
        pj, cv, thc = sb("pre_conv", [P, 3, W]), sb("conv", [P, 3, C]), sb("tanh_conv", [P, 3, C])
        tk = sb("qkv_tokens", [P, T, 3, P])
        sqs = thc[:].rearrange("p a b -> p (a b)")[:, 0:T * 2 * P].rearrange("p (t a d) -> p t a d", t=T, a=2)
        kn, qn, kbe, kg, bv = (sb(n, [P, T, P]) for n in ("k_norm", "q_norm", "k_beta_decay", "k_end", "v_beta"))
        ss, ms, rn, mh = (sb(n, [P, T, 2]) for n in ("ss2", "ms2", "rn2", "minus_half"))
        sc = sb("scales", [P, 4, T])
        kT, qT = sb("kT", [P, TOK]), sb("qT", [P, TOK])
        gsel = sb("G_selected", [H, 2, TOK])
        E = sb("E", [P, 2, TOK])
        AT, atT = sb("AT", [P, TOK]), sb("attnT", [P, TOK])
        X, XT, Q = sb("X", [P, TOK]), sb("XT", [P, TOK]), sb("Q", [P, TOK])
        ML = sb("A_level", [P, 2, TOK])
        wN = sb("w_minus_T", [P, TOK])
        u, o_a, o, g, sqj = (sb(n, [P, P]) for n in ("u", "o_intra", "o", "g", "squares"))
        zr, tz, zs = (sb(n, [P, TOK]) for n in ("z", "tanh_z", "z_silu"))
        sm = sb("small", [P, 4])
        St = [sb("state_prompt", [P, P]), sb("state_sample", [P, P])]
        newc = sb("new_cache", [P, 2, 72])
        cr = sb("new_cache_rows", [72, 2, P])

        names = {"w_loaded0": 16, "w_loaded1": 16, "w_loaded2": 16, "w_loaded3": 16, "state_loaded": 16, "prompt_stored": 16,
                 "sample_stored": 16, "gsel_ready": 1, "G_psum": 1, "arg_ready": 1, "E_ready": 2, "proj_psum": 8, "proj_copied": 8,
                 "cache_put": 1, "conv_step": 9, "conv_ready": 3, "tanh_conv": 3, "silu_ready": 3, "cache_saved": 1, "tanh_z": 1,
                 "z_ready": 1,
                 "tok_psum": T, "tok_copied": T, "tok_squared": 1, "ss_ready": 1, "ms_ready": 1, "rn_ready": 1, "scale_a": 1, "scale_b": 1,
                 "kq_norm": 1, "kq_psum": 1, "kq_copied": 1, "kk_psum": 1, "A_ready": 1, "attn_ready": 1, "level_ready": NL,
                 "A1_ready": 1, "XT1_ready": 1, "X1_psum": 1, "X1_copied": 1,
                 "Q_psum": NL, "Q_copied": NL, "XX_psum": NL, "X_ready": NL, "w_psum": 1, "w_copied": 1, "kv_scaled": 1,
                 "u_psum": T, "u_copied": T, "o_psum": T, "o_copied": T, "o_ready": PT, "squared": T, "mean_ready": T, "rstd_ready": T,
                 "state_psum": T, "state_ready": T, "g_ready": T, "gT_psum": T, "gT_copied": T}
        s = {n: sig(n, k) for n, k in names.items()}
        cleared = sig("cleared")
        cacheT_psum, cacheT_copied, cache_stored = sig("cache_psum", 2), sig("cache_copied", 2), sig("cache_stored", 32)

        def tiles(x, t):
            return x[0:rows(t), t * P:t * P + rows(t)]

        def bank(n, t):
            return PS[n[0]][:, t * P:(t + 1) * P] if t < PT else PS[5][0:DEC, n[1]:n[1] + DEC]

        def blocks(x):
            return x.rearrange("p (t c) -> p t c", t=PT)

        def each_block(c):
            return c.rearrange("p (a c) -> p a c", a=1).broadcast_to([P, PT, P])


        def project(pe, h, a, b):
            for i in range(a, b) if h is not None else ():
                n, k = divmod(i, KT)
                ct, half = divmod(n, 2)
                if k == 0:
                    if half == 0:
                        pe.wait_ge(*s[f"w_loaded{ct}"].done(h, 15))
                    pe.wait_ge(*(s["proj_copied"].done(h, n - 2) if n >= 2 else s["proj_copied"].before(h, 0)))
                last = pe.matmul(PS[half][:, 0:HALF], wT[:, k, ct * P:(ct + 1) * P], M["hT"][:, k, half * HALF:(half + 1) * HALF],
                                 start=(k == 0), stop=(k == KT - 1))
                if k == KT - 1:
                    last.then_inc(s["proj_psum"].sem, 1)

        def take_projection(act, h, n):
            if h is None:
                return
            ct, half = divmod(n, 2)
            if n == 0:
                act.wait_ge(*s["cache_saved"].before(h, 0))
            if n == 6:
                act.wait_ge(*s["z_ready"].before(h, 0))
            act.wait_ge(*s["proj_psum"].done(h, n))
            if ct == 3:
                act.activation(zr[:, half * HALF:(half + 1) * HALF], PS[half][:, 0:HALF], ACT.Copy).then_inc(s["proj_copied"].sem, 1)
            elif half == 0:
                act.activation(pj[:, ct, 3:3 + HALF], PS[0][:, 0:HALF], ACT.Copy).then_inc(s["proj_copied"].sem, 1)
            else:
                act.activation(pj[:, ct, 3 + HALF:3 + SEQ], PS[1][:, 0:SEQ - HALF], ACT.Copy)
                act.activation(pj[:, ct, 6 + SEQ:W], PS[1][:, SEQ - HALF:HALF], ACT.Copy).then_inc(s["proj_copied"].sem, 1)

        def tanh_conv(act, h, ct):
            if h is None:
                return
            act.wait_ge(*s["conv_ready"].done(h, ct))
            if ct == 0:
                act.wait_ge(*s["ss_ready"].before(h, 0))
            act.activation(thc[:, ct, :], cv[:, ct, :], ACT.Tanh, scale=0.5).then_inc(s["tanh_conv"].sem, 1)

        def tanh_z(act, h):
            if h is None:
                return
            act.wait_ge(*s["proj_copied"].done(h, 7))
            act.activation(tz[:], zr[:], ACT.Tanh, scale=0.5).then_inc(s["tanh_z"].sem, 1)

        def convolve(dve, h, ct):
            if h is None:
                return
            if ct == 0:
                dve.wait_ge(*s["cache_saved"].before(h, 0))
                dve.wait_ge(*s["tok_psum"].before(h, 0))
                for c in range(3):
                    last = dve.tensor_copy(pj[:, c, S0:S0 + 3], cacheT_of(M, h, c))
                last.then_inc(s["cache_put"].sem, 1)
                dve.wait_ge(*s["cache_put"].done(h, 0))
            dve.wait_ge(*s["proj_copied"].done(h, 2 * ct + 1))
            for j in range(4):
                wj = M["conv"][:, bass.ds(h + (24 * j + 8 * ct), 1)]
                if j == 0:
                    ins = dve.tensor_scalar(cv[:, ct, :], pj[:, ct, 0:C], wj, None, ALU.mult)
                else:
                    ins = dve.scalar_tensor_tensor(cv[:, ct, :], pj[:, ct, j:j + C], wj, cv[:, ct, :], ALU.mult, ALU.add)
                if j < 3:
                    ins.then_inc(s["conv_step"].sem, 1)
                    dve.wait_ge(*s["conv_step"].done(h, 3 * ct + j))
                else:
                    ins.then_inc(s["conv_ready"].sem, 1)

        def silu_conv(dve, h, ct):
            if h is None:
                return
            dve.wait_ge(*s["tanh_conv"].done(h, ct))
            dve.scalar_tensor_tensor(cv[:, ct, :], thc[:, ct, :], 1.0, cv[:, ct, :], ALU.add, ALU.mult).then_inc(s["silu_ready"].sem, 1)

        def save_cache(dve, h):
            if h is None:
                return
            for ct in range(3):
                for i, c0 in enumerate((SEQ, W - 3)):
                    last = dve.tensor_copy(new_cache_of(newc, i, h, ct), pj[:, ct, c0:c0 + 3])
            last.then_inc(s["cache_saved"].sem, 1)

        def select_G(dve, h):
            if h is None:
                return
            dve.wait_ge(*s["G_psum"].before(h, 0))
            dve.tensor_scalar(gsel[:], M["grow"][:], M["const"][0:H, bass.ds(h + M.at["diag8"][0], 1)], None, ALU.mult
                              ).then_inc(s["gsel_ready"].sem, 1)

        def pe_turn(pe, h, ahead):
            pe.wait_ge(*s["silu_ready"].done(h, 2))
            pe.wait_ge(*s["state_ready"].before(h, 0))
            pe.wait_ge(*s["u_copied"].before(h, 0))
            for t in range(T):
                if t == PT:
                    pe.wait_ge(*s["gT_copied"].before(h, 0))
                pe.sem_inc(M.passed, 1)
                for i in range(3):
                    last = pe.transpose(PS[TB[t]][0:rows(t), i * P:(i + 1) * P], cv[:, i, conv_cols(t)], M.c("ident", P, P))
                last.then_inc(s["tok_psum"].sem, 1)
            pe.wait_ge(*s["gsel_ready"].done(h, 0))
            pe.wait_ge(*s["o_ready"].before(h, 0))
            pe.wait_ge(*s["o_copied"].before(h, 0))
            for i in range(2):
                if i:
                    pe.wait_ge(*s["tok_copied"].done(h, 1))
                last = pe.matmul(PS[GB[i]][:, 0:SEQ], M.c("ones", H), gsel[:, i, 0:SEQ], start=True, stop=True)
            for i in range(2):
                last = pe.matmul(PS[6][:, i * DEC:(i + 1) * DEC], M.c("ones", H), gsel[:, i, SEQ:TOK], start=True, stop=True)
            last.then_inc(s["G_psum"].sem, 1)
            project(pe, ahead, 0, 18)
            pe.wait_ge(*s["tok_copied"].done(h, T - 1))
            pe.wait_ge(*s["kq_norm"].done(h, 0))
            pe.sem_inc(M.passed, 1)
            for i, x in enumerate((kn, qn)):
                for t in range(T):
                    R = rows(t)
                    out = PS[2 + i][:, t * P:(t + 1) * P] if t < PT else PS[5][:, i * DEC:(i + 1) * DEC]
                    last = pe.transpose(out, x[0:R, t, :], M.c("ident", R, R))
            last.then_inc(s["kq_psum"].sem, 1)
            project(pe, ahead, 18, 20)
            pe.wait_ge(*s["kq_copied"].done(h, 0))
            for i, x in enumerate((kT, qT)):
                for t in range(T):
                    last = pe.matmul(bank((2 + i, i * DEC), t), kT[:, cols(t)], x[:, cols(t)], start=True, stop=True)
            last.then_inc(s["kk_psum"].sem, 1)
            project(pe, ahead, 20, 28)
            pe.wait_ge(*s["XT1_ready"].done(h, 0))
            pe.wait_ge(*s["attn_ready"].done(h, 0))
            pe.sem_inc(M.passed, 1)
            for t in range(T):
                last = pe.transpose(bank((4, 0), t), tiles(XT, t), M.c("ident", rows(t), rows(t)))
            last.then_inc(s["X1_psum"].sem, 1)
            project(pe, ahead, 28, 30)
            pe.wait_ge(*s["X1_copied"].done(h, 0))
            for n in range(NL):
                n_t = T if n < NL - 1 else PT
                pe.wait_ge(*s["level_ready"].done(h, n))
                if n:
                    pe.wait_ge(*s["X_ready"].done(h, n - 1))
                for t in range(n_t):
                    last = pe.matmul(bank((2, 2 * DEC), t), tiles(ML[:, n % 2, :], t), tiles(X, t), start=True, stop=True)
                last.then_inc(s["Q_psum"].sem, 1)
                project(pe, ahead, 30 + 6 * n, 32 + 6 * n)
                pe.wait_ge(*s["Q_copied"].done(h, n))
                for t in range(n_t):
                    if n < NL - 1:
                        pe.matmul(bank((3, 0), t), tiles(XT, t), tiles(Q, t), start=True, stop=True)
                    last = pe.matmul(bank((4, DEC), t), tiles(Q, t), tiles(XT, t), start=True, stop=True)
                last.then_inc(s["XX_psum"].sem, 1)
                project(pe, ahead, 32 + 6 * n, min(36 + 6 * n, 8 * KT))
            pe.wait_ge(*s["X_ready"].done(h, NL - 1))
            pe.wait_ge(*s["kv_scaled"].done(h, 0))
            for t in range(T):
                R = rows(t)
                out = PS[2][:, t * P:t * P + R] if t < PT else PS[5][:, 0:DEC]
                last = pe.matmul(out, kbe[0:R, t, :], tiles(XT, t), start=True, stop=True)
            last.then_inc(s["w_psum"].sem, 1)

            def turn_g(t):
                pe.wait_ge(*s["g_ready"].done(h, t))
                pe.wait_ge(*s["gT_copied"].before(h, t))
                pe.sem_inc(M.passed, 1)
                pe.transpose(PS[5][:, 0:rows(t)], g[0:rows(t), :], M.c("ident", rows(t), rows(t))).then_inc(s["gT_psum"].sem, 1)

            for t in range(T):
                R, S = rows(t), St[t // PT]
                if t == 1:
                    pe.wait_ge(*s["w_copied"].done(h, 0))
                if t:
                    pe.wait_ge(*s["state_ready"].before(h, t))
                if t == PT:
                    pe.wait_ge(*s["state_loaded"].done(h, 15))
                pe.wait_ge(*s["u_copied"].before(h, t))
                pairs = [(tiles(XT, t), bv[0:R, t, :])] + ([(wN[:, cols(t)], S[:])] if t else [])
                pe.sem_inc(M.passed, 1)
                matmul_chain(pe, PS[6][0:R, 0:P], pairs).then_inc(s["u_psum"].sem, 1)
                pe.wait_ge(*s["o_copied"].before(h, t))
                if t:
                    pe.wait_ge(*s["o_ready"].before(h, t - 1))
                    pe.matmul(PS[7][0:R, 0:P], qT[:, cols(t)], S[:], start=True, stop=True)
                pe.wait_ge(*s["u_copied"].done(h, t))
                pe.sem_inc(M.passed, 1)
                pe.matmul(PS[4][:, 0:P], kg[0:R, t, :], u[0:R, :], start=True, stop=True).then_inc(s["state_psum"].sem, 1)
                pe.matmul(PS[7][0:R, P:2 * P], tiles(atT, t), u[0:R, :], start=True, stop=True).then_inc(s["o_psum"].sem, 1)
                if t:
                    turn_g(t - 1)
            turn_g(T - 1)

        def act_turn(act, h, ahead):
            act.wait_ge(*s["sample_stored"].before(h, 0))
            act.dma_start(St[1][:], IN["state_gdn"][0, 0][bass.ds(h, 1)].rearrange("a p v -> p (a v)")).then_inc(s["state_loaded"].sem, 16)
            for t in range(T):
                R = rows(t)
                act.wait_ge(*s["tok_psum"].done(h, t))
                act.activation(tk[0:R, t, :, :], PS[TB[t]][0:R, 0:3 * P].rearrange("p (a d) -> p a d", a=3), ACT.Copy
                               ).then_inc(s["tok_copied"].sem, 1)
            act.wait_ge(*s["tok_copied"].done(h, T - 1))
            act.wait_ge(*s["silu_ready"].done(h, 2))
            act.activation(sqs, tk[:, :, 0:2, :], ACT.Square).then_inc(s["tok_squared"].sem, 1)
            take_projection(act, ahead, 0)
            act.wait_ge(*s["arg_ready"].done(h, 0))
            act.activation(E[:, :, 0:SEQ], E[:, :, 0:SEQ], ACT.Exp).then_inc(s["E_ready"].sem, 1)
            act.activation(E[0:DEC, :, SEQ:TOK], E[0:DEC, :, SEQ:TOK], ACT.Exp).then_inc(s["E_ready"].sem, 1)
            take_projection(act, ahead, 1)
            act.wait_ge(*s["kq_psum"].done(h, 0))
            for i, x in enumerate((kT, qT)):
                act.activation(x[:, 0:SEQ], PS[2 + i][:, 0:SEQ], ACT.Copy)
                last = act.activation(x[:, SEQ:TOK], PS[5][:, i * DEC:(i + 1) * DEC], ACT.Copy)
            last.then_inc(s["kq_copied"].sem, 1)
            tanh_conv(act, ahead, 0)
            take_projection(act, ahead, 2)
            act.wait_ge(*s["X1_psum"].done(h, 0))
            act.activation(X[:, 0:SEQ], PS[4][:, :], ACT.Copy)
            act.activation(X[0:DEC, SEQ:TOK], PS[5][0:DEC, 0:DEC], ACT.Copy).then_inc(s["X1_copied"].sem, 1)
            for n in range(NL):
                act.wait_ge(*s["Q_psum"].done(h, n))
                last = act.activation(Q[:, 0:SEQ], PS[2][:, :], ACT.Copy)
                if n < NL - 1:
                    last = act.activation(Q[0:DEC, SEQ:TOK], PS[5][0:DEC, 2 * DEC:3 * DEC], ACT.Copy)
                last.then_inc(s["Q_copied"].sem, 1)
                if n == 0:
                    take_projection(act, ahead, 3)
                elif n == 1:
                    take_projection(act, ahead, 4)
                elif n == 2:
                    tanh_conv(act, ahead, 1)
                    take_projection(act, ahead, 5)
                elif n == 4:
                    tanh_conv(act, ahead, 2)
                    take_projection(act, ahead, 6)
                elif n == 5:
                    take_projection(act, ahead, 7)
            act.wait_ge(*s["w_psum"].done(h, 0))
            act.activation(wN[:, 0:SEQ], PS[2][:, :], ACT.Copy, scale=-1.0)
            act.activation(wN[:, SEQ:TOK], PS[5][:, 0:DEC], ACT.Copy, scale=-1.0).then_inc(s["w_copied"].sem, 1)
            for t in range(T):
                R = rows(t)
                act.wait_ge(*s["u_psum"].done(h, t))
                act.wait_ge(*s["o_psum"].before(h, t))
                act.activation(u[0:R, :], PS[6][0:R, 0:P], ACT.Copy).then_inc(s["u_copied"].sem, 1)
                act.wait_ge(*s["o_psum"].done(h, t))
                act.wait_ge(*s["g_ready"].before(h, t))
                act.activation(o_a[0:R, :], PS[7][0:R, P:2 * P], ACT.Copy).then_inc(s["o_copied"].sem, 1)
                act.wait_ge(*(s["o_ready"].done(h, t - 1) if t else s["o_copied"].done(h, t)))
                act.activation(sqj[0:R, :], (o if t else o_a)[0:R, :], ACT.Square, accum_out=sm[0:R, 0:1]).then_inc(s["squared"].sem, 1)
                if t == 0:
                    tanh_z(act, ahead)
                if t >= PT - 1:
                    i = t - PT + 1
                    act.wait_ge(*s["state_ready"].done(h, t))
                    act.dma_start(OUT[("pgdn", "sgdn")[i]][0, 0][bass.ds(h, 1)].rearrange("a p v -> p (a v)"), St[i][:]
                                  ).then_inc(s[("prompt_stored", "sample_stored")[i]].sem, 16)

        def dve_turn(dve, h, ahead):
            dve.wait_ge(*s["tanh_z"].done(h, 0))
            dve.wait_ge(*s["gT_copied"].before(h, 0))
            dve.scalar_tensor_tensor(zs[:], tz[:], 1.0, zr[:], ALU.add, ALU.mult).then_inc(s["z_ready"].sem, 1)
            dve.wait_ge(*s["tok_squared"].done(h, 0))
            dve.tensor_reduce(ss[:], sqs, AX.X, ALU.add).then_inc(s["ss_ready"].sem, 1)
            dve.wait_ge(*s["G_psum"].done(h, 0))
            dve.wait_ge(*s["attn_ready"].before(h, 0))
            for i, name in ((1, "neg_strict"), (0, "neg_causal")):
                for t in range(T):
                    R = rows(t)
                    src = PS[GB[i]][0:R, t * P:t * P + R] if t < PT else PS[6][0:R, i * DEC:(i + 1) * DEC]
                    last = dve.scalar_tensor_tensor(E[0:R, i, t * P:t * P + R], src, M["Gcol"][0:R, t, bass.ds(h, 1)],
                                                    M.c(name, R)[:, 0:R], ALU.subtract, ALU.add)
            last.then_inc(s["arg_ready"].sem, 1)
            dve.wait_ge(*s["rn_ready"].done(h, 0))
            dve.wait_ge(*s["kv_scaled"].before(h, 0))
            dve.tensor_scalar(sc[:, 0, :], rn[:, :, 1], 0.5, None, ALU.mult)
            dve.tensor_scalar(sc[:, 1, :], rn[:, :, 0], 0.5 * P ** -0.5, None, ALU.mult).then_inc(s["scale_a"].sem, 1)
            dve.wait_ge(*s["scale_a"].done(h, 0))

            def gcol(i):
                return M["gcols"][:, i, :, bass.ds(h, 1)].rearrange("p t a -> p (t a)")

            def spread(x):
                return x.rearrange("p (t a) -> p t a", a=1).broadcast_to([P, T, P])

            dve.tensor_tensor(kn[:], tk[:, :, 1, :], spread(sc[:, 0, :]), ALU.mult)
            dve.tensor_tensor(qn[:], tk[:, :, 0, :], spread(sc[:, 1, :]), ALU.mult).then_inc(s["kq_norm"].sem, 1)
            dve.tensor_tensor(sc[:, 2, :], sc[:, 0, :], gcol(1), ALU.mult)
            dve.tensor_tensor(sc[:, 3, :], sc[:, 0, :], gcol(3), ALU.mult).then_inc(s["scale_b"].sem, 1)
            dve.wait_ge(*s["scale_b"].done(h, 0))
            dve.tensor_tensor(kbe[:], tk[:, :, 1, :], spread(sc[:, 2, :]), ALU.mult)
            dve.tensor_tensor(kg[:], tk[:, :, 1, :], spread(sc[:, 3, :]), ALU.mult)
            dve.tensor_tensor(bv[:], tk[:, :, 2, :], spread(gcol(2)), ALU.mult).then_inc(s["kv_scaled"].sem, 1)
            convolve(dve, ahead, 0)
            dve.wait_ge(*s["kk_psum"].done(h, 0))
            dve.wait_ge(*s["E_ready"].done(h, 1))
            dve.tensor_tensor(AT[:, 0:SEQ], PS[2][:, :], E[:, 1, 0:SEQ], ALU.mult)
            dve.tensor_tensor(AT[0:DEC, SEQ:TOK], PS[5][0:DEC, 0:DEC], E[0:DEC, 1, SEQ:TOK], ALU.mult).then_inc(s["A_ready"].sem, 1)
            dve.wait_ge(*s["A_ready"].done(h, 0))
            dve.tensor_tensor(blocks(Q[:, 0:SEQ]), blocks(AT[:, 0:SEQ]), each_block(M.c("levels")[:, 0:P]), ALU.mult)
            dve.tensor_tensor(tiles(Q, PT), tiles(AT, PT), M.c("levels", DEC)[:, 0:DEC], ALU.mult).then_inc(s["A1_ready"].sem, 1)
            dve.wait_ge(*s["A1_ready"].done(h, 0))
            dve.tensor_tensor(blocks(XT[:, 0:SEQ]), each_block(M.c("ident")), blocks(Q[:, 0:SEQ]), ALU.subtract)
            dve.tensor_tensor(tiles(XT, PT), M.c("ident", DEC, DEC), tiles(Q, PT), ALU.subtract).then_inc(s["XT1_ready"].sem, 1)
            dve.tensor_tensor(atT[0:DEC, SEQ:TOK], PS[5][0:DEC, DEC:2 * DEC], E[0:DEC, 0, SEQ:TOK], ALU.mult)
            dve.tensor_tensor(atT[:, 0:SEQ], PS[3][:, :], E[:, 0, 0:SEQ], ALU.mult).then_inc(s["attn_ready"].sem, 1)
            dve.wait_ge(*s["X1_copied"].done(h, 0))
            for n in range(NL):
                if n == 1:
                    silu_conv(dve, ahead, 0)
                    convolve(dve, ahead, 1)
                elif n == 3:
                    silu_conv(dve, ahead, 1)
                    convolve(dve, ahead, 2)
                elif n == 4:
                    save_cache(dve, ahead)
                    select_G(dve, ahead)
                elif n == 5:
                    silu_conv(dve, ahead, 2)
                dve.wait_ge(*s["XX_psum"].done(h, n))
                if n < NL - 1:
                    dve.tensor_tensor(X[:, 0:SEQ], X[:, 0:SEQ], PS[3][:, :], ALU.subtract)
                    dve.tensor_tensor(X[0:DEC, SEQ:TOK], X[0:DEC, SEQ:TOK], PS[5][0:DEC, 0:DEC], ALU.subtract)
                    dve.tensor_tensor(XT[0:DEC, SEQ:TOK], XT[0:DEC, SEQ:TOK], PS[5][0:DEC, DEC:2 * DEC], ALU.subtract)
                dve.tensor_tensor(XT[:, 0:SEQ], XT[:, 0:SEQ], PS[4][:, :], ALU.subtract).then_inc(s["X_ready"].sem, 1)
                dve.wait_ge(*s["X_ready"].done(h, n))
            for t in range(T):
                R, S = rows(t), St[t // PT]
                if t == 0:
                    dve.wait_ge(*s["prompt_stored"].before(h, 0))
                if t == PT:
                    dve.wait_ge(*s["state_loaded"].done(h, 15))
                dve.wait_ge(*s["state_psum"].done(h, t))
                if t == 0:
                    dve.tensor_copy(S[:], PS[4][:, 0:P]).then_inc(s["state_ready"].sem, 1)
                else:
                    dve.wait_ge(*s["state_ready"].before(h, t))
                    dve.scalar_tensor_tensor(S[:], S[:], M["gcols"][:, 4, t, bass.ds(h, 1)], PS[4][:, 0:P], ALU.mult, ALU.add
                                             ).then_inc(s["state_ready"].sem, 1)
                dve.wait_ge(*s["o_copied"].done(h, t))
                if t:
                    dve.wait_ge(*s["g_ready"].before(h, t))
                    dve.scalar_tensor_tensor(o[0:R, :], PS[7][0:R, 0:P], M["gcols"][0:R, 0, t, bass.ds(h, 1)], o_a[0:R, :],
                                             ALU.mult, ALU.add).then_inc(s["o_ready"].sem, 1)
                dve.wait_ge(*s["rstd_ready"].done(h, t))
                dve.wait_ge(*s["gT_psum"].before(h, t))
                dve.tensor_scalar(g[0:R, :], (o if t else o_a)[0:R, :], sm[0:R, 2:3], None, ALU.mult).then_inc(s["g_ready"].sem, 1)
                for tt in ([t - 1] if t else []) + ([t] if t == T - 1 else []):
                    dve.wait_ge(*s["gT_psum"].done(h, tt))
                    dve.scalar_tensor_tensor(M["gT"][:, bass.ds(h + 8, 1), cols(tt)].rearrange("p a t -> p (a t)"), PS[5][:, 0:rows(tt)],
                                             M["vec"][:, bass.ds(h + 56, 1)], zs[:, cols(tt)], ALU.mult, ALU.mult
                                             ).then_inc(s["gT_copied"].sem, 1)

        def pool_turn(pool, h):
            pool.wait_ge(*s["ss_ready"].done(h, 0))
            pool.sem_inc(M.passed, 1)
            pool.tensor_scalar(ms[:], ss[:], 0.25, EPS, ALU.mult, ALU.add).then_inc(s["ms_ready"].sem, 1)
            pool.wait_ge(*s["ms_ready"].done(h, 0))
            pool.tensor_tensor(rn[:], ms[:], mh[:], ALU.pow).then_inc(s["rn_ready"].sem, 1)
            pool.wait_ge(*s["A_ready"].done(h, 0))
            for n in range(NL):
                if n >= 2:
                    pool.wait_ge(*s["Q_psum"].done(h, n - 2))
                lev = M.c("levels")[:, (n + 1) * P:(n + 2) * P]
                for t in range(T if n < NL - 1 else PT):
                    R = rows(t)
                    last = pool.tensor_tensor(tiles(ML[:, n % 2, :], t), tiles(AT, t), lev[0:R, 0:R], ALU.mult)
                last.then_inc(s["level_ready"].sem, 1)
            for t in range(T):
                R = rows(t)
                pool.wait_ge(*s["squared"].done(h, t))
                pool.sem_inc(M.passed, 1)
                pool.tensor_scalar(sm[0:R, 1:2], sm[0:R, 0:1], 1.0 / P, EPS, ALU.mult, ALU.add).then_inc(s["mean_ready"].sem, 1)
                pool.wait_ge(*s["mean_ready"].done(h, t))
                pool.tensor_tensor(sm[0:R, 2:3], sm[0:R, 1:2], M.c("half", R), ALU.pow).then_inc(s["rstd_ready"].sem, 1)

        nc.all_engine_barrier()
        with nc.Block() as block:

            @block.sync
            def _(sp):
                def load(h, ct):
                    sp.dma_start(wT[:, :, ct * P:(ct + 1) * P], w_in[:, :, bass.ds(h * P + sec[ct], P)]).then_inc(s[f"w_loaded{ct}"].sem, 16)
                for ct in range(4):
                    load(0, ct)
                with sp.Fori(1, H) as h:
                    for ct in range(4):
                        sp.wait_ge(*s["proj_psum"].done(h - 1, 2 * ct + 1))
                        load(h, ct)
                sp.wait_ge(*s["prompt_stored"].before(H, 0))
                sp.wait_ge(*s["sample_stored"].before(H, 0))
                for i, name in enumerate(("pconv", "sconv")):
                    sp.wait_ge(*cacheT_copied.done(0, i))
                    sp.dma_start(OUT[name][0, 0].rearrange("r (c p) -> (r c) p", p=P), cr[:, i, :]).then_inc(cache_stored.sem, 16)
                sp.wait_ge(*cache_stored.done(0, 31))

            @block.gpsimd
            def _(pool):
                pool.memset(mh[:], -0.5)
                with pool.Fori(0, H) as h:
                    pool_turn(pool, h)

            @block.tensor
            def _(pe):
                project(pe, 0, 0, 8 * KT)
                with pe.Fori(0, H - 1) as h:
                    pe_turn(pe, h, h + 1)
                pe_turn(pe, H - 1, None)
                pe.wait_ge(*s["cache_saved"].before(H, 0))
                for i in range(2):
                    pe.transpose(PS[i][0:72, 0:P], newc[:, i, :], M.c("ident", P, P)).then_inc(cacheT_psum.sem, 1)

            @block.scalar
            def _(act):
                for n in range(8):
                    take_projection(act, 0, n)
                    if n in (3, 5, 7):
                        tanh_conv(act, 0, (n - 3) // 2)
                tanh_z(act, 0)
                with act.Fori(0, H - 1) as h:
                    act_turn(act, h, h + 1)
                act_turn(act, H - 1, None)

            @block.vector
            def _(dve):
                dve.memset(tk[:], 0.0)
                dve.memset(pj[:, :, 0:3], 0.0).then_inc(cleared.sem, 1)
                select_G(dve, 0)
                for ct in range(3):
                    convolve(dve, 0, ct)
                    if ct:
                        silu_conv(dve, 0, ct - 1)
                save_cache(dve, 0)
                silu_conv(dve, 0, 2)
                with dve.Fori(0, H - 1) as h:
                    dve_turn(dve, h, h + 1)
                dve_turn(dve, H - 1, None)
                for i in range(2):
                    dve.wait_ge(*cacheT_psum.done(0, i))
                    dve.tensor_copy(cr[:, i, :], PS[i][0:72, 0:P]).then_inc(cacheT_copied.sem, 1)


def cacheT_of(M, h, ct):
    return M["cacheT"][:].rearrange("p (r c) -> p r c", r=3)[:, :, bass.ds(h + 8 * ct, 1)].rearrange("p r a -> p (r a)")


def new_cache_of(newc, i, h, ct):
    return newc[:, i, :].rearrange("p (r c) -> p r c", r=3)[:, :, bass.ds(h + 8 * ct, 1)].rearrange("p r a -> p (r a)")


def output(nc, M, IN, OUT, l):
    with Phase(nc, f"output{l}") as ph:
        sb, sig = ph.sb, ph.counter
        K = 16
        wo = sb("w_out", [P, K, D])
        y, yn = sb("y", [P, 2, D]), sb("squares", [P, D])
        gp, gate = sb("g_post_rows", [2, D]), sb("gate_rows", [P, 2, D])
        sel = sb("cond_select", [2, 2, P])
        ss, ms, rs = sb("ss", [P, T]), sb("ms", [P, T]), sb("rs", [P, T])
        loaded, gpl = [sig(f"w_out_loaded{i}", 64) for i in range(4)], sig("g_post_loaded", 32)
        sel_ready, gate_psum, gate_ready = sig("gates_scaled", 2), sig("gate_psum", 4), sig("gate_copied", 4)
        (y_psum, y_copied, squared, mean_ready, rstd_ready, y_norm, y_gated, x_ready) = (sig(n, T) for n in (
            "y_psum", "y_copied", "squared", "mean_ready", "rstd_ready", "y_norm", "y_gated", "x_ready"))
        stored = sig("x_stored", 16 * T)
        PS = M["ps"]
        with nc.Block() as block:

            @block.sync
            def _(sp):
                w = IN[("w_out_even", "w_out_odd")[l]][0].rearrange("(k p) n -> p k n", p=P)
                for i in range(2):
                    sp.dma_start(gp[i:i + 1, :], IN["g_post"][l:l + 1, :]).then_inc(gpl.sem, 16)
                for k in range(K):
                    sp.dma_start(wo[:, k, :], w[:, k, :]).then_inc(loaded[k // 4].sem, 16)
                if l == 1:
                    for t in range(T):
                        sp.wait_ge(*x_ready.done(0, t))
                        out = OUT["y_p"][0, cols(t), :] if t < PT else OUT["y_s"][0]
                        sp.dma_start(out, M["x"][0:rows(t), t, :]).then_inc(stored.sem, 16)
                    sp.wait_ge(*stored.done(0, 16 * T - 1))

            @block.gpsimd
            def _(pool):
                for t in range(T):
                    R = rows(t)
                    pool.wait_ge(*squared.done(0, t))
                    pool.tensor_scalar(ms[0:R, t:t + 1], ss[0:R, t:t + 1], 1.0 / D, EPS, ALU.mult, ALU.add).then_inc(mean_ready.sem, 1)
                    pool.wait_ge(*mean_ready.done(0, t))
                    pool.tensor_tensor(rs[0:R, t:t + 1], ms[0:R, t:t + 1], M.c("half", R), ALU.pow).then_inc(rstd_ready.sem, 1)

            @block.tensor
            def _(pe):
                pe.wait_ge(*sel_ready.done(0, 1))
                for m in range(2):
                    for half in range(2):
                        pe.matmul(PS[4 + 2 * m + half][:, :], sel[:, m, :], M["gate"][:, l, half * 512:(half + 1) * 512],
                                  start=True, stop=True).then_inc(gate_psum.sem, 1)
                for t in range(T):
                    R = rows(t)
                    if t >= 2:
                        pe.wait_ge(*y_copied.done(0, t - 2))
                    for half in range(2):
                        for k in range(K):
                            if t == 0 and half == 0 and k % 4 == 0:
                                pe.wait_ge(*loaded[k // 4].done(0, 63))
                            last = pe.matmul(PS[2 * (t % 2) + half][0:R, :], M["gT"][:, k, cols(t)], wo[:, k, half * 512:(half + 1) * 512],
                                             start=(k == 0), stop=(k == K - 1))
                    last.then_inc(y_psum.sem, 1)

            @block.scalar
            def _(act):
                for n in range(4):
                    act.wait_ge(*gate_psum.done(0, n))
                    act.activation(gate[:, n // 2, (n % 2) * 512:(n % 2 + 1) * 512], PS[4 + n][:, :], ACT.Copy).then_inc(gate_ready.sem, 1)
                for t in range(T):
                    R = rows(t)
                    act.wait_ge(*y_psum.done(0, t))
                    if t >= 2:
                        act.wait_ge(*x_ready.done(0, t - 2))
                    act.activation(y[0:R, t % 2, 0:512], PS[2 * (t % 2)][0:R, :], ACT.Copy)
                    act.activation(y[0:R, t % 2, 512:D], PS[2 * (t % 2) + 1][0:R, :], ACT.Copy).then_inc(y_copied.sem, 1)
                    act.wait_ge(*y_copied.done(0, t))
                    act.activation(yn[0:R, :], y[0:R, t % 2, :], ACT.Square, accum_out=ss[0:R, t:t + 1]).then_inc(squared.sem, 1)

            @block.vector
            def _(dve):
                dve.wait_ge(*gpl.done(0, 31))
                dve.tensor_tensor(M["gate"][:, l, :], M["gate"][:, l, :], gp[:], ALU.mult).then_inc(sel_ready.sem, 1)
                for m in range(2):
                    last = dve.tensor_scalar(sel[:, m, :], M.c("ones", 2), M.c("ident", 2)[:, m:m + 1], None, ALU.mult)
                last.then_inc(sel_ready.sem, 1)
                dve.wait_ge(*gate_ready.done(0, 3))
                for t in range(T):
                    R = rows(t)
                    yt = y[0:R, t % 2, :]
                    dve.wait_ge(*rstd_ready.done(0, t))
                    dve.scalar_tensor_tensor(yt, yt, rs[0:R, t:t + 1], gate[0:R, COND[t], :], ALU.mult, ALU.mult).then_inc(y_gated.sem, 1)
                    dve.wait_ge(*y_gated.done(0, t))
                    dve.tensor_tensor(M["x"][0:R, t, :], M["x"][0:R, t, :], yt, ALU.add).then_inc(x_ready.sem, 1)


class Memory(dict):

    def c(self, name, n=P, m=None):
        a, b = self.at[name]
        return self["const"][0:n, a:(b if m is None else a + m)]


def build(nc, IN, OUT, at):
    with ExitStack() as ctx:
        def sb(name, shape):
            return ctx.enter_context(nc.sbuf_tensor(name, shape, F32))

        M = Memory()
        M.at = at
        M.passed = ctx.enter_context(nc.semaphore("passed"))
        M.const_loaded = ctx.enter_context(nc.semaphore("const_loaded"))
        M["const"] = sb("const", [P, max(b for _, b in at.values())])
        M["x"] = sb("x", [P, T, D])
        M["hT"] = sb("hT", [P, KT, TOK])
        M["gT"] = sb("gT", [P, 16, TOK])
        M["vec"], M["conv"] = sb("vectors", [P, 68]), sb("conv_taps", [P, 96])
        M["modT"], M["gate"] = sb("modT", [P, 2, 16, 2]), sb("gate", [2, 2, D])
        M["ps"] = [ctx.enter_context(nc.psum_tensor(f"bank{i}", [P, 512], F32)) for i in range(8)]
        setup(nc, M, IN, OUT)
        with ExitStack() as layer:
            for name, shape in (("negM", [P, EVEN_H, TOK]), ("ucol", [P, T, EVEN_H]), ("mcols", [P, 4, T, EVEN_H])):
                M[name] = layer.enter_context(nc.sbuf_tensor(name, shape, F32))
            even_gates(nc, M, IN, OUT)
            heads(nc, M, IN, OUT, "A")
            heads(nc, M, IN, OUT, "B")
        output(nc, M, IN, OUT, 0)
        with ExitStack() as layer:
            for name, shape in (("a1T", [RANK, TOK]), ("grow", [GDN_H, 2, TOK]), ("Gcol", [P, T, GDN_H]), ("gcols", [P, 5, T, GDN_H]),
                                ("cacheT", [P, 72])):
                M[name] = layer.enter_context(nc.sbuf_tensor(name, shape, F32))
            odd_gates(nc, M, IN, OUT)
            heads(nc, M, IN, OUT, "C")
            gdn_heads(nc, M, IN, OUT)
        output(nc, M, IN, OUT, 1)


_OUTS = [("y_p", (1, SEQ, D)), ("y_s", (1, DEC, D))] + [
    (side + n, (1, 1) + shape) for side in "ps" for n, shape in (
        ("C", (4, 256, 256)), ("n", (4, 256)), ("m", (4,)), ("ret", (4, 256, 256)), ("gla", (4, 128, 256)),
        ("gdn", (8, 128, 128)), ("conv", (3, 3072)))]
_INS = ["x_prompt", "x_sample", "c_prompt", "c_sample", "state_mlstm_C", "state_mlstm_n", "state_mlstm_m", "state_ret",
        "state_gla", "state_gdn", "cache_gdn_conv", "w_ada", "b_ada", "g_pre", "g_post", "w_in_even", "b_if_even",
        "g_head_even", "w_out_even", "w_in_odd", "w_a2", "b_a2", "conv_w", "a_log", "dt_bias", "g_head_odd", "w_out_odd"]


def kernel(**inputs):
    import concourse.bacc as bacc
    from concourse.bass_utils import run_bass_kernel_spmd

    nc = bacc.Bacc("TRN2", target_bir_lowering=False, num_devices=1)
    const, at = shape_constants()
    arrays, IN, OUT = {"in_const": const}, {}, {}
    for name in _INS:
        arrays["in_" + name] = np.ascontiguousarray(inputs[name])
    for name, a in arrays.items():
        IN[name[3:]] = nc.dram_tensor(name, a.shape, F32, kind="ExternalInput").ap()
    for name, shape in _OUTS:
        OUT[name] = nc.dram_tensor("out_" + name, shape, F32, kind="ExternalOutput").ap()
    build(nc, IN, OUT, at)
    r = run_bass_kernel_spmd(nc, [arrays], core_ids=[0])
    return tuple(r.results[0]["out_" + name] for name, _ in _OUTS)
```

```python
from contextlib import ExitStack

import numpy as np

import concourse.bass as bass
from concourse import mybir

F32 = mybir.dt.float32
F32R = mybir.dt.float32r
U32 = mybir.dt.uint32
ACT = mybir.ActivationFunctionType
ALU = mybir.AluOpType
AX = mybir.AxisListType

P = 128
D = 1024
KT = D // P
SEQ, DEC = 512, 64
TOK = SEQ + DEC
HALF = TOK // 2
PT = SEQ // P
T = PT + 1
EPS = 1e-6
NEG = -1e30
EVEN_H, GLA_H, GDN_H = 4, 4, 8
RANK = 16
LEVELS = (1, 2, 4, 8, 16, 32, 64)
COND = [0] * PT + [1]


def rows(t):
    return P if t < PT else DEC


def cols(t):
    return slice(t * P, t * P + rows(t))


def shape_constants():
    s, t = np.arange(P)[:, None], np.arange(P)[None, :]
    lg = np.log(1.0 - 2.0 ** (-5.0 - np.arange(EVEN_H)))
    parts = {
        "ident": np.eye(P),
        "ones": np.ones((P, P)),
        "mask": (s <= t) * 1.0,
        "neg_causal": np.where(s <= t, 0.0, NEG),
        "neg_strict": np.where(s < t, 0.0, NEG),
        "half": np.full((P, 1), -0.5),
        "levels": np.concatenate([((s // (2 * n) == t // (2 * n)) & (s % (2 * n) < n) & (t % (2 * n) >= n)) * 1.0
                                  for n in LEVELS], axis=1),
        "decay": np.concatenate([np.where(s <= t, np.exp(np.maximum(t - s, 0) * g), 0.0) for g in lg], axis=1),
        "q_decay": np.exp((s + 1.0) * lg[None, :]),
        "k_decay": np.concatenate([np.exp((P - 1.0 - s) * lg), np.exp(np.maximum(DEC - 1.0 - s, 0) * lg)], axis=1),
        "s_decay": np.broadcast_to(np.concatenate([np.exp(P * lg), np.exp(DEC * lg)])[None, :], (P, 2 * EVEN_H)),
    }
    for n, name in ((EVEN_H, "diag4"), (GDN_H, "diag8")):
        parts[name] = np.broadcast_to(np.eye(P, n)[:, None, :], (P, T, n)).reshape(P, T * n)
    inv = 10000.0 ** (-np.arange(P, dtype=np.float64) / P)
    pos = np.concatenate([np.arange(SEQ), 512 + np.arange(DEC)])
    parts["cos"], parts["sin"] = np.cos(inv[:, None] * pos), np.sin(inv[:, None] * pos)
    where, at = {}, 0
    for name, a in parts.items():
        where[name] = (at, at + a.shape[1])
        at += a.shape[1]
    return np.concatenate(list(parts.values()), axis=1).astype(np.float32), where


class Signal:

    def __init__(self, sem, per, first):
        self.sem, self.per, self.first = sem, per, first

    def done(self, turn, k):
        return self.sem, turn * self.per + (self.first + k + 1)

    def before(self, turn, k):
        return self.sem, turn * self.per + (self.first + k)


class Link:

    def __init__(self, eng, step, turn=0):
        self.eng, self.step, self.turn, self.k = eng, step, turn, 0

    def __call__(self, ins, n=1):
        ins.then_inc(self.step.sem, 1)
        self.eng.wait_ge(*self.step.done(self.turn, self.k))
        self.k += 1

    def close(self):
        assert self.k == self.step.per, (self.k, self.step.per)


class Phase:

    def __init__(self, nc, name, first=0):
        self.nc, self.name, self.first, self.ctx, self.counters = nc, name, first, ExitStack(), []

    def __enter__(self):
        return self

    def __exit__(self, *exc):
        if exc[0] is None:
            self.nc.clear_and_free_semaphores([s.sem for s in self.counters])
            self.nc.all_engine_barrier()
        self.ctx.close()
        return False

    def sb(self, name, shape, dt=F32):
        return self.ctx.enter_context(self.nc.sbuf_tensor(f"{self.name}_{name}", shape, dt))

    def counter(self, name, per=1, lead=1):
        first = self.first * lead
        s = Signal(self.nc.alloc_semaphore(f"{self.name}_{name}"), per, first)
        if first:
            engines = (self.nc.sync, self.nc.gpsimd, self.nc.scalar, self.nc.vector, self.nc.tensor)
            engines[len(self.counters) % 5].sem_inc(s.sem, first)
        self.counters.append(s)
        return s


def matmul_chain(pe, out, pairs):
    for n, (a, b) in enumerate(pairs):
        last = pe.matmul(out, a, b, start=(n == 0), stop=(n == len(pairs) - 1))
    return last


def split_matmul(pe, out, w, x, first, last):
    pe.matmul(out, w[0], x[1], start=first, stop=False)
    pe.matmul(out, w[1], x[0], start=False, stop=False)
    return pe.matmul(out, w[0], x[0], start=False, stop=last)


def setup(nc, M, IN, OUT):
    with Phase(nc, "setup") as ph:
        vec = ph.sb("vec_rows", [P, P])
        conv_rows = ph.sb("conv_rows", [P, P])
        tc = ph.sb("tanh_c", [P, 16])
        cs = ph.sb("silu_c", [P, KT, 2])
        wada = ph.sb("w_ada", [P, 2, 3 * D])
        bada = ph.sb("b_ada", [2, 2, 3 * D])
        mod = ph.sb("mod_rows", [2, 2, 2 * D])
        loaded = ph.counter("small_loaded", 16 * 11)
        ada_loaded = [ph.counter(f"ada_loaded{i}", 16 * KT) for i in range(2)]
        bada_loaded = ph.counter("b_ada_loaded", 64)
        x_loaded = ph.counter("x_loaded", 32)
        vec_psum = ph.counter("vec_psum")
        vec_copied = ph.counter("vec_copied", 2)
        tanh_done = ph.counter("tanh_done")
        cs_half = ph.counter("silu_c_half")
        cs_ready = ph.counter("silu_c_ready")
        ada_used = ph.counter("ada_used", 2 * KT)
        mod_ready = ph.counter("mod_ready", 2 * 6)
        modT_psum = ph.counter("modT_psum", 2)
        modT_copied = ph.counter("modT_copied", 2)
        scaled = ph.counter("scaled", 4)
        gh_scaled = ph.counter("g_head_scaled", 4)
        PS = M["ps"]
        with nc.Block() as block:

            @block.sync
            def _(sp):
                sp.dma_start(M["const"][:], IN["const"]).then_inc(M.const_loaded, 16)
                rowsof = [(IN["c_prompt"][0], 0, 8), (IN["c_sample"][0], 8, 8),
                          (IN["g_pre"][0], 16, 8), (IN["g_pre"][1], 24, 8),
                          (IN["g_head_even"][0], 32, 16), (IN["g_head_odd"][0], 48, 16), (IN["b_a2"][0], 64, 4)]
                for src, at, n in rowsof:
                    sp.dma_start(vec[at:at + n, :], src.rearrange("(r c) -> r c", c=P)).then_inc(loaded.sem, 16)
                for j in range(4):
                    sp.dma_start(conv_rows[24 * j:24 * j + 24, :],
                                 IN["conv_w"][0, j].rearrange("(r c) -> r c", c=P)).then_inc(loaded.sem, 16)
                for l in range(2):
                    for k in range(KT):
                        i = l * KT + k
                        if i >= 2:
                            sp.wait_ge(*ada_used.done(0, i - 2))
                        sp.dma_start(wada[:, i % 2, :], IN["w_ada"][l, k * P:(k + 1) * P, :]).then_inc(
                            ada_loaded[i % 2].sem, 16)
                        if i == 0:
                            for m in range(2):
                                sp.dma_start(bada[m:m + 1, :, :], IN["b_ada"].rearrange("(a l) n -> a l n", a=1)
                                             ).then_inc(bada_loaded.sem, 32)
                sp.dma_start(M["x"][:, 0:PT, :], IN["x_prompt"][0].rearrange("(t p) d -> p t d", p=P)).then_inc(x_loaded.sem, 16)
                sp.dma_start(M["x"][0:DEC, PT, :], IN["x_sample"][0]).then_inc(x_loaded.sem, 16)
                sp.wait_ge(*x_loaded.done(0, 31))

            @block.tensor
            def _(pe):
                pe.wait_ge(*loaded.done(0, 16 * 11 - 1))
                pe.wait_ge(M.const_loaded, 16)
                pe.transpose(PS[7][:, 0:68], vec[0:68, :], M.c("ident", 68, 68))
                pe.transpose(PS[7][:, 128:224], conv_rows[0:96, :], M.c("ident", 96, 96)).then_inc(vec_psum.sem, 1)
                pe.wait_ge(*cs_ready.done(0, 0))
                for l in range(2):
                    for k in range(KT):
                        i = l * KT + k
                        pe.wait_ge(*ada_loaded[i % 2].done(0, 16 * (i // 2) + 15))
                        if l and k == 0:
                            pe.wait_ge(*mod_ready.done(0, 5))
                        for n in range(6):
                            last = pe.matmul(PS[n][0:2, :], cs[:, k, :], wada[:, i % 2, n * 512:(n + 1) * 512],
                                             start=(k == 0), stop=(k == KT - 1))
                        last.then_inc(ada_used.sem, 1)
                    pe.wait_ge(*mod_ready.done(0, 6 * l + 5))
                    if l:
                        pe.wait_ge(*modT_copied.done(0, 0))
                    for c in range(16):
                        last = pe.transpose(PS[6][:, 2 * c:2 * c + 2], mod[0:2, l, c * P:(c + 1) * P], M.c("ident", 2, 2))
                    last.then_inc(modT_psum.sem, 1)

            @block.scalar
            def _(act):
                act.wait_ge(*vec_copied.done(0, 1))
                act.activation(tc[:], M["vec"][:, 0:16], ACT.Tanh, scale=0.5).then_inc(tanh_done.sem, 1)

            @block.vector
            def _(dve):
                dve.wait_ge(*vec_psum.done(0, 0))
                dve.tensor_copy(M["vec"][:], PS[7][:, 0:68]).then_inc(vec_copied.sem, 1)
                dve.tensor_copy(M["conv"][:], PS[7][:, 128:224]).then_inc(vec_copied.sem, 1)
                dve.wait_ge(*tanh_done.done(0, 0))
                dve.scalar_tensor_tensor(tc[:], tc[:], 1.0, M["vec"][:, 0:16], ALU.add, ALU.mult).then_inc(cs_half.sem, 1)
                dve.wait_ge(*cs_half.done(0, 0))
                dve.tensor_scalar(cs[:].rearrange("p k m -> p m k"), tc[:].rearrange("p (m k) -> p m k", m=2), 0.5, None,
                                  ALU.mult).then_inc(cs_ready.sem, 1)
                for a, b, f in ((32, 40, 0.25), (40, 48, 0.5), (48, 64, 0.5)):
                    dve.tensor_scalar(M["vec"][:, a:b], M["vec"][:, a:b], f, None, ALU.mult).then_inc(gh_scaled.sem, 1)
                dve.memset(M["x"][DEC:P, PT, :], 0.0).then_inc(gh_scaled.sem, 1)
                dve.wait_ge(*bada_loaded.done(0, 63))
                for l in range(2):
                    dve.wait_ge(*ada_used.done(0, l * KT + KT - 1))
                    for n in range(6):
                        out = mod[:, l, n * 512:(n + 1) * 512] if n < 4 else M["gate"][:, l, (n - 4) * 512:(n - 3) * 512]
                        dve.tensor_tensor(out, PS[n][0:2, :], bada[:, l, n * 512:(n + 1) * 512], ALU.add).then_inc(
                            mod_ready.sem, 1)
                    dve.wait_ge(*modT_psum.done(0, l))
                    dve.tensor_copy(M["modT"][:, l, :, :], PS[6][:, 0:32].rearrange("p (c m) -> p c m", m=2)).then_inc(
                        modT_copied.sem, 1)
                    dve.wait_ge(*modT_copied.done(0, l))
                    for m in range(2):
                        dve.scalar_tensor_tensor(M["modT"][:, l, KT:2 * KT, m], M["modT"][:, l, KT:2 * KT, m], 1.0,
                                                 M["vec"][:, 16 + 8 * l:24 + 8 * l], ALU.add, ALU.mult).then_inc(scaled.sem, 1)


def norm_steps(ph, M, l):
    S = {n: ph.counter(n, k) for n, k in (("sq", T), ("mean", T), ("rstd", T), ("xn", T), ("xT_psum", 2 * T),
                                         ("hT_act", T), ("hT_dve", T))}
    PS = M["ps"]
    sqj = ph.sb("squares", [P, D])
    ss, ms, rs = ph.sb("ss", [P, T]), ph.sb("ms", [P, T]), ph.sb("rs", [P, T])
    xn = ph.sb("xn", [P, 2, D])

    def act_steps(act):
        for t in range(T):
            if t:
                act.wait_ge(*S["sq"].done(0, t - 1))
            act.activation(sqj[0:rows(t), :], M["x"][0:rows(t), t, :], ACT.Square, accum_out=ss[0:rows(t), t:t + 1]
                           ).then_inc(S["sq"].sem, 1)
        for t in range(T):
            act.wait_ge(*S["xT_psum"].done(0, 2 * t))
            for k in range(4):
                last = act.activation(M["hT"][:, k, cols(t)], PS[2 * (t % 2)][:, k * P:k * P + rows(t)], ACT.Identity,
                                      bias=M["modT"][:, l, k, COND[t]:COND[t] + 1],
                                      scale=M["modT"][:, l, KT + k, COND[t]:COND[t] + 1])
            last.then_inc(S["hT_act"].sem, 1)

    def pool_steps(pool):
        for t in range(T):
            R = rows(t)
            pool.wait_ge(*S["sq"].done(0, t))
            pool.tensor_scalar(ms[0:R, t:t + 1], ss[0:R, t:t + 1], 1.0 / D, EPS, ALU.mult, ALU.add).then_inc(S["mean"].sem, 1)
            pool.wait_ge(*S["mean"].done(0, t))
            pool.tensor_tensor(rs[0:R, t:t + 1], ms[0:R, t:t + 1], M.c("half", R), ALU.pow).then_inc(S["rstd"].sem, 1)

    def dve_steps(dve):
        def scale(t):
            R = rows(t)
            dve.wait_ge(*S["rstd"].done(0, t))
            if t >= 2:
                dve.wait_ge(*S["xT_psum"].done(0, 2 * (t - 2) + 1))
            dve.tensor_scalar(xn[0:R, t % 2, :], M["x"][0:R, t, :], rs[0:R, t:t + 1], None, ALU.mult).then_inc(S["xn"].sem, 1)
        scale(0)
        for t in range(T):
            if t + 1 < T:
                scale(t + 1)
            dve.wait_ge(*S["xT_psum"].done(0, 2 * t + 1))
            for k in range(4, KT):
                last = dve.tensor_scalar(M["hT"][:, k, cols(t)], PS[2 * (t % 2) + 1][:, (k - 4) * P:(k - 4) * P + rows(t)],
                                         M["modT"][:, l, KT + k, COND[t]:COND[t] + 1],
                                         M["modT"][:, l, k, COND[t]:COND[t] + 1], ALU.mult, ALU.add)
            last.then_inc(S["hT_dve"].sem, 1)

    def pe_steps(pe):
        for t in range(T):
            R = rows(t)
            pe.wait_ge(*S["xn"].done(0, t))
            for half in range(2):
                if t >= 2:
                    pe.wait_ge(*S[("hT_act", "hT_dve")[half]].done(0, t - 2))
                for k in range(4):
                    kk = 4 * half + k
                    last = pe.transpose(PS[2 * (t % 2) + half][:, k * P:k * P + R], xn[0:R, t % 2, kk * P:(kk + 1) * P],
                                        M.c("ident", R, R))
                last.then_inc(S["xT_psum"].sem, 1)
        pe.wait_ge(*S["hT_act"].done(0, T - 1))
        pe.wait_ge(*S["hT_dve"].done(0, T - 1))

    return act_steps, pool_steps, dve_steps, pe_steps, S


class SplitInput:

    def __init__(self, ph, M):
        self.M, self.high_ready, self.low_ready = M, ph.counter("hT_high", KT), ph.counter("hT_low", KT)

    def act_steps(self, act, S):
        act.wait_ge(*S["hT_act"].done(0, T - 1))
        act.wait_ge(*S["hT_dve"].done(0, T - 1))
        for k in range(KT):
            act.activation(self.M["hT_high"][:, k, :], self.M["hT"][:, k, :], ACT.Copy).then_inc(self.high_ready.sem, 1)

    def dve_steps(self, dve):
        for k in range(KT):
            dve.wait_ge(*self.high_ready.done(0, k))
            dve.tensor_tensor(self.M["hT_low"][:, k, :], self.M["hT"][:, k, :], self.M["hT_high"][:, k, :].bitcast(F32),
                              ALU.subtract).then_inc(self.low_ready.sem, 1)


def small_projection(pe, M, w, c0, n, banks):
    for half in range(2):
        last = matmul_chain(pe, M["ps"][banks[half]][0:n, 0:HALF],
                            [(w[:, k, c0:c0 + n], M["hT"][:, k, half * HALF:(half + 1) * HALF]) for k in range(KT)])
    return last


def log_sigmoid(act, dve, x, a, b, out, S, turn=0):
    if dve is not None:
        dve.scalar_tensor_tensor(a, x, -1.0, x, ALU.mult, ALU.max).then_inc(S["abs"].sem, 1)
        dve.wait_ge(*S["exp"].done(turn, 0))
        dve.tensor_scalar(b, b, 1.0, None, ALU.add).then_inc(S["plus"].sem, 1)
        dve.wait_ge(*S["log"].done(turn, 0))
        return dve.scalar_tensor_tensor(out, x, 0.0, a, ALU.min, ALU.subtract)
    act.wait_ge(*S["abs"].done(turn, 0))
    act.activation(b, a, ACT.Exp, scale=-1.0).then_inc(S["exp"].sem, 1)
    act.wait_ge(*S["plus"].done(turn, 0))
    act.activation(a, b, ACT.Ln).then_inc(S["log"].sem, 1)


FIRST_TILES = {"mlstm": ("w_in_even", (0, P)), "retention": ("w_in_even", (4 * D, 4 * D + P)), "gla": ("w_in_odd", (0, 512)),
               "gdn": ("w_in_odd", tuple(2 * D + RANK + i * D for i in range(3)) + (6 * D + RANK + 2 * GDN_H,)),
               "output0": ("w_out_even", (0,)), "output1": ("w_out_odd", (0,))}


class FirstLoads:

    def __init__(self, ph, M, IN, phase):
        name, self.at = FIRST_TILES[phase]
        self.w = IN[name][0].rearrange("(k p) n -> p k n", p=P)
        k = self.w.shape[1]
        self.place = M["x"][:].rearrange("p t d -> p (t d)")[:, 0:len(self.at) * k * P].rearrange("p (a k c) -> p a k c", a=len(self.at), k=k)
        self.loaded = ph.counter("first_loaded", 16 * len(self.at))

    def start(self, sp):
        for i in range(len(self.at)):
            sp.dma_start(self.place[:, i], self.w[:, :, self.at[i]:self.at[i] + P]).then_inc(self.loaded.sem, 16)

    def finish(self, sp):
        sp.wait_ge(*self.loaded.done(0, 16 * len(self.at) - 1))


def even_gates(nc, M, IN, OUT):
    with Phase(nc, "even_gates") as ph:
        M["hT"] = ph.sb("hT", [P, KT, TOK])
        act_norm, pool_norm, dve_norm, pe_norm, norm_signals = norm_steps(ph, M, 0)
        split = SplitInput(ph, M)
        first = FirstLoads(ph, M, IN, "mlstm")
        H = EVEN_H
        sb, sig = ph.sb, ph.counter
        wg = sb("w_gates", [P, KT, 64])
        bif = sb("b_if", [H, 2])
        mprev = sb("m_prev", [H, T + 2])
        gi, gf, ta, tb, lf = (sb(n, [H, TOK]) for n in ("gate_i", "gate_f", "ls_a", "ls_b", "log_f"))
        b, u, Mx, m = (sb(n, [H, TOK]) for n in ("cum_f", "u_rows", "M_rows", "m_rows"))
        mp_rows, me_rows = sb("mp_rows", [H, T, H]), sb("me_rows", [H, T, H])
        msel = sb("M_selected", [H, H, TOK])
        col = sb("gate_cols", [P, 3, T, H])
        bro = sb("gate_broadcast", [P, 2, T, H])
        arg = sb("gate_args", [P, 4, T, H])
        wl = sig("w_gates_loaded", 16 * 6)
        proj, copied = sig("gates_psum", 2), sig("gates_copied", 4)
        S = {n: sig("ls_" + n) for n in ("abs", "exp", "plus", "log")}
        lk = sig("vector_step")
        rows_ready, colsp, bp, bcopied = sig("rows_ready"), sig("cols_psum"), sig("M_psum", 2 * H), sig("M_copied", 2 * H)
        args_ready, exps = sig("args_ready"), sig("gate_exps")
        cleared = sig("cols_cleared")
        m_stored = sig("m_stored", 32)
        PS = M["ps"]
        with nc.Block() as block:

            @block.sync
            def _(sp):
                sp.wait_ge(*cleared.done(0, 0))
                for i in range(2):
                    sp.dma_start(wg[:, :, 32 * i:32 * i + H], IN["w_in_even"][0, :, 9 * D + i * H:9 * D + (i + 1) * H].rearrange(
                        "(k p) n -> p k n", p=P)).then_inc(wl.sem, 16)
                for i in range(2):
                    sp.dma_start(bif[:, i:i + 1], IN["b_if_even"][0, i * H:(i + 1) * H].rearrange("(h a) -> h a", a=1)).then_inc(wl.sem, 16)
                sp.dma_start(mprev[:, PT:PT + 1], IN["state_mlstm_m"][0, 0].rearrange("(h a) -> h a", a=1)).then_inc(wl.sem, 32)
                sp.wait_ge(*norm_signals["xn"].done(0, T - 1))
                first.start(sp)
                sp.wait_ge(*rows_ready.done(0, 0))
                sp.dma_start(OUT["pm"][0, 0].rearrange("(h a) -> h a", a=1), mprev[:, T:T + 1]).then_inc(m_stored.sem, 16)
                sp.dma_start(OUT["sm"][0, 0].rearrange("(h a) -> h a", a=1), mprev[:, T + 1:T + 2]).then_inc(m_stored.sem, 16)
                sp.wait_ge(*m_stored.done(0, 31))
                first.finish(sp)

            @block.gpsimd
            def _(pool):
                pool_norm(pool)

            @block.tensor
            def _(pe):
                pe_norm(pe)
                pe.wait_ge(*wl.done(0, 95))
                small_projection(pe, M, wg, 0, 32 + H, (4, 5)).then_inc(proj.sem, 1)
                pe.wait_ge(*rows_ready.done(0, 0))
                for n, r in enumerate((u, Mx, m)):
                    for t in range(T):
                        at = (n * T + t) * H
                        pe.transpose(PS[0][0:rows(t), at:at + H], r[:, cols(t)], M.c("ident", H, H))
                for n, r in enumerate((mp_rows, me_rows)):
                    last = pe.matmul(PS[1][:, n * T * H:(n + 1) * T * H], M.c("ones", H), r[:].rearrange("p t h -> p (t h)"),
                                     start=True, stop=True)
                last.then_inc(colsp.sem, 1)
                for h in range(H):
                    for half in range(2):
                        n = 2 * h + half
                        if n >= 2:
                            pe.wait_ge(*bcopied.done(0, n - 2))
                        pe.matmul(PS[2 + half][:, 0:HALF], M.c("ones", H), msel[:, h, half * HALF:(half + 1) * HALF],
                                  start=True, stop=True).then_inc(bp.sem, 1)

            @block.scalar
            def _(act):
                act_norm(act)
                split.act_steps(act, norm_signals)
                for i, g in enumerate((gi, gf)):
                    act.wait_ge(*proj.done(0, 0))
                    for half in range(2):
                        act.activation(g[:, half * HALF:(half + 1) * HALF], PS[4 + half][32 * i:32 * i + H, 0:HALF], ACT.Identity,
                                       bias=bif[:, i:i + 1]).then_inc(copied.sem, 1)
                log_sigmoid(act, None, gf[:], ta[:], tb[:], lf[:], S)
                act.wait_ge(*args_ready.done(0, 0))
                act.activation(M["mcols"][:], arg[:], ACT.Exp).then_inc(exps.sem, 1)
                for n in range(2 * H):
                    act.wait_ge(*bp.done(0, n))
                    act.activation(M["negM"][:, n // 2, (n % 2) * HALF:(n % 2 + 1) * HALF], PS[2 + n % 2][:, 0:HALF],
                                   ACT.Copy).then_inc(bcopied.sem, 1)

            @block.vector
            def _(dve):
                link = Link(dve, lk)
                dve.memset(wg[:], 0.0).then_inc(cleared.sem, 1)
                dve.memset(mprev[:, 0:1], 0.0)
                dve.memset(col[:], 0.0)
                dve_norm(dve)
                split.dve_steps(dve)
                dve.wait_ge(*copied.done(0, 3))
                link(log_sigmoid(None, dve, gf[:], ta[:], tb[:], lf[:], S))
                for t in range(T):
                    last = dve.tensor_tensor_scan(b[:, cols(t)], M.c("ones", H, rows(t)), lf[:, cols(t)], 0.0, ALU.mult, ALU.add)
                link(last)
                link(dve.tensor_tensor(u[:], gi[:], b[:], ALU.subtract))
                dve.wait_ge(*wl.done(0, 95))
                for t in range(T):
                    end = t * P + rows(t) - 1
                    link(dve.tensor_tensor_scan(Mx[:, cols(t)], u[:, cols(t)], u[:, cols(t)], mprev[:, t:t + 1], ALU.max, ALU.max))
                    to = t + 1 if t < PT - 1 else (T if t == PT - 1 else T + 1)
                    link(dve.tensor_tensor(mprev[:, to:to + 1], b[:, end:end + 1], Mx[:, end:end + 1], ALU.add))
                dve.tensor_tensor(m[:], b[:], Mx[:], ALU.add)
                for h in range(H):
                    dve.tensor_scalar(msel[:, h, :], Mx[:], M.c("diag4", H)[:, h:h + 1], -1.0, ALU.mult, ALU.mult)
                for t in range(T):
                    end = t * P + rows(t) - 1
                    dve.tensor_scalar(mp_rows[:, t, :], M.c("diag4", H)[:, 0:H], mprev[:, t:t + 1], None, ALU.mult)
                    last = dve.tensor_scalar(me_rows[:, t, :], M.c("diag4", H)[:, 0:H], Mx[:, end:end + 1], None, ALU.mult)
                last.then_inc(rows_ready.sem, 1)
                dve.wait_ge(*colsp.done(0, 0))
                src = PS[0][:, 0:3 * T * H].rearrange("p (n t h) -> p n t h", n=3, t=T)
                dve.tensor_copy(col[:, :, 0:PT, :], src[:, :, 0:PT, :])
                dve.tensor_copy(col[0:DEC, :, PT, :], src[0:DEC, :, PT, :])
                link(dve.tensor_copy(bro[:].rearrange("p n t h -> p (n t h)"), PS[1][:, 0:2 * T * H]))
                dve.tensor_copy(M["ucol"][:], col[:, 0])
                dve.tensor_tensor(arg[:, 0], bro[:, 0], col[:, 1], ALU.subtract)
                dve.tensor_tensor(arg[:, 1], col[:, 0], bro[:, 1], ALU.subtract)
                dve.tensor_tensor(arg[:, 2], bro[:, 0], bro[:, 1], ALU.subtract)
                dve.tensor_scalar(arg[:, 3], col[:, 2], -1.0, None, ALU.mult).then_inc(args_ready.sem, 1)


def heads(nc, M, IN, OUT, kind):
    H, DV = 4, 256
    DT = {"A": 2, "B": 2, "C": 1}[kind]
    NV = DV + 1 if kind == "A" else DV
    NG = 2 * DV if kind == "A" else DV
    CT = 2 * DT
    NA = 2 if kind == "C" else 0
    NP = NA + 2 * CT
    w_in = IN["w_in_odd" if kind == "C" else "w_in_even"][0].rearrange("(k p) n -> p k n", p=P)
    q0, k0, v0 = {"A": (0, D, 2 * D), "B": (4 * D, 5 * D, 6 * D), "C": (0, 512, D)}[kind]
    gates0 = {"A": [3 * D, 7 * D], "B": [8 * D], "C": [5 * D + 32]}[kind]
    S_in = IN[{"A": "state_mlstm_C", "B": "state_ret", "C": "state_gla"}[kind]][0, 0]
    pS = OUT[{"A": "pC", "B": "pret", "C": "pgla"}[kind]][0, 0]
    sS = OUT[{"A": "sC", "B": "sret", "C": "sgla"}[kind]][0, 0]
    g_col = {"A": 32, "B": 40, "C": 48}[kind]
    g_row = {"A": 0, "B": 8, "C": 0}[kind]
    ms_scale = 1.0 / (4 * DV) if kind == "A" else 1.0 / DV
    QS = (P if kind == "C" else DV) ** -0.5
    PS = M["ps"]
    with Phase(nc, {"A": "mlstm", "B": "retention", "C": "gla"}[kind], first=1) as ph:
        sb, sig = ph.sb, ph.counter
        place = M["x"][:].rearrange("p t d -> p (t d)")
        rqk, rv = (place[:, i * 2 * D:(i + 1) * 2 * D].rearrange("p (a k c) -> p a k c", a=2, k=KT) for i in range(2))
        qkh, qkl = (sb(n, [P, 2, KT, P], F32R) for n in ("w_qk_high", "w_qk_low"))
        vh, vl = (sb(n, [P, KT, NG + DV], F32R) for n in ("w_v_high", "w_v_low"))
        qk = sb("qkT", [P, CT, TOK]) if kind == "B" else M["gT"][:, 8:8 + CT, :]
        v = sb("v", [P, NV])
        th = sb("tanh", [P, NG])
        zs = sb("z_silu", [P, DV])
        sT = sb("scores", [P, P])
        kw = sb("k_weighted", [P, DT * P])
        num_a, num, hg, g = sb("intra", [P, NV]), sb("num", [P, NV]), sb("h_gated", [P, DV]), sb("g", [P, DV])
        sq = sb("squares", [P, DV])
        sm = sb("small", [P, 8])
        St = [sb("state_prompt", [P, DT, NV]), sb("state_sample", [P, DT, NV])]
        if kind == "A":
            E, arg = sb("E", [P, P]), sb("E_arg", [P, P])
            logit_ready, decay_ready = sig("logit_ready", T), sig("decay_ready", T)
        if kind in "BC":
            raw = sb("qkT_raw", [P, CT, TOK]) if kind == "B" else M["gT"][:, 12:12 + CT, :]
        if kind == "B":
            ra, rb = sb("rope_a", [P, TOK]), sb("rope_b", [P, TOK])
        if kind == "C":
            wa = sb("w_a2", [RANK, P])
            la, lb, lc, bT = (sb(n, [P, TOK]) for n in ("ls_x", "ls_a", "ls_b", "cum_a"))
            ends = sb("block_ends", [P, 3, T])
            eend = sb("block_exps", [P, 3, T])
            Sc = sb("state_scaled", [P, DV])
            nS = sb("state_new", [P, DV])
            wal = sig("w_a2_loaded", 16)
            Lg = {n: sig("ls_" + n) for n in ("abs", "exp", "plus", "log")}
            shifted, exps, b_ready = sig("b_shifted"), sig("b_exps", 3), sig("b_ready")
            sc_ready, nS_ready = sig("state_scaled_ready", PT), sig("state_new_ready", T)
        first = FirstLoads(ph, M, IN, {"A": "retention", "B": "output0", "C": "gdn"}[kind])
        NC = (NG + DV) // P
        after = {"A": (0, 2, 2, 4, 4, 6), "B": (0, 2, 4, 6), "C": (1, 2, 3, 4)}[kind]
        wql = [sig(f"w_qk_loaded{i}", 16 * CT // 2) for i in range(2)]
        wvl = [sig(f"w_v_loaded{i}", 16 * NC // 2) for i in range(2)]
        qk_high, qk_low, v_high, v_low = sig("w_qk_split_high", CT), sig("w_qk_split_low", CT), sig("w_v_split_high", NC), sig("w_v_split_low", NC)
        sl = sig("state_loaded", 32 if kind == "A" else 16)
        p_st, s_st = sig("prompt_state_stored", 32 if kind == "A" else 16), sig("sample_state_stored", 32 if kind == "A" else 16)
        qk_psum, qk_copied, qk_ready = sig("qk_psum", NP, lead=NP), sig("qk_copied", NP), sig("qk_ready")
        filled = sig("filled")
        (gates_psum, tanh_done, gates_used, v_psum, v_copied, scores_psum, scores_ready, kw_ready,
         nums_psum, intra_copied, state_psum, state_ready, squared, mean_ready, rstd_ready, g_ready, gT_psum,
         gT_copied) = (sig(n, T) for n in (
             "gates_psum", "tanh_done", "gates_used", "v_psum", "v_copied", "scores_psum",
             "scores_ready", "kw_ready", "nums_psum", "intra_copied", "state_psum", "state_ready", "squared",
             "mean_ready", "rstd_ready", "g_ready", "gT_psum", "gT_copied"))
        num_ready = sig("num_ready", PT)
        if kind == "A":
            den, hg_ready = sig("den_step", 4 * T), sig("h_gated_ready", T)
        NL = {"A": 0, "B": 11, "C": 5}[kind]
        lk = sig("vector_step", NL)

        def q_side(t):
            return slice(0, DT), cols(t)

        def qk_slot_free(eng, h, ct):
            if ct >= 2:
                eng.wait_ge(*qk_psum.done(h, NA + 2 * (ct - 2) + 1))
            else:
                eng.wait_ge(*qk_psum.done(h - 1, NA + 2 * (CT - 2 + ct) + 1))

        def high_qk(act, h, ct):
            if h is None:
                return
            act.wait_ge(*wql[ct % 2].done(h, 16 * (ct // 2) + 15))
            qk_slot_free(act, h, ct)
            act.activation(qkh[:, ct % 2], rqk[:, ct % 2], ACT.Copy).then_inc(qk_high.sem, 1)

        def low_qk(dve, h, ct):
            if h is None:
                return
            dve.wait_ge(*qk_high.done(h, ct))
            qk_slot_free(dve, h, ct)
            dve.tensor_tensor(qkl[:, ct % 2], rqk[:, ct % 2], qkh[:, ct % 2].bitcast(F32), ALU.subtract).then_inc(qk_low.sem, 1)

        def high_v(act, h, c):
            if c < 2:
                act.wait_ge(*v_psum.before(h, 0))
            act.wait_ge(*wvl[c % 2].done(h, 16 * (c // 2) + 15))
            act.activation(vh[:, :, c * P:(c + 1) * P], rv[:, c % 2], ACT.Copy).then_inc(v_high.sem, 1)

        def low_v(dve, h, c):
            if c < 2:
                dve.wait_ge(*v_psum.before(h, 0))
            dve.wait_ge(*v_high.done(h, c))
            dve.tensor_tensor(vl[:, :, c * P:(c + 1) * P], rv[:, c % 2], vh[:, :, c * P:(c + 1) * P].bitcast(F32), ALU.subtract
                              ).then_inc(v_low.sem, 1)

        nc.all_engine_barrier()
        with nc.Block() as block:

            @block.sync
            def _(sp):
                def load_qk(h, ct):
                    c0 = q0 + ct * P if ct < DT else k0 + (ct - DT) * P
                    sp.dma_start(rqk[:, ct % 2], w_in[:, :, bass.ds(h * (DT * P) + c0, P)]).then_inc(wql[ct % 2].sem, 16)

                def turn(h, ahead):
                    if kind == "C":
                        sp.wait_ge(*qk_psum.before(h, 0))
                        sp.dma_start(wa[:], IN["w_a2"][0][:, bass.ds(h * P, P)]).then_inc(wal.sem, 16)
                    for ct in range(2, CT):
                        sp.wait_ge(*qk_low.done(h, ct - 2))
                        load_qk(h, ct)
                    for c in range(NC):
                        c0 = (gates0 + [v0])[c // 2] + c % 2 * P
                        sp.wait_ge(*(v_low.done(h, c - 2) if c >= 2 else v_low.before(h, 0)))
                        sp.dma_start(rv[:, c % 2], w_in[:, :, bass.ds(h * DV + c0, P)]).then_inc(wvl[c % 2].sem, 16)
                    if ahead is not None:
                        for ct in range(2):
                            sp.wait_ge(*qk_low.done(h, CT - 2 + ct))
                            load_qk(ahead, ct)

                for ct in range(2):
                    sp.sem_inc(wql[ct].sem, 16)
                with sp.Fori(0, H - 1) as h:
                    turn(h, h + 1)
                turn(H - 1, None)
                sp.wait_ge(*qk_low.done(H - 1, CT - 1))
                sp.wait_ge(*v_low.done(H - 1, NC - 1))
                first.start(sp)
                first.finish(sp)
                sp.wait_ge(*p_st.before(H, 0))
                sp.wait_ge(*s_st.before(H, 0))

            @block.gpsimd
            def _(pool):
                with pool.Fori(0, H) as h:
                    for t in range(T):
                        R = rows(t)
                        pool.wait_ge(*squared.done(h, t))
                        pool.sem_inc(M.passed, 1)
                        pool.tensor_scalar(sm[0:R, 4:5], sm[0:R, 3:4], ms_scale, EPS, ALU.mult, ALU.add).then_inc(mean_ready.sem, 1)
                        pool.wait_ge(*mean_ready.done(h, t))
                        pool.tensor_tensor(sm[0:R, 5:6], sm[0:R, 4:5], M.c("half", R), ALU.pow).then_inc(rstd_ready.sem, 1)

            @block.tensor
            def _(pe):
                def turn_g(h, t):
                    pe.wait_ge(*g_ready.done(h, t))
                    pe.wait_ge(*gT_copied.before(h, t))
                    pe.sem_inc(M.passed, 1)
                    R = rows(t)
                    for d in range(2):
                        last = pe.transpose(PS[7][:, d * P:d * P + R], g[0:R, d * P:(d + 1) * P], M.c("ident", R, R))
                    last.then_inc(gT_psum.sem, 1)

                def turn(h, previous):
                    pe.wait_ge(*state_ready.before(h, 0))
                    if kind == "C":
                        pe.wait_ge(*wal.done(h, 15))
                        for n in range(2):
                            pe.wait_ge(*qk_copied.before(h, 0))
                            pe.matmul(PS[n][:, 0:HALF], wa[:], M["a1T"][:, n * HALF:(n + 1) * HALF],
                                      start=True, stop=True).then_inc(qk_psum.sem, 1)
                        if previous is not None:
                            turn_g(previous, T - 1)
                    for ct in range(CT):
                        pe.wait_ge(*qk_low.done(h, ct))
                        for half in range(2):
                            n = NA + 2 * ct + half
                            pe.wait_ge(*(qk_copied.done(h, n - 2) if n >= 2 else qk_copied.before(h, 0)))
                            to = slice(half * HALF, (half + 1) * HALF)
                            for k in range(KT):
                                last = split_matmul(pe, PS[half][:, 0:HALF], (qkh[:, ct % 2, k, :], qkl[:, ct % 2, k, :]),
                                                    (M["hT_high"][:, k, to], M["hT_low"][:, k, to]), k == 0, k == KT - 1)
                            last.then_inc(qk_psum.sem, 1)
                        if kind != "C" and ct == 0 and previous is not None:
                            turn_g(previous, T - 1)

                    def project(t, c0, n, out):
                        for k in range(KT):
                            last = split_matmul(pe, out, (M["hT_high"][:, k, cols(t)], M["hT_low"][:, k, cols(t)]),
                                                (vh[:, k, c0:c0 + n], vl[:, k, c0:c0 + n]), k == 0, k == KT - 1)
                        return last

                    def project_gates(t):
                        pe.wait_ge(*gates_used.before(h, t))
                        project(t, 0, NG, PS[2][0:rows(t), 0:NG]).then_inc(gates_psum.sem, 1)

                    def project_v(t):
                        pe.wait_ge(*v_copied.before(h, t))
                        project(t, NG, DV, PS[3][0:rows(t), 0:DV]).then_inc(v_psum.sem, 1)

                    for t in range(T):
                        R, cs = rows(t), cols(t)
                        if t == 0:
                            pe.wait_ge(*v_low.done(h, NG // P - 1))
                        if t == 0:
                            project_gates(t)
                            pe.wait_ge(*v_low.done(h, NC - 1))
                            project_v(t)
                            pe.wait_ge(*(qk_copied.done(h, NP - 1) if kind == "A" else qk_ready.done(h, 0)))
                        else:
                            project_v(t)
                        pe.wait_ge(*kw_ready.before(h, t))
                        matmul_chain(pe, PS[4][0:R, 0:R], [(qk[:, DT + d, cs], qk[:, d, cs]) for d in range(DT)])
                        for d in range(DT):
                            last = pe.transpose(PS[4][0:R, (d + 1) * P:(d + 2) * P], qk[:, DT + d, cs], M.c("ident", P, P))
                        last.then_inc(scores_psum.sem, 1)
                        if t:
                            project_gates(t)
                        if t and kind != "C":
                            pe.wait_ge(*num_ready.before(h, t - 1))
                            pe.wait_ge(*(sl.done(h, sl.per - 1) if t == PT else state_ready.before(h, t)))
                            matmul_chain(pe, PS[5][0:R, 0:NV], [(qk[:, d, cs], St[t // PT][:, d, :]) for d in range(DT)])
                        pe.wait_ge(*scores_ready.done(h, t))
                        pe.wait_ge(*v_copied.done(h, t))
                        pe.wait_ge(*intra_copied.before(h, t))
                        pairs = [(sT[0:R, 0:R], v[0:R, :])]
                        if t and kind == "C":
                            pe.wait_ge(*sc_ready.done(h, t - 1))
                            pairs.append((qk[:, 0, cs], Sc[:]))
                        pe.sem_inc(M.passed, 1)
                        matmul_chain(pe, PS[6][0:R, 0:NV], pairs).then_inc(nums_psum.sem, 1)
                        pe.wait_ge(*kw_ready.done(h, t))
                        pe.wait_ge(*(nS_ready if kind == "C" else state_ready).before(h, t))
                        pe.sem_inc(M.passed, 1)
                        for d in range(DT):
                            last = pe.matmul(PS[d][:, 0:NV], kw[0:R, d * P:(d + 1) * P], v[0:R, :], start=True, stop=True)
                        last.then_inc(state_psum.sem, 1)
                        if t:
                            turn_g(h, t - 1)

                turn(0, None)
                with pe.Fori(1, H) as h:
                    turn(h, h - 1)
                turn_g(H - 1, T - 1)

            @block.scalar
            def _(act):
                def turn(h, ahead):
                    for n in range(NP):
                        ct, half = (n - NA) // 2, n % 2
                        act.wait_ge(*qk_psum.done(h, n))
                        to = slice(half * HALF, (half + 1) * HALF)
                        if n < NA:
                            act.sem_inc(M.passed, 1)
                            act.activation(la[:, to], PS[half][:, 0:HALF], ACT.Identity, bias=M["vec"][:, bass.ds(h + 64, 1)]
                                           ).then_inc(qk_copied.sem, 1)
                            if n == NA - 1:
                                log_sigmoid(act, None, None, lb[:], lc[:], None, Lg, h)
                        else:
                            scale = QS if (ct >= DT) == (kind == "A") else 1.0
                            act.activation((qk if kind == "A" else raw)[:, ct, to], PS[half][:, 0:HALF], ACT.Copy,
                                           scale=scale).then_inc(qk_copied.sem, 1)
                        if kind == "C" and n == NA + 1:
                            act.wait_ge(*shifted.done(h, 0))
                            act.activation(lb[:], la[:], ACT.Exp).then_inc(exps.sem, 1)
                            act.activation(lc[:], la[:], ACT.Exp, scale=-1.0).then_inc(exps.sem, 1)
                            act.activation(eend[:], ends[:], ACT.Exp).then_inc(exps.sem, 1)
                        if half == 1 and 2 <= ct + 2 < CT:
                            high_qk(act, h, ct + 2)
                        for c in range(NC):
                            if after[c] == n:
                                high_v(act, h, c)
                        if n == NP - 2:
                            act.wait_ge(*s_st.before(h, 0))
                            src = S_in[bass.ds(h, 1)].rearrange("a (d p) v -> p (a d) v", p=P)
                            act.dma_start(St[1][:, :, 0:DV], src).then_inc(sl.sem, 16)
                            if kind == "A":
                                n_in = IN["state_mlstm_n"][0, 0][bass.ds(h, 1)].rearrange("a (d p b) -> p (a d) b", p=P, b=1)
                                act.dma_start(St[1][:, :, DV:NV], n_in, allow_slow_non_contiguous=True).then_inc(sl.sem, 16)
                    for t in range(T):
                        R = rows(t)
                        if kind == "A":
                            act.wait_ge(*logit_ready.done(h, t))
                            act.activation(E[0:R, 0:R], arg[0:R, 0:R], ACT.Exp).then_inc(decay_ready.sem, 1)
                        def tanh_gates():
                            act.wait_ge(*gates_psum.done(h, t))
                            act.wait_ge(*(hg_ready if kind == "A" else gates_used).before(h, t))
                            act.activation(th[0:R, :], PS[2][0:R, 0:NG], ACT.Tanh, scale=0.5).then_inc(tanh_done.sem, 1)
                        if t == 0:
                            tanh_gates()
                        act.wait_ge(*v_psum.done(h, t))
                        act.wait_ge(*state_psum.before(h, t))
                        act.activation(v[0:R, 0:DV], PS[3][0:R, 0:DV], ACT.Copy).then_inc(v_copied.sem, 1)
                        if t:
                            tanh_gates()
                        act.wait_ge(*nums_psum.done(h, t))
                        act.wait_ge(*g_ready.before(h, t))
                        act.activation(num_a[0:R, :], PS[6][0:R, 0:NV], ACT.Copy).then_inc(intra_copied.sem, 1)
                        if kind == "A":
                            act.wait_ge(*hg_ready.done(h, t))
                        elif kind == "B" and t:
                            act.wait_ge(*num_ready.done(h, t - 1))
                        else:
                            act.wait_ge(*intra_copied.done(h, t))
                        src = hg if kind == "A" else (num if kind == "B" and t else num_a)
                        act.activation(sq[0:R, :], src[0:R, 0:DV], ACT.Square, accum_out=sm[0:R, 3:4]).then_inc(squared.sem, 1)
                        if t in (1, 2):
                            high_qk(act, ahead, t - 1)
                        if t >= PT - 1:
                            i = t - PT + 1
                            act.wait_ge(*state_ready.done(h, t))
                            st = (p_st, s_st)[i]
                            act.dma_start((pS, sS)[i][bass.ds(h, 1)].rearrange("a (d p) v -> p (a d) v", p=P),
                                           St[i][:, :, 0:DV]).then_inc(st.sem, 16)
                            if kind == "A":
                                n_out = OUT[("pn", "sn")[i]][0, 0][bass.ds(h, 1)].rearrange("a (d p b) -> p (a d) b", p=P, b=1)
                                act.dma_start(n_out, St[i][:, :, DV:NV], allow_slow_non_contiguous=True).then_inc(st.sem, 16)

                for ct in range(2):
                    high_qk(act, 0, ct)
                with act.Fori(0, H - 1) as h:
                    turn(h, h + 1)
                turn(H - 1, None)

            @block.vector
            def _(dve):
                if kind == "A":
                    dve.memset(v[:, DV:NV], 1.0).then_inc(filled.sem, 1)
                if kind == "C":
                    dve.memset(sT[:], 0.0).then_inc(filled.sem, 1)
                    dve.wait_ge(*filled.done(0, 0))
                def turn(h, ahead):
                    link = Link(dve, lk, h)
                    if kind == "A":
                        for n in range(NP):
                            for c in range(NC):
                                if after[c] == n:
                                    low_v(dve, h, c)
                            if n in (1, 3):
                                low_qk(dve, h, n // 2 + 2)
                    elif kind == "B":
                        for i in range(2):
                            if i == 0:
                                low_v(dve, h, 0)
                                low_qk(dve, h, 2)
                                low_v(dve, h, 1)
                                low_qk(dve, h, 3)
                            else:
                                low_v(dve, h, 2)
                                low_v(dve, h, 3)
                            dve.wait_ge(*qk_copied.done(h, 4 * i + 3))
                            x1, x2 = raw[:, 2 * i, :], raw[:, 2 * i + 1, :]
                            for a, b, out, op in ((x1, x2, 0, ALU.subtract), (x2, x1, 1, ALU.add)):
                                link(dve.tensor_tensor(ra[:], a, M.c("cos"), ALU.mult))
                                link(dve.tensor_tensor(rb[:], b, M.c("sin"), ALU.mult))
                                last = dve.tensor_tensor(qk[:, 2 * i + out, :], ra[:], rb[:], op)
                                if (i, out) == (1, 1):
                                    last.then_inc(qk_ready.sem, 1)
                                else:
                                    link(last)
                    elif kind == "C":
                        dve.wait_ge(*qk_copied.done(h, NA - 1))
                        link(log_sigmoid(None, dve, la[:], lb[:], lc[:], la[:], Lg, h))
                        low_v(dve, h, 0)
                        link(dve.tensor_scalar(la[:], la[:], 1.0 / 16.0, None, ALU.mult))
                        low_v(dve, h, 1)
                        for t in range(T):
                            last = dve.tensor_tensor_scan(bT[:, cols(t)], M.c("ones")[:, 0:rows(t)], la[:, cols(t)], 0.0,
                                                          ALU.mult, ALU.add)
                        link(last)
                        for t in range(T):
                            mid = t * P + rows(t) // 2 - 1
                            end = t * P + rows(t) - 1
                            dve.tensor_copy(ends[:, 0, t:t + 1], bT[:, mid:mid + 1])
                            dve.tensor_copy(ends[:, 2, t:t + 1], bT[:, end:end + 1])
                            last = dve.tensor_scalar(ends[:, 1, t:t + 1], bT[:, end:end + 1], bT[:, mid:mid + 1], None, ALU.subtract)
                        link(last)
                        for t in range(T):
                            last = dve.tensor_scalar(la[:, cols(t)], bT[:, cols(t)], ends[:, 0, t:t + 1], None, ALU.subtract)
                        last.then_inc(shifted.sem, 1)
                        dve.wait_ge(*exps.done(h, 2))
                        dve.wait_ge(*qk_copied.done(h, NA + 1))
                        link(dve.tensor_tensor(qk[:, 0, :], raw[:, 0, :], lb[:], ALU.mult))
                        for c in range(2, NC):
                            low_v(dve, h, c)
                        dve.wait_ge(*qk_copied.done(h, NP - 1))
                        dve.tensor_tensor(qk[:, 1, :], raw[:, 1, :], lc[:], ALU.mult).then_inc(qk_ready.sem, 1)
                    for t in range(T):
                        R, cs = rows(t), cols(t)
                        S = St[t // PT]
                        u = h + t * H
                        if kind == "A":
                            dve.scalar_tensor_tensor(arg[0:R, 0:R], M["negM"][0:R, bass.ds(h, 1), cs].rearrange("p a t -> p (a t)"),
                                                     M["ucol"][0:R, t, bass.ds(h, 1)], M.c("neg_causal", R)[:, 0:R],
                                                     ALU.add, ALU.add).then_inc(logit_ready.sem, 1)
                            dve.wait_ge(*decay_ready.done(h, t))
                        dve.wait_ge(*scores_psum.done(h, t))
                        if kind == "C":
                            dve.sem_inc(M.passed, 1)
                            dve.copy_predicated(sT[0:R, 0:R], M.c("mask", R)[:, 0:R].bitcast(U32), PS[4][0:R, 0:R]).then_inc(scores_ready.sem, 1)
                            dve.tensor_copy(kw[0:R, :], PS[4][0:R, P:2 * P]).then_inc(kw_ready.sem, 1)
                        else:
                            if kind == "A":
                                by, kc = E[0:R, 0:R], M["mcols"][0:R, 1, t, bass.ds(h, 1)]
                            else:
                                by = M["const"][0:R, bass.ds(h * P + M.at["decay"][0], R)]
                                kc = M["const"][0:R, bass.ds(h + M.at["k_decay"][0] + H * (t // PT), 1)]
                            dve.tensor_tensor(sT[0:R, 0:R], PS[4][0:R, 0:R], by, ALU.mult).then_inc(scores_ready.sem, 1)
                            dve.tensor_scalar(kw[0:R, :], PS[4][0:R, P:(1 + DT) * P], kc, None, ALU.mult).then_inc(kw_ready.sem, 1)
                        if t == PT:
                            dve.wait_ge(*sl.done(h, sl.per - 1))
                        if t == 0:
                            dve.wait_ge(*p_st.before(h, 0))
                        if t:
                            dve.wait_ge(*state_ready.before(h, t))
                        if kind == "C" and t:
                            dve.tensor_scalar(Sc[:], S[:, 0, :], eend[:, 0, t:t + 1], None, ALU.mult).then_inc(sc_ready.sem, 1)
                        dve.wait_ge(*tanh_done.done(h, t))
                        dve.wait_ge(*g_ready.before(h, t))
                        dve.scalar_tensor_tensor(zs[0:R, :], th[0:R, NG - DV:NG], 1.0, PS[2][0:R, NG - DV:NG], ALU.add, ALU.mult
                                                 ).then_inc(gates_used.sem, 1)
                        dve.wait_ge(*state_psum.done(h, t))
                        if kind == "C":
                            dve.tensor_scalar(nS[:], PS[0][:, 0:NV], eend[:, 1, t:t + 1], None, ALU.mult).then_inc(nS_ready.sem, 1)
                            dve.wait_ge(*nS_ready.done(h, t))
                            if t == 0:
                                dve.tensor_copy(S[:, 0, :], nS[:]).then_inc(state_ready.sem, 1)
                            else:
                                dve.scalar_tensor_tensor(S[:, 0, :], S[:, 0, :], eend[:, 2, t:t + 1], nS[:], ALU.mult, ALU.add
                                                         ).then_inc(state_ready.sem, 1)
                        else:
                            dec = (M["mcols"][:, 2, t, bass.ds(h, 1)] if kind == "A" else
                                   M["const"][:, bass.ds(h + M.at["s_decay"][0] + H * (t // PT), 1)])
                            for d in range(DT):
                                if t == 0:
                                    last = dve.tensor_copy(S[:, d, :], PS[d][:, 0:NV])
                                else:
                                    last = dve.scalar_tensor_tensor(S[:, d, :], S[:, d, :], dec, PS[d][:, 0:NV], ALU.mult, ALU.add)
                            last.then_inc(state_ready.sem, 1)
                        dve.wait_ge(*intra_copied.done(h, t))
                        n_src = num_a
                        if t and kind != "C":
                            w = (M["mcols"][0:R, 0, t, bass.ds(h, 1)] if kind == "A" else
                                 M["const"][0:R, bass.ds(h + M.at["q_decay"][0], 1)])
                            dve.scalar_tensor_tensor(num[0:R, :], PS[5][0:R, 0:NV], w, num_a[0:R, :], ALU.mult, ALU.add
                                                     ).then_inc(num_ready.sem, 1)
                            dve.wait_ge(*num_ready.done(h, t - 1))
                            n_src = num
                        if kind == "A":
                            dcol = n_src[0:R, DV:NV]
                            dve.scalar_tensor_tensor(sm[0:R, 0:1], dcol, -1.0, dcol, ALU.mult, ALU.max).then_inc(den.sem, 1)
                            dve.wait_ge(*den.done(h, 4 * t))
                            dve.tensor_tensor(sm[0:R, 1:2], sm[0:R, 0:1], M["mcols"][0:R, 3, t, bass.ds(h, 1)], ALU.max).then_inc(den.sem, 1)
                            dve.wait_ge(*den.done(h, 4 * t + 1))
                            dve.reciprocal(sm[0:R, 2:3], sm[0:R, 1:2]).then_inc(den.sem, 1)
                            dve.wait_ge(*den.done(h, 4 * t + 2))
                            dve.tensor_scalar(hg[0:R, :], n_src[0:R, 0:DV], sm[0:R, 2:3], None, ALU.mult).then_inc(den.sem, 1)
                            dve.wait_ge(*den.done(h, 4 * t + 3))
                            dve.scalar_tensor_tensor(hg[0:R, :], th[0:R, 0:DV], 1.0, hg[0:R, :], ALU.add, ALU.mult).then_inc(hg_ready.sem, 1)
                            fin = hg
                        else:
                            fin = n_src
                        dve.wait_ge(*rstd_ready.done(h, t))
                        dve.wait_ge(*gates_used.done(h, t))
                        dve.wait_ge(*gT_psum.before(h, t))
                        dve.scalar_tensor_tensor(g[0:R, :], fin[0:R, 0:DV], sm[0:R, 5:6], zs[0:R, :], ALU.mult, ALU.mult
                                                 ).then_inc(g_ready.sem, 1)
                        for tt in ([t - 1] if t else []) + ([t] if t == T - 1 else []):
                            dve.wait_ge(*gT_psum.done(h, tt))
                            for d in range(2):
                                last = dve.tensor_scalar(M["gT"][:, bass.ds(h * 2 + (g_row + d), 1), cols(tt)].rearrange("p a t -> p (a t)"),
                                                         PS[7][:, d * P:d * P + rows(tt)], M["vec"][:, bass.ds(h * 2 + (g_col + d), 1)],
                                                         None, ALU.mult)
                            last.then_inc(gT_copied.sem, 1)
                        if t in (1, 2):
                            low_qk(dve, ahead, t - 1)
                    link.close()

                for ct in range(2):
                    low_qk(dve, 0, ct)
                with dve.Fori(0, H - 1) as h:
                    turn(h, h + 1)
                turn(H - 1, None)


def odd_gates(nc, M, IN, OUT):
    with Phase(nc, "odd_gates") as ph:
        M["hT"] = ph.sb("hT", [P, KT, TOK])
        act_norm, pool_norm, dve_norm, pe_norm, norm_signals = norm_steps(ph, M, 1)
        H = GDN_H
        sb, sig = ph.sb, ph.counter
        wg = sb("w_gates", [P, KT, 96])
        cleared = sig("w_gates_cleared")
        dt_b, a_l = sb("dt_bias", [H, 1]), sb("a_log", [H, 1])
        ndt, ea = sb("minus_dt", [H, 1]), sb("exp_a", [H, 1])
        cache = sb("cache_rows", [72, P])
        gi, ta, tb = (sb(n, [H, 2, TOK]) for n in ("gate_in", "ls_a", "ls_b"))
        ge_rows = sb("ge_rows", [H, T, H])
        col, bro = sb("gate_cols", [P, 2, T, H]), sb("gate_broadcast", [P, T, H])
        arg = sb("gate_args", [P, 5, T, H])
        wl = sig("w_gates_loaded", 16 * 6)
        proj, copied = sig("gates_psum", 3), sig("gates_copied", 6)
        S = {n: sig("ls_" + n) for n in ("abs", "exp", "plus", "log")}
        lk = sig("vector_step")
        exp_a, rows_ready, colsp, args_ready, exps = (sig(n) for n in ("exp_a_ready", "rows_ready", "cols_psum", "args_ready", "gate_exps"))
        signs, beta = sig("minus_dt_ready"), sig("beta_halved")
        cachep, cachec = sig("cache_psum"), sig("cache_copied")
        x_kept = sig("x_kept", 32)
        split = SplitInput(ph, M)
        first = FirstLoads(ph, M, IN, "gla")
        PS = M["ps"]
        rows_g = M["grow"]
        with nc.Block() as block:

            @block.sync
            def _(sp):
                w_in = IN["w_in_odd"][0].rearrange("(k p) n -> p k n", p=P)
                sp.wait_ge(*cleared.done(0, 0))
                for i, (c0, n) in enumerate(((2 * D, RANK), (5 * D + RANK, H), (5 * D + RANK + H, H))):
                    sp.dma_start(wg[:, :, 32 * i:32 * i + n], w_in[:, :, c0:c0 + n]).then_inc(wl.sem, 16)
                sp.dma_start(dt_b[:], IN["dt_bias"][0].rearrange("(h a) -> h a", a=1)).then_inc(wl.sem, 16)
                sp.dma_start(a_l[:], IN["a_log"][0].rearrange("(h a) -> h a", a=1)).then_inc(wl.sem, 16)
                sp.dma_start(OUT["y_p"][0].rearrange("(t p) d -> p t d", p=P), M["x"][:, 0:PT, :]).then_inc(x_kept.sem, 16)
                sp.dma_start(OUT["y_s"][0], M["x"][0:DEC, PT, :]).then_inc(x_kept.sem, 16)
                sp.dma_start(cache[:], IN["cache_gdn_conv"][0, 0].rearrange("r (c p) -> (r c) p", p=P)).then_inc(wl.sem, 16)
                sp.wait_ge(*x_kept.done(0, 31))
                sp.wait_ge(*norm_signals["xn"].done(0, T - 1))
                first.start(sp)
                first.finish(sp)

            @block.gpsimd
            def _(pool):
                pool_norm(pool)

            @block.tensor
            def _(pe):
                pe_norm(pe)
                pe.wait_ge(*wl.done(0, 95))
                small_projection(pe, M, wg, 0, 64 + H, (4, 5)).then_inc(proj.sem, 1)
                pe.transpose(PS[1][:, 0:72], cache[:], M.c("ident", 72, 72)).then_inc(cachep.sem, 1)
                pe.wait_ge(*rows_ready.done(0, 0))
                for n, r in enumerate((rows_g[:, 0, :], gi[:, 1, :])):
                    for t in range(T):
                        at = (n * T + t) * H
                        pe.transpose(PS[0][0:rows(t), at:at + H], r[:, cols(t)], M.c("ident", H, H))
                pe.matmul(PS[2][:, 0:T * H], M.c("ones", H), ge_rows[:].rearrange("p t h -> p (t h)"),
                          start=True, stop=True).then_inc(colsp.sem, 1)

            @block.scalar
            def _(act):
                act_norm(act)
                split.act_steps(act, norm_signals)
                act.wait_ge(*wl.done(0, 95))
                act.activation(ea[:], a_l[:], ACT.Exp).then_inc(exp_a.sem, 1)
                act.wait_ge(*signs.done(0, 0))
                for i in range(3):
                    act.wait_ge(*proj.done(0, 0))
                    for half in range(2):
                        to = slice(half * HALF, (half + 1) * HALF)
                        src = PS[4 + half][32 * i:32 * i + 32]
                        if i == 1:
                            act.activation(gi[:, 0, to], src[0:H, 0:HALF], ACT.Identity, bias=ndt[:], scale=-1.0).then_inc(copied.sem, 1)
                        else:
                            n = (RANK, 0, H)[i]
                            out = M["a1T"][:, to] if i == 0 else gi[:, 1, to]
                            act.activation(out, src[0:n, 0:HALF], ACT.Copy).then_inc(copied.sem, 1)
                log_sigmoid(act, None, None, ta[:], tb[:], None, S)
                act.wait_ge(*args_ready.done(0, 0))
                act.activation(M["gcols"][:], arg[:], ACT.Exp).then_inc(exps.sem, 1)

            @block.vector
            def _(dve):
                link = Link(dve, lk)
                dve.memset(wg[:], 0.0).then_inc(cleared.sem, 1)
                dve.memset(col[:], 0.0)
                dve.wait_ge(*wl.done(0, 95))
                dve.tensor_scalar(ndt[:], dt_b[:], -1.0, None, ALU.mult).then_inc(signs.sem, 1)
                dve_norm(dve)
                split.dve_steps(dve)
                dve.wait_ge(*cachep.done(0, 0))
                dve.tensor_copy(M["cacheT"][:], PS[1][:, 0:72]).then_inc(cachec.sem, 1)
                dve.wait_ge(*copied.done(0, 5))
                link(log_sigmoid(None, dve, gi[:], ta[:], tb[:], gi[:], S))
                dve.wait_ge(*exp_a.done(0, 0))
                link(dve.tensor_scalar(gi[:, 0, :], gi[:, 0, :], ea[:], None, ALU.mult))
                for t in range(T):
                    last = dve.tensor_tensor_scan(rows_g[:, 0, cols(t)], M.c("ones", H, rows(t)), gi[:, 0, cols(t)], 0.0, ALU.mult, ALU.add)
                link(last)
                dve.tensor_tensor(rows_g[:, 1, :], rows_g[:, 0, :], gi[:, 1, :], ALU.add)
                for t in range(T):
                    end = t * P + rows(t) - 1
                    last = dve.tensor_scalar(ge_rows[:, t, :], M.c("diag8", H)[:, 0:H], rows_g[:, 0, end:end + 1], None, ALU.mult)
                last.then_inc(rows_ready.sem, 1)
                dve.wait_ge(*colsp.done(0, 0))
                src = PS[0][:, 0:2 * T * H].rearrange("p (n t h) -> p n t h", n=2, t=T)
                dve.tensor_copy(col[:, :, 0:PT, :], src[:, :, 0:PT, :])
                dve.tensor_copy(col[0:DEC, :, PT, :], src[0:DEC, :, PT, :])
                link(dve.tensor_copy(bro[:].rearrange("p t h -> p (t h)"), PS[2][:, 0:T * H]))
                dve.tensor_copy(M["Gcol"][:], col[:, 0])
                dve.tensor_copy(arg[:, 0], col[:, 0])
                dve.tensor_tensor(arg[:, 1], col[:, 0], col[:, 1], ALU.add)
                dve.tensor_copy(arg[:, 2], col[:, 1])
                dve.tensor_tensor(arg[:, 3], bro[:], col[:, 0], ALU.subtract)
                dve.tensor_copy(arg[:, 4], bro[:]).then_inc(args_ready.sem, 1)
                dve.wait_ge(*exps.done(0, 0))
                dve.tensor_scalar(M["gcols"][:, 2], M["gcols"][:, 2], 0.5, None, ALU.mult).then_inc(beta.sem, 1)


def gdn_heads(nc, M, IN, OUT):
    H = GDN_H
    NL = len(LEVELS) - 1
    W = 3 + SEQ + 3 + DEC
    C = W - 3
    S0 = SEQ + 3
    PS = M["ps"]
    w_in = IN["w_in_odd"][0].rearrange("(k p) n -> p k n", p=P)
    sec = [2 * D + RANK + i * D for i in range(3)] + [6 * D + RANK + 2 * H]
    TB = (4, 6, 2, 3, 5)
    GB = (7, 4)

    def conv_cols(t):
        return slice(t * P, (t + 1) * P) if t < PT else slice(S0, S0 + DEC)

    with Phase(nc, "gdn", first=1) as ph:
        sb, sig = ph.sb, ph.counter
        place = M["x"][:].rearrange("p t d -> p (t d)")
        wraw = place[:, 0:4 * D].rearrange("p (a k c) -> p a k c", a=4, k=KT)
        wh, wl = (sb(n, [P, 2, KT, P], F32R) for n in ("w_high", "w_low"))
        pj, cv, thc = sb("pre_conv", [P, 3, W]), sb("conv", [P, 3, C]), sb("tanh_conv", [P, 3, C])
        tk = sb("qkv_tokens", [P, T, 3, P])
        sqs = thc[:].rearrange("p a b -> p (a b)")[:, 0:T * 2 * P].rearrange("p (t a d) -> p t a d", t=T, a=2)
        kn, qn, kbe, kg, bv = (sb(n, [P, T, P]) for n in ("k_norm", "q_norm", "k_beta_decay", "k_end", "v_beta"))
        ss, ms, rn, mh = (sb(n, [P, T, 2]) for n in ("ss2", "ms2", "rn2", "minus_half"))
        sc = sb("scales", [P, 4, T])
        kT, qT = sb("kT", [P, TOK]), sb("qT", [P, TOK])
        E = sb("E", [P, 2, TOK])
        gsel = E[0:H]
        AT, atT = sb("AT", [P, TOK]), sb("attnT", [P, TOK])
        XX, Q = sb("X_and_XT", [P, 2, TOK]), sb("Q", [P, TOK])
        X, XT = XX[:, 0, :], XX[:, 1, :]
        wN = Q
        ML = sb("A_level", [P, 2, TOK])
        u, o_a, o, g, sqj = (place[:, 4 * D + i * P:4 * D + (i + 1) * P] for i in range(5))
        zr, tz = (x[:].rearrange("p t d -> p (t d)")[:, 0:TOK] for x in (kn, qn))
        zs = sb("z_silu", [P, TOK])
        sm = sb("small", [P, 4])
        St = [sb("state_prompt", [P, P]), sb("state_sample", [P, P])]
        newc = sb("new_cache", [P, 2, 72])
        cr = tk[0:72, 0, 0:2, :]

        names = {"w_loaded0": 16, "w_loaded1": 16, "w_loaded2": 16, "w_loaded3": 16, "state_loaded": 16, "prompt_stored": 16,
                 "sample_stored": 16, "gsel_ready": 1, "G_psum": 1, "arg_ready": 1, "E_ready": 2, "proj_psum": 8, "proj_copied": 8,
                 "cache_put": 1, "conv_step": 9, "conv_ready": 3, "tanh_conv": 3, "silu_ready": 3, "cache_saved": 1, "tanh_z": 1,
                 "z_ready": 1,
                 "tok_psum": T, "tok_copied": T, "tok_squared": 1, "ss_ready": 1, "ms_ready": 1, "rn_ready": 1, "scale_a": 1, "scale_b": 1,
                 "kq_norm": 1, "kq_psum": 1, "kq_copied": 1, "kk_psum": 1, "A_ready": 1, "attn_ready": 1, "level_ready": NL,
                 "A1_ready": 1, "XT1_ready": 1, "X1_psum": 1, "X1_copied": 1,
                 "Q_psum": 2 * NL, "Q_copied": 2 * NL, "XX_psum": 2 * NL, "X_ready": 2 * NL, "w_psum": 1, "w_copied": 1, "kv_scaled": 1,
                 "u_psum": T, "u_copied": T, "o_psum": T, "o_copied": T, "o_ready": PT, "squared": T, "mean_ready": T, "rstd_ready": T,
                 "state_psum": T, "state_ready": T, "g_ready": T, "gT_psum": T, "gT_copied": T}
        names.update({"w_split_high": 4, "w_split_low": 4})
        s = {n: sig(n, k, {"proj_psum": 8, "gT_copied": T}.get(n, 1)) for n, k in names.items()}
        first = FirstLoads(ph, M, IN, "output1")
        cleared = sig("cleared")
        cacheT_psum, cacheT_copied, cache_stored = sig("cache_psum", 2), sig("cache_copied", 2), sig("cache_stored", 32)

        def tiles(x, t):
            return x[0:rows(t), t * P:t * P + rows(t)]

        def bank(n, t):
            return PS[n[0]][:, t * P:(t + 1) * P] if t < PT else PS[5][0:DEC, n[1]:n[1] + DEC]

        def blocks(x):
            return x.rearrange("p (t c) -> p t c", t=PT)

        def each_block(c):
            return c.rearrange("p (a c) -> p a c", a=1).broadcast_to([P, PT, P])

        def group(n, i):
            return ((0, 1), (2, 3) + ((PT,) if n < NL - 1 else ()))[i]

        def Q_bank(t):
            return PS[2 + 4 * (t // 2)][:, t % 2 * P:(t % 2 + 1) * P] if t < PT else PS[6][0:DEC, 2 * P:2 * P + DEC]

        def X_bank(i, t):
            return (PS[3 + t // 2][:, (2 * i + t % 2) * P:(2 * i + t % 2 + 1) * P] if t < PT
                    else PS[5][0:DEC, i * DEC:(i + 1) * DEC])


        def project(pe, h, a, b):
            for i in range(a, b) if h is not None else ():
                n, k = divmod(i, KT)
                ct, half = divmod(n, 2)
                if k == 0:
                    if half == 0:
                        pe.wait_ge(*s["w_split_low"].done(h, ct))
                    pe.wait_ge(*(s["proj_copied"].done(h, n - 2) if n >= 2 else s["proj_copied"].before(h, 0)))
                to = slice(half * HALF, (half + 1) * HALF)
                last = split_matmul(pe, PS[half][:, 0:HALF], (wh[:, ct % 2, k, :], wl[:, ct % 2, k, :]),
                                    (M["hT_high"][:, k, to], M["hT_low"][:, k, to]), k == 0, k == KT - 1)
                if k == KT - 1:
                    last.then_inc(s["proj_psum"].sem, 1)

        def slot_free(eng, h, ct):
            if ct >= 2:
                eng.wait_ge(*s["proj_psum"].done(h, 2 * (ct - 2) + 1))
            else:
                eng.wait_ge(*s["proj_psum"].done(h - 1, 2 * (ct + 2) + 1))

        def high(act, h, ct):
            if h is None:
                return
            act.wait_ge(*s[f"w_loaded{ct}"].done(h, 15))
            slot_free(act, h, ct)
            act.activation(wh[:, ct % 2], wraw[:, ct], ACT.Copy).then_inc(s["w_split_high"].sem, 1)

        def low(dve, h, ct):
            if h is None:
                return
            dve.wait_ge(*s["w_split_high"].done(h, ct))
            slot_free(dve, h, ct)
            dve.tensor_tensor(wl[:, ct % 2], wraw[:, ct], wh[:, ct % 2].bitcast(F32), ALU.subtract).then_inc(s["w_split_low"].sem, 1)

        def take_projection(act, h, n):
            if h is None:
                return
            ct, half = divmod(n, 2)
            if n == 0:
                act.wait_ge(*s["cache_saved"].before(h, 0))
            if n == 6:
                act.wait_ge(*s["z_ready"].before(h, 0))
                act.wait_ge(*s["kq_psum"].before(h, 0))
            act.wait_ge(*s["proj_psum"].done(h, n))
            if ct == 3:
                act.activation(zr[:, half * HALF:(half + 1) * HALF], PS[half][:, 0:HALF], ACT.Copy).then_inc(s["proj_copied"].sem, 1)
            elif half == 0:
                act.activation(pj[:, ct, 3:3 + HALF], PS[0][:, 0:HALF], ACT.Copy).then_inc(s["proj_copied"].sem, 1)
            else:
                act.activation(pj[:, ct, 3 + HALF:3 + SEQ], PS[1][:, 0:SEQ - HALF], ACT.Copy)
                act.activation(pj[:, ct, 6 + SEQ:W], PS[1][:, SEQ - HALF:HALF], ACT.Copy).then_inc(s["proj_copied"].sem, 1)

        def tanh_conv(act, h, ct):
            if h is None:
                return
            act.wait_ge(*s["conv_ready"].done(h, ct))
            if ct == 0:
                act.wait_ge(*s["ss_ready"].before(h, 0))
            act.activation(thc[:, ct, :], cv[:, ct, :], ACT.Tanh, scale=0.5).then_inc(s["tanh_conv"].sem, 1)

        def tanh_z(act, h):
            if h is None:
                return
            act.wait_ge(*s["proj_copied"].done(h, 7))
            act.activation(tz, zr, ACT.Tanh, scale=0.5).then_inc(s["tanh_z"].sem, 1)

        def convolve(dve, h, ct, j0=0, j1=4):
            if h is None:
                return
            if ct == 0 and j0 == 0:
                dve.wait_ge(*s["cache_saved"].before(h, 0))
                dve.wait_ge(*s["tok_psum"].before(h, 0))
                for c in range(3):
                    last = dve.tensor_copy(pj[:, c, S0:S0 + 3], cacheT_of(M, h, c))
                last.then_inc(s["cache_put"].sem, 1)
                dve.wait_ge(*s["cache_put"].done(h, 0))
            dve.wait_ge(*s["proj_copied"].done(h, 2 * ct + 1))
            for j in range(j0, j1):
                wj = M["conv"][:, bass.ds(h + (24 * j + 8 * ct), 1)]
                if j:
                    dve.wait_ge(*s["conv_step"].done(h, 3 * ct + j - 1))
                if j == 0:
                    ins = dve.tensor_scalar(cv[:, ct, :], pj[:, ct, 0:C], wj, None, ALU.mult)
                else:
                    ins = dve.scalar_tensor_tensor(cv[:, ct, :], pj[:, ct, j:j + C], wj, cv[:, ct, :], ALU.mult, ALU.add)
                ins.then_inc(s["conv_step" if j < 3 else "conv_ready"].sem, 1)

        def silu_conv(dve, h, ct):
            if h is None:
                return
            dve.wait_ge(*s["tanh_conv"].done(h, ct))
            dve.scalar_tensor_tensor(cv[:, ct, :], thc[:, ct, :], 1.0, cv[:, ct, :], ALU.add, ALU.mult).then_inc(s["silu_ready"].sem, 1)

        def save_cache(dve, h):
            if h is None:
                return
            for ct in range(3):
                for i, c0 in enumerate((SEQ, W - 3)):
                    last = dve.tensor_copy(new_cache_of(newc, i, h, ct), pj[:, ct, c0:c0 + 3])
            last.then_inc(s["cache_saved"].sem, 1)

        def select_G(dve, h):
            if h is None:
                return
            dve.wait_ge(*s["G_psum"].before(h, 0))
            dve.tensor_scalar(gsel, M["grow"][:], M["const"][0:H, bass.ds(h + M.at["diag8"][0], 1)], None, ALU.mult
                              ).then_inc(s["gsel_ready"].sem, 1)

        def gT_bank(t):
            return PS[5 if t < T - 1 else 7][:, 0:rows(t)]

        def turn_g(pe, h, t):
            pe.wait_ge(*s["g_ready"].done(h, t))
            pe.wait_ge(*s["gT_copied"].before(h, t))
            pe.sem_inc(M.passed, 1)
            pe.transpose(gT_bank(t), g[0:rows(t), :], M.c("ident", rows(t), rows(t))).then_inc(s["gT_psum"].sem, 1)

        def pe_turn(pe, h, ahead, previous):
            pe.wait_ge(*s["silu_ready"].done(h, 2))
            pe.wait_ge(*s["state_ready"].before(h, 0))
            pe.wait_ge(*s["u_copied"].before(h, 0))

            def turn_tokens(t):
                for i in range(3):
                    last = pe.transpose(PS[TB[t]][0:rows(t), i * P:(i + 1) * P], cv[:, i, conv_cols(t)], M.c("ident", P, P))
                last.then_inc(s["tok_psum"].sem, 1)

            pe.sem_inc(M.passed, 1)
            for t in range(PT):
                turn_tokens(t)
            pe.wait_ge(*s["gT_copied"].done(h - 1, T - 2))
            pe.sem_inc(M.passed, 1)
            turn_tokens(PT)
            pe.wait_ge(*s["o_ready"].before(h, 0))
            pe.wait_ge(*s["o_copied"].before(h, 0))
            if previous is not None:
                turn_g(pe, previous, T - 1)
            pe.wait_ge(*s["gsel_ready"].done(h, 0))
            pe.wait_ge(*s["tok_copied"].done(h, 1))
            pe.matmul(PS[GB[1]][:, 0:SEQ], M.c("ones", H), gsel[:, 1, 0:SEQ], start=True, stop=True)
            pe.wait_ge(*s["gT_copied"].before(h, 0))
            pe.matmul(PS[GB[0]][:, 0:SEQ], M.c("ones", H), gsel[:, 0, 0:SEQ], start=True, stop=True)
            for i in range(2):
                last = pe.matmul(PS[6][:, i * DEC:(i + 1) * DEC], M.c("ones", H), gsel[:, i, SEQ:TOK], start=True, stop=True)
            last.then_inc(s["G_psum"].sem, 1)
            project(pe, ahead, 0, 16)
            pe.wait_ge(*s["tok_copied"].done(h, T - 1))
            pe.wait_ge(*s["kq_norm"].done(h, 0))
            pe.sem_inc(M.passed, 1)
            for i, x in enumerate((kn, qn)):
                for t in range(T):
                    R = rows(t)
                    out = PS[2 + i][:, t * P:(t + 1) * P] if t < PT else PS[5][:, i * DEC:(i + 1) * DEC]
                    last = pe.transpose(out, x[0:R, t, :], M.c("ident", R, R))
            last.then_inc(s["kq_psum"].sem, 1)
            project(pe, ahead, 16, 18)
            pe.wait_ge(*s["kq_copied"].done(h, 0))
            for i, x in enumerate((kT, qT)):
                for t in range(T):
                    last = pe.matmul(bank((2 + i, i * DEC), t), kT[:, cols(t)], x[:, cols(t)], start=True, stop=True)
            last.then_inc(s["kk_psum"].sem, 1)
            project(pe, ahead, 18, 26)
            pe.wait_ge(*s["XT1_ready"].done(h, 0))
            pe.wait_ge(*s["attn_ready"].done(h, 0))
            pe.sem_inc(M.passed, 1)
            for t in range(T):
                last = pe.transpose(bank((4, 0), t), tiles(XT, t), M.c("ident", rows(t), rows(t)))
            last.then_inc(s["X1_psum"].sem, 1)
            project(pe, ahead, 26, 28)
            pe.wait_ge(*s["X1_copied"].done(h, 0))
            for n in range(NL):
                pe.wait_ge(*s["level_ready"].done(h, n))
                for i in range(2):
                    if n:
                        pe.wait_ge(*s["X_ready"].done(h, 2 * (n - 1) + i))
                    for t in group(n, i):
                        last = pe.matmul(Q_bank(t), tiles(ML[:, n % 2, :], t), tiles(X, t), start=True, stop=True)
                    last.then_inc(s["Q_psum"].sem, 1)
                project(pe, ahead, *((28 + 5 * n, 30 + 5 * n) if n < 4 else (40 + 2 * n, 41 + 2 * n)))
                for i in range(2):
                    pe.wait_ge(*s["Q_copied"].done(h, 2 * n + i))
                    for t in group(n, i):
                        if n < NL - 1:
                            pe.matmul(X_bank(0, t), tiles(XT, t), tiles(Q, t), start=True, stop=True)
                        last = pe.matmul(X_bank(1, t), tiles(Q, t), tiles(XT, t), start=True, stop=True)
                    last.then_inc(s["XX_psum"].sem, 1)
                project(pe, ahead, *((30 + 5 * n, 33 + 5 * n) if n < 4 else (41 + 2 * n, 42 + 2 * n)))
            pe.wait_ge(*s["X_ready"].done(h, 2 * NL - 1))
            pe.wait_ge(*s["kv_scaled"].done(h, 0))
            for t in range(T):
                R = rows(t)
                out = PS[2][:, t * P:t * P + R] if t < PT else PS[5][:, 0:DEC]
                last = pe.matmul(out, kbe[0:R, t, :], tiles(XT, t), start=True, stop=True)
            last.then_inc(s["w_psum"].sem, 1)

            for t in range(T):
                R, S = rows(t), St[t // PT]
                if t == 1:
                    pe.wait_ge(*s["w_copied"].done(h, 0))
                if t:
                    pe.wait_ge(*s["state_ready"].before(h, t))
                if t == PT:
                    pe.wait_ge(*s["state_loaded"].done(h, 15))
                pe.wait_ge(*s["u_copied"].before(h, t))
                pairs = [(tiles(XT, t), bv[0:R, t, :])] + ([(wN[:, cols(t)], S[:])] if t else [])
                pe.sem_inc(M.passed, 1)
                matmul_chain(pe, PS[6][0:R, 0:P], pairs).then_inc(s["u_psum"].sem, 1)
                project(pe, ahead, *((52, 55), (55, 58), (58, 60), (60, 62), (62, 64))[t])
                pe.wait_ge(*s["o_copied"].before(h, t))
                if t:
                    pe.wait_ge(*s["o_ready"].before(h, t - 1))
                    pe.matmul(PS[7][0:R, 0:P], qT[:, cols(t)], S[:], start=True, stop=True)
                pe.wait_ge(*s["u_copied"].done(h, t))
                pe.sem_inc(M.passed, 1)
                pe.matmul(PS[4][:, 0:P], kg[0:R, t, :], u[0:R, :], start=True, stop=True).then_inc(s["state_psum"].sem, 1)
                pe.matmul(PS[7][0:R, P:2 * P], tiles(atT, t), u[0:R, :], start=True, stop=True).then_inc(s["o_psum"].sem, 1)
                if t:
                    turn_g(pe, h, t - 1)

        def act_turn(act, h, ahead, second):
            for t in range(T):
                R = rows(t)
                act.wait_ge(*s["tok_psum"].done(h, t))
                act.activation(tk[0:R, t, :, :], PS[TB[t]][0:R, 0:3 * P].rearrange("p (a d) -> p a d", a=3), ACT.Copy
                               ).then_inc(s["tok_copied"].sem, 1)
            act.wait_ge(*s["tok_copied"].done(h, T - 1))
            act.wait_ge(*s["silu_ready"].done(h, 2))
            act.activation(sqs, tk[:, :, 0:2, :], ACT.Square).then_inc(s["tok_squared"].sem, 1)
            tanh_z(act, h)
            high(act, ahead, 1)
            take_projection(act, ahead, 0)
            act.wait_ge(*s["arg_ready"].done(h, 0))
            act.activation(E[:, :, 0:SEQ], E[:, :, 0:SEQ], ACT.Exp).then_inc(s["E_ready"].sem, 1)
            act.activation(E[0:DEC, :, SEQ:TOK], E[0:DEC, :, SEQ:TOK], ACT.Exp).then_inc(s["E_ready"].sem, 1)
            take_projection(act, ahead, 1)
            high(act, ahead, 2)
            act.wait_ge(*s["sample_stored"].before(h, 0))
            act.dma_start(St[1][:], IN["state_gdn"][0, 0][bass.ds(h, 1)].rearrange("a p v -> p (a v)")).then_inc(s["state_loaded"].sem, 16)
            act.wait_ge(*s["kq_psum"].done(h, 0))
            for i, x in enumerate((kT, qT)):
                act.activation(x[:, 0:SEQ], PS[2 + i][:, 0:SEQ], ACT.Copy)
                last = act.activation(x[:, SEQ:TOK], PS[5][:, i * DEC:(i + 1) * DEC], ACT.Copy)
            last.then_inc(s["kq_copied"].sem, 1)
            take_projection(act, ahead, 2)
            act.wait_ge(*s["X1_psum"].done(h, 0))
            act.activation(X[:, 0:SEQ], PS[4][:, :], ACT.Copy)
            act.activation(X[0:DEC, SEQ:TOK], PS[5][0:DEC, 0:DEC], ACT.Copy).then_inc(s["X1_copied"].sem, 1)
            for n in range(NL):
                for i in range(2):
                    act.wait_ge(*s["Q_psum"].done(h, 2 * n + i))
                    last = act.activation(Q[:, 2 * i * P:2 * (i + 1) * P], PS[2 + 4 * i][:, 0:2 * P], ACT.Copy)
                    if i and n < NL - 1:
                        last = act.activation(Q[0:DEC, SEQ:TOK], Q_bank(PT), ACT.Copy)
                    last.then_inc(s["Q_copied"].sem, 1)
                if n == 0:
                    take_projection(act, ahead, 3)
                    high(act, ahead, 3)
                elif n == 2:
                    tanh_conv(act, ahead, 0)
                    take_projection(act, ahead, 4)
                elif n == 3:
                    tanh_conv(act, ahead, 1)
                    take_projection(act, ahead, 5)
                elif n == 4:
                    high(act, second, 0)
            act.wait_ge(*s["w_psum"].done(h, 0))
            act.activation(wN[:, 0:SEQ], PS[2][:, :], ACT.Copy, scale=-1.0)
            act.activation(wN[:, SEQ:TOK], PS[5][:, 0:DEC], ACT.Copy, scale=-1.0).then_inc(s["w_copied"].sem, 1)
            for t in range(T):
                R = rows(t)
                act.wait_ge(*s["u_psum"].done(h, t))
                act.wait_ge(*s["o_psum"].before(h, t))
                act.activation(u[0:R, :], PS[6][0:R, 0:P], ACT.Copy).then_inc(s["u_copied"].sem, 1)
                act.wait_ge(*s["o_psum"].done(h, t))
                act.wait_ge(*s["g_ready"].before(h, t))
                act.activation(o_a[0:R, :], PS[7][0:R, P:2 * P], ACT.Copy).then_inc(s["o_copied"].sem, 1)
                act.wait_ge(*(s["o_ready"].done(h, t - 1) if t else s["o_copied"].done(h, t)))
                act.activation(sqj[0:R, :], (o if t else o_a)[0:R, :], ACT.Square, accum_out=sm[0:R, 0:1]).then_inc(s["squared"].sem, 1)
                if t == 0:
                    tanh_conv(act, ahead, 2)
                if t == 1:
                    take_projection(act, ahead, 6)
                if t == 4:
                    take_projection(act, ahead, 7)
                if t >= PT - 1:
                    i = t - PT + 1
                    act.wait_ge(*s["state_ready"].done(h, t))
                    act.dma_start(OUT[("pgdn", "sgdn")[i]][0, 0][bass.ds(h, 1)].rearrange("a p v -> p (a v)"), St[i][:]
                                  ).then_inc(s[("prompt_stored", "sample_stored")[i]].sem, 16)

        def dve_turn(dve, h, ahead, second):
            dve.wait_ge(*s["tok_squared"].done(h, 0))
            dve.tensor_reduce(ss[:], sqs, AX.X, ALU.add).then_inc(s["ss_ready"].sem, 1)
            dve.wait_ge(*s["tanh_z"].done(h, 0))
            dve.wait_ge(*s["gT_copied"].before(h, 0))
            dve.scalar_tensor_tensor(zs[:], tz, 1.0, zr, ALU.add, ALU.mult).then_inc(s["z_ready"].sem, 1)
            dve.wait_ge(*s["G_psum"].done(h, 0))
            dve.wait_ge(*s["attn_ready"].before(h, 0))
            for i, name in ((1, "neg_strict"), (0, "neg_causal")):
                for t in range(T):
                    R = rows(t)
                    src = PS[GB[i]][0:R, t * P:t * P + R] if t < PT else PS[6][0:R, i * DEC:(i + 1) * DEC]
                    last = dve.scalar_tensor_tensor(E[0:R, i, t * P:t * P + R], src, M["Gcol"][0:R, t, bass.ds(h, 1)],
                                                    M.c(name, R)[:, 0:R], ALU.subtract, ALU.add)
            last.then_inc(s["arg_ready"].sem, 1)
            dve.wait_ge(*s["rn_ready"].done(h, 0))
            dve.wait_ge(*s["kv_scaled"].before(h, 0))
            dve.tensor_scalar(sc[:, 0, :], rn[:, :, 1], 0.5, None, ALU.mult)
            dve.tensor_scalar(sc[:, 1, :], rn[:, :, 0], 0.5 * P ** -0.5, None, ALU.mult).then_inc(s["scale_a"].sem, 1)
            dve.wait_ge(*s["scale_a"].done(h, 0))

            def gcol(i):
                return M["gcols"][:, i, :, bass.ds(h, 1)].rearrange("p t a -> p (t a)")

            def spread(x):
                return x.rearrange("p (t a) -> p t a", a=1).broadcast_to([P, T, P])

            dve.wait_ge(*s["z_ready"].done(h, 0))
            dve.tensor_tensor(kn[:], tk[:, :, 1, :], spread(sc[:, 0, :]), ALU.mult)
            dve.tensor_tensor(qn[:], tk[:, :, 0, :], spread(sc[:, 1, :]), ALU.mult).then_inc(s["kq_norm"].sem, 1)
            low(dve, ahead, 1)
            dve.tensor_tensor(sc[:, 2, :], sc[:, 0, :], gcol(1), ALU.mult)
            dve.tensor_tensor(sc[:, 3, :], sc[:, 0, :], gcol(3), ALU.mult).then_inc(s["scale_b"].sem, 1)
            dve.wait_ge(*s["scale_b"].done(h, 0))
            dve.tensor_tensor(kbe[:], tk[:, :, 1, :], spread(sc[:, 2, :]), ALU.mult)
            dve.tensor_tensor(kg[:], tk[:, :, 1, :], spread(sc[:, 3, :]), ALU.mult)
            dve.tensor_tensor(bv[:], tk[:, :, 2, :], spread(gcol(2)), ALU.mult).then_inc(s["kv_scaled"].sem, 1)
            low(dve, ahead, 2)
            dve.wait_ge(*s["kk_psum"].done(h, 0))
            dve.wait_ge(*s["E_ready"].done(h, 1))
            dve.tensor_tensor(AT[:, 0:SEQ], PS[2][:, :], E[:, 1, 0:SEQ], ALU.mult)
            dve.tensor_tensor(AT[0:DEC, SEQ:TOK], PS[5][0:DEC, 0:DEC], E[0:DEC, 1, SEQ:TOK], ALU.mult).then_inc(s["A_ready"].sem, 1)
            dve.wait_ge(*s["A_ready"].done(h, 0))
            dve.tensor_tensor(blocks(Q[:, 0:SEQ]), blocks(AT[:, 0:SEQ]), each_block(M.c("levels")[:, 0:P]), ALU.mult)
            dve.tensor_tensor(tiles(Q, PT), tiles(AT, PT), M.c("levels", DEC)[:, 0:DEC], ALU.mult).then_inc(s["A1_ready"].sem, 1)
            dve.wait_ge(*s["A1_ready"].done(h, 0))
            dve.tensor_tensor(blocks(XT[:, 0:SEQ]), each_block(M.c("ident")), blocks(Q[:, 0:SEQ]), ALU.subtract)
            dve.tensor_tensor(tiles(XT, PT), M.c("ident", DEC, DEC), tiles(Q, PT), ALU.subtract).then_inc(s["XT1_ready"].sem, 1)
            dve.tensor_tensor(atT[0:DEC, SEQ:TOK], PS[5][0:DEC, DEC:2 * DEC], E[0:DEC, 0, SEQ:TOK], ALU.mult)
            dve.tensor_tensor(atT[:, 0:SEQ], PS[3][:, :], E[:, 0, 0:SEQ], ALU.mult).then_inc(s["attn_ready"].sem, 1)
            dve.wait_ge(*s["X1_copied"].done(h, 0))
            for n in range(NL):
                convolve(dve, ahead, n // 2, 2 * (n % 2), 2 * (n % 2) + 2)
                if n == 1:
                    low(dve, ahead, 3)
                elif n == 3:
                    silu_conv(dve, ahead, 0)
                elif n == 4:
                    silu_conv(dve, ahead, 1)
                for i in range(2):
                    dve.wait_ge(*s["XX_psum"].done(h, 2 * n + i))
                    if n:
                        dve.wait_ge(*s["X_ready"].done(h, 2 * (n - 1) + i))
                    k = 0 if n < NL - 1 else 1
                    at = slice(2 * i * P, 2 * (i + 1) * P)
                    last = dve.tensor_tensor(XX[:, k:2, at], XX[:, k:2, at], PS[3 + i][:, 2 * k * P:4 * P].rearrange("p (a c) -> p a c", a=2 - k),
                                             ALU.subtract)
                    if i and n < NL - 1:
                        last = dve.tensor_tensor(XX[0:DEC, :, SEQ:TOK], XX[0:DEC, :, SEQ:TOK],
                                                 PS[5][0:DEC, 0:2 * DEC].rearrange("p (a c) -> p a c", a=2), ALU.subtract)
                    last.then_inc(s["X_ready"].sem, 1)
            for t in range(T):
                R, S = rows(t), St[t // PT]
                if t == 0:
                    dve.wait_ge(*s["prompt_stored"].before(h, 0))
                if t == PT:
                    dve.wait_ge(*s["state_loaded"].done(h, 15))
                dve.wait_ge(*s["state_psum"].done(h, t))
                if t == 0:
                    dve.tensor_copy(S[:], PS[4][:, 0:P]).then_inc(s["state_ready"].sem, 1)
                else:
                    dve.wait_ge(*s["state_ready"].before(h, t))
                    dve.scalar_tensor_tensor(S[:], S[:], M["gcols"][:, 4, t, bass.ds(h, 1)], PS[4][:, 0:P], ALU.mult, ALU.add
                                             ).then_inc(s["state_ready"].sem, 1)
                dve.wait_ge(*s["o_copied"].done(h, t))
                if t:
                    dve.wait_ge(*s["g_ready"].before(h, t))
                    dve.scalar_tensor_tensor(o[0:R, :], PS[7][0:R, 0:P], M["gcols"][0:R, 0, t, bass.ds(h, 1)], o_a[0:R, :],
                                             ALU.mult, ALU.add).then_inc(s["o_ready"].sem, 1)
                if t == 0:
                    save_cache(dve, ahead)
                    select_G(dve, ahead)
                elif t == 1:
                    low(dve, second, 0)
                elif t == 2:
                    silu_conv(dve, ahead, 2)
                dve.wait_ge(*s["rstd_ready"].done(h, t))
                dve.wait_ge(*s["gT_psum"].before(h, t))
                dve.tensor_scalar(g[0:R, :], (o if t else o_a)[0:R, :], sm[0:R, 2:3], None, ALU.mult).then_inc(s["g_ready"].sem, 1)
                for tt in ([t - 1] if t else []) + ([t] if t == T - 1 else []):
                    dve.wait_ge(*s["gT_psum"].done(h, tt))
                    dve.scalar_tensor_tensor(M["gT"][:, bass.ds(h + 8, 1), cols(tt)].rearrange("p a t -> p (a t)"), gT_bank(tt),
                                             M["vec"][:, bass.ds(h + 56, 1)], zs[:, cols(tt)], ALU.mult, ALU.mult
                                             ).then_inc(s["gT_copied"].sem, 1)

        def pool_turn(pool, h):
            pool.wait_ge(*s["ss_ready"].done(h, 0))
            pool.sem_inc(M.passed, 1)
            pool.tensor_scalar(ms[:], ss[:], 0.25, EPS, ALU.mult, ALU.add).then_inc(s["ms_ready"].sem, 1)
            pool.wait_ge(*s["ms_ready"].done(h, 0))
            pool.tensor_tensor(rn[:], ms[:], mh[:], ALU.pow).then_inc(s["rn_ready"].sem, 1)
            pool.wait_ge(*s["A_ready"].done(h, 0))
            for n in range(NL):
                if n >= 2:
                    pool.wait_ge(*s["Q_psum"].done(h, 2 * n - 3))
                lev = M.c("levels")[:, (n + 1) * P:(n + 2) * P]
                for t in range(T if n < NL - 1 else PT):
                    R = rows(t)
                    last = pool.tensor_tensor(tiles(ML[:, n % 2, :], t), tiles(AT, t), lev[0:R, 0:R], ALU.mult)
                last.then_inc(s["level_ready"].sem, 1)
            for t in range(T):
                R = rows(t)
                pool.wait_ge(*s["squared"].done(h, t))
                pool.sem_inc(M.passed, 1)
                pool.tensor_scalar(sm[0:R, 1:2], sm[0:R, 0:1], 1.0 / P, EPS, ALU.mult, ALU.add).then_inc(s["mean_ready"].sem, 1)
                pool.wait_ge(*s["mean_ready"].done(h, t))
                pool.tensor_tensor(sm[0:R, 2:3], sm[0:R, 1:2], M.c("half", R), ALU.pow).then_inc(s["rstd_ready"].sem, 1)

        nc.all_engine_barrier()
        with nc.Block() as block:

            @block.sync
            def _(sp):
                def load(h, ct):
                    sp.dma_start(wraw[:, ct], w_in[:, :, bass.ds(h * P + sec[ct], P)]).then_inc(s[f"w_loaded{ct}"].sem, 16)
                for ct in range(4):
                    sp.sem_inc(s[f"w_loaded{ct}"].sem, 16)
                with sp.Fori(1, H) as h:
                    for ct in range(4):
                        sp.wait_ge(*s["w_split_low"].done(h - 1, ct))
                        load(h, ct)
                sp.wait_ge(*s["w_split_low"].done(H - 1, 3))
                first.start(sp)
                sp.wait_ge(*s["prompt_stored"].before(H, 0))
                sp.wait_ge(*s["sample_stored"].before(H, 0))
                first.finish(sp)
                for i, name in enumerate(("pconv", "sconv")):
                    sp.wait_ge(*cacheT_copied.done(0, i))
                    sp.dma_start(OUT[name][0, 0].rearrange("r (c p) -> (r c) p", p=P), cr[:, i, :]).then_inc(cache_stored.sem, 16)
                sp.wait_ge(*cache_stored.done(0, 31))

            @block.gpsimd
            def _(pool):
                pool.memset(mh[:], -0.5)
                with pool.Fori(0, H) as h:
                    pool_turn(pool, h)

            @block.tensor
            def _(pe):
                project(pe, 0, 0, 8 * KT)
                pe_turn(pe, 0, 1, None)
                with pe.Fori(1, H - 1) as h:
                    pe_turn(pe, h, h + 1, h - 1)
                pe_turn(pe, H - 1, None, H - 2)
                turn_g(pe, H - 1, T - 1)
                pe.wait_ge(*s["cache_saved"].before(H, 0))
                for i in range(2):
                    pe.transpose(PS[i][0:72, 0:P], newc[:, i, :], M.c("ident", P, P)).then_inc(cacheT_psum.sem, 1)

            @block.scalar
            def _(act):
                high(act, 0, 0)
                high(act, 0, 1)
                for n in range(8):
                    take_projection(act, 0, n)
                    if n in (1, 3):
                        high(act, 0, n // 2 + 2)
                    if n == 5:
                        high(act, 1, 0)
                    if n in (3, 5, 7):
                        tanh_conv(act, 0, (n - 3) // 2)
                with act.Fori(0, H - 2) as h:
                    act_turn(act, h, h + 1, h + 2)
                act_turn(act, H - 2, H - 1, None)
                act_turn(act, H - 1, None, None)

            @block.vector
            def _(dve):
                dve.memset(tk[:], 0.0)
                dve.memset(pj[:, :, 0:3], 0.0).then_inc(cleared.sem, 1)
                select_G(dve, 0)
                low(dve, 0, 0)
                low(dve, 0, 1)
                for ct in range(3):
                    if ct < 2:
                        low(dve, 0, ct + 2)
                    convolve(dve, 0, ct)
                    if ct:
                        silu_conv(dve, 0, ct - 1)
                save_cache(dve, 0)
                silu_conv(dve, 0, 2)
                low(dve, 1, 0)
                with dve.Fori(0, H - 2) as h:
                    dve_turn(dve, h, h + 1, h + 2)
                dve_turn(dve, H - 2, H - 1, None)
                dve_turn(dve, H - 1, None, None)
                for i in range(2):
                    dve.wait_ge(*cacheT_psum.done(0, i))
                    dve.tensor_copy(cr[:, i, :], PS[i][0:72, 0:P]).then_inc(cacheT_copied.sem, 1)


def cacheT_of(M, h, ct):
    return M["cacheT"][:].rearrange("p (r c) -> p r c", r=3)[:, :, bass.ds(h + 8 * ct, 1)].rearrange("p r a -> p (r a)")


def new_cache_of(newc, i, h, ct):
    return newc[:, i, :].rearrange("p (r c) -> p r c", r=3)[:, :, bass.ds(h + 8 * ct, 1)].rearrange("p r a -> p (r a)")


def output(nc, M, IN, OUT, l):
    K = 16
    TURNS = D // (2 * P)
    with Phase(nc, f"output{l}", first=1) as ph:
        sb, sig = ph.sb, ph.counter
        raw = sb("w_out", [P, K, P])
        first_tile = M["x"][:].rearrange("p t d -> p (t d)")[:, 0:K * P].rearrange("p (k c) -> p k c", k=K)
        wh, wl = sb("w_high", [P, 2, K, P], F32R), sb("w_low", [P, 2, K, P], F32R)
        gh, gl = sb("gT_high", [P, K, TOK], F32R), sb("gT_low", [P, K, TOK], F32R)
        free = M["gT"][:].rearrange("p k t -> p (k t)")
        y = free[:, 0:T * D].rearrange("p (t d) -> p t d", t=T)
        yT = free[:, T * D:T * D + 2 * TOK].rearrange("p (a t) -> p a t", a=2)
        sq = free[:, T * D + 2 * TOK:T * D + 2 * TOK + T * P].rearrange("p (t d) -> p t d", t=T)
        at = T * D + 2 * TOK + T * P
        gate = free[:, at:at + 2 * D].rearrange("p (a c) -> p a c", a=8)
        gp, sel = sb("g_post_rows", [2, 4, 2 * P]), sb("cond_select", [2, 2, P])
        ss = sb("ss", [P, T, D // P])
        tot, ms, rs, mh = (sb(n, [P, T]) for n in ("ss_total", "ms", "rs", "minus_half"))
        loaded, gpl = [sig(f"w_out_loaded{c}", 32) for c in range(4)], sig("g_post_loaded", 32)
        sel_ready, gate_psum, gate_ready = sig("gates_scaled", 2), sig("gate_psum", 4), sig("gate_copied", 4)
        g_hi, g_lo, w_hi, w_lo = sig("g_high", K), sig("g_low", K), sig("w_high", 8), sig("w_low", 8)
        y_psum, yT_copied = sig("y_psum", 4, lead=4), sig("yT_copied", 4, lead=4)
        tok_psum = sig("y_tokens_psum", 2, lead=2)
        squared, y_gated = sig("squared", 2), sig("y_gated", 2)
        cleared, added, mean_ready, rstd_ready, x_ready = sig("cleared"), sig("added"), sig("mean_ready"), sig("rstd_ready"), sig("x_ready", T)
        stored, x_loaded = sig("x_stored", 16 * T), sig("x_loaded", 32)
        PS = M["ps"]
        X_P, X_S = (IN["x_prompt"], IN["x_sample"]) if l == 0 else (OUT["y_p"], OUT["y_s"])
        w_src = IN[("w_out_even", "w_out_odd")[l]][0].rearrange("(k p) n -> p k n", p=P)
        nc.all_engine_barrier()
        with nc.Block() as block:

            @block.sync
            def _(sp):
                def load(p, j):
                    for c in range(4):
                        sp.dma_start(raw[:, 4 * c:4 * c + 4, :], w_src[:, 4 * c:4 * c + 4, bass.ds(p * (2 * P) + j * P, P)]
                                     ).then_inc(loaded[c].sem, 16)

                def turn(p, more):
                    sp.wait_ge(*w_lo.done(p, 3))
                    load(p, 1)
                    if more:
                        sp.wait_ge(*w_lo.done(p, 7))
                        load(p + 1, 0)

                for c in range(4):
                    sp.sem_inc(loaded[c].sem, 16)
                for i in range(2):
                    sp.dma_start(gp[i:i + 1], IN["g_post"][l:l + 1, :].rearrange("a (b c) -> a b c", b=4)).then_inc(gpl.sem, 16)
                turn(0, True)
                sp.dma_start(M["x"][:, 0:PT, :], X_P[0].rearrange("(t p) d -> p t d", p=P)).then_inc(x_loaded.sem, 16)
                sp.dma_start(M["x"][0:DEC, PT, :], X_S[0]).then_inc(x_loaded.sem, 16)
                with sp.Fori(1, TURNS - 1) as p:
                    turn(p, True)
                turn(TURNS - 1, False)
                if l == 1:
                    for t in range(T):
                        sp.wait_ge(*x_ready.done(0, t))
                        out = OUT["y_p"][0, cols(t), :] if t < PT else OUT["y_s"][0]
                        sp.dma_start(out, M["x"][0:rows(t), t, :]).then_inc(stored.sem, 16)
                    sp.wait_ge(*stored.done(0, 16 * T - 1))

            @block.gpsimd
            def _(pool):
                pool.memset(mh[:], -0.5)
                pool.wait_ge(*added.done(0, 0))
                pool.tensor_scalar(ms[:], tot[:], 1.0 / D, EPS, ALU.mult, ALU.add).then_inc(mean_ready.sem, 1)
                pool.wait_ge(*mean_ready.done(0, 0))
                pool.tensor_tensor(rs[:], ms[:], mh[:], ALU.pow).then_inc(rstd_ready.sem, 1)

            @block.tensor
            def _(pe):
                def multiply(p, j, half):
                    i = 2 * j + half
                    to = slice(half * HALF, (half + 1) * HALF)
                    pe.wait_ge(*yT_copied.done(p - 1, i))
                    for k in range(K):
                        if half == 0 and k % 4 == 0:
                            pe.wait_ge(*w_lo.done(p, 4 * j + k // 4))
                        if half == 0 and j == 0:
                            pe.wait_ge(*g_lo.done(0, k))
                        last = split_matmul(pe, PS[i][:, 0:HALF], (wh[:, j, k, :], wl[:, j, k, :]), (gh[:, k, to], gl[:, k, to]),
                                            k == 0, k == K - 1)
                    last.then_inc(y_psum.sem, 1)

                def turn_y(p, j):
                    pe.wait_ge(*yT_copied.done(p, 2 * j + 1))
                    pe.wait_ge(*squared.before(p, j))
                    pe.wait_ge(*y_gated.before(p, j))
                    pe.sem_inc(M.passed, 1)
                    for t in range(T):
                        out = PS[4 + 2 * j][:, t * P:(t + 1) * P] if t < PT else PS[5 + 2 * j][0:DEC, 0:P]
                        last = pe.transpose(out, yT[:, j, cols(t)], M.c("ident", P, P))
                    last.then_inc(tok_psum.sem, 1)

                def turn(p, more):
                    multiply(p, 0, 1)
                    multiply(p, 1, 0)
                    turn_y(p, 0)
                    multiply(p, 1, 1)
                    if more:
                        multiply(p + 1, 0, 0)
                    turn_y(p, 1)

                pe.wait_ge(*sel_ready.done(0, 1))
                for m in range(2):
                    for half in range(2):
                        pe.matmul(PS[4 + 2 * m + half][:, :], sel[:, m, :], M["gate"][:, l, half * 512:(half + 1) * 512],
                                  start=True, stop=True).then_inc(gate_psum.sem, 1)
                multiply(0, 0, 0)
                pe.wait_ge(*gate_ready.done(0, 3))
                with pe.Fori(0, TURNS - 1) as p:
                    turn(p, True)
                turn(TURNS - 1, False)

            @block.scalar
            def _(act):
                def high(p, j, c, raw=raw):
                    act.wait_ge(*loaded[c].done(p, 16 * j + 15))
                    if c == 0:
                        act.wait_ge(*(y_psum.before(p, 0) if j else y_psum.done(p - 1, 1)))
                    act.activation(wh[:, j, 4 * c:4 * c + 4, :], raw[:, 4 * c:4 * c + 4, :], ACT.Copy).then_inc(w_hi.sem, 1)

                def take(p, j, half):
                    act.wait_ge(*y_psum.done(p, 2 * j + half))
                    act.wait_ge(*tok_psum.done(p - 1, j))
                    act.activation(yT[:, j, half * HALF:(half + 1) * HALF], PS[2 * j + half][:, 0:HALF], ACT.Copy).then_inc(yT_copied.sem, 1)

                def squares(p, j):
                    act.wait_ge(*tok_psum.done(p, j))
                    act.wait_ge(*squared.before(p, j))
                    for t in range(T):
                        R = rows(t)
                        src = PS[4 + 2 * j][:, t * P:(t + 1) * P] if t < PT else PS[5 + 2 * j][0:DEC, 0:P]
                        last = act.activation(sq[0:R, t, :], src, ACT.Square, accum_out=ss[0:R, t, bass.ds(2 * p + j, 1)])
                    last.then_inc(squared.sem, 1)

                def turn(p, more):
                    for c in range(4):
                        high(p, 1, c)
                    take(p, 0, 1)
                    take(p, 1, 0)
                    squares(p, 0)
                    if more:
                        for c in range(4):
                            high(p + 1, 0, c)
                    take(p, 1, 1)
                    if more:
                        take(p + 1, 0, 0)
                    squares(p, 1)

                for c in range(4):
                    high(0, 0, c, first_tile)
                    for k in range(4 * c, 4 * c + 4):
                        act.activation(gh[:, k, :], M["gT"][:, k, :], ACT.Copy).then_inc(g_hi.sem, 1)
                act.wait_ge(*g_lo.done(0, K - 1))
                for n in range(4):
                    m, half = divmod(n, 2)
                    act.wait_ge(*gate_psum.done(0, n))
                    act.activation(gate[:, 4 * m + 2 * half:4 * m + 2 * half + 2, :], PS[4 + n][:, :].rearrange("p (a c) -> p a c", a=2),
                                   ACT.Copy).then_inc(gate_ready.sem, 1)
                act.wait_ge(*cleared.done(0, 0))
                take(0, 0, 0)
                with act.Fori(0, TURNS - 1) as p:
                    turn(p, True)
                turn(TURNS - 1, False)

            @block.vector
            def _(dve):
                def low(p, j, c, raw=raw):
                    dve.wait_ge(*w_hi.done(p, 4 * j + c))
                    dve.tensor_tensor(wl[:, j, 4 * c:4 * c + 4, :], raw[:, 4 * c:4 * c + 4, :], wh[:, j, 4 * c:4 * c + 4, :].bitcast(F32), ALU.subtract
                                      ).then_inc(w_lo.sem, 1)

                def gated(p, j):
                    at = slice(j * P, (j + 1) * P)
                    ch = bass.ds(p * (2 * P) + j * P, P)
                    dve.wait_ge(*tok_psum.done(p, j))
                    dve.wait_ge(*squared.done(p, j))
                    dve.tensor_tensor(y[:, 0:PT, ch], PS[4 + 2 * j][:, :].rearrange("p (t c) -> p t c", t=PT),
                                      gate[:, bass.ds(p, 1), at].broadcast_to([P, PT, P]), ALU.mult)
                    dve.tensor_tensor(y[0:DEC, PT, ch], PS[5 + 2 * j][0:DEC, 0:P],
                                      gate[0:DEC, bass.ds(p + 4, 1), at].rearrange("p a c -> p (a c)"), ALU.mult).then_inc(y_gated.sem, 1)

                def turn(p, more):
                    for c in range(4):
                        low(p, 1, c)
                    gated(p, 0)
                    if more:
                        for c in range(4):
                            low(p + 1, 0, c)
                    gated(p, 1)

                dve.memset(ss[:], 0.0).then_inc(cleared.sem, 1)
                dve.wait_ge(*gpl.done(0, 31))
                gl_rows = M["gate"][:, l, :].rearrange("m (b c) -> m b c", b=4)
                dve.tensor_tensor(gl_rows, gl_rows, gp[:], ALU.mult).then_inc(sel_ready.sem, 1)
                for m in range(2):
                    last = dve.tensor_scalar(sel[:, m, :], M.c("ones", 2), M.c("ident", 2)[:, m:m + 1], None, ALU.mult)
                last.then_inc(sel_ready.sem, 1)
                for c in range(4):
                    low(0, 0, c, first_tile)
                    for k in range(4 * c, 4 * c + 4):
                        dve.wait_ge(*g_hi.done(0, k))
                        dve.tensor_tensor(gl[:, k, :], M["gT"][:, k, :], gh[:, k, :].bitcast(F32), ALU.subtract).then_inc(g_lo.sem, 1)
                dve.wait_ge(*gate_ready.done(0, 3))
                dve.wait_ge(*g_lo.done(0, K - 1))
                with dve.Fori(0, TURNS - 1) as p:
                    turn(p, True)
                turn(TURNS - 1, False)
                dve.tensor_reduce(tot[:], ss[:], AX.X, ALU.add).then_inc(added.sem, 1)
                dve.wait_ge(*rstd_ready.done(0, 0))
                dve.wait_ge(*y_gated.done(TURNS - 1, 1))
                dve.wait_ge(*x_loaded.done(0, 31))
                for t in range(T):
                    R = rows(t)
                    dve.scalar_tensor_tensor(M["x"][0:R, t, :], y[0:R, t, :], rs[0:R, t:t + 1], M["x"][0:R, t, :], ALU.mult, ALU.add
                                             ).then_inc(x_ready.sem, 1)


class Memory(dict):

    def c(self, name, n=P, m=None):
        a, b = self.at[name]
        return self["const"][0:n, a:(b if m is None else a + m)]


def build(nc, IN, OUT, at):
    with ExitStack() as ctx:
        def sb(name, shape):
            return ctx.enter_context(nc.sbuf_tensor(name, shape, F32))

        M = Memory()
        M.at = at
        M.passed = ctx.enter_context(nc.semaphore("passed"))
        M.const_loaded = ctx.enter_context(nc.semaphore("const_loaded"))
        M["const"] = sb("const", [P, max(b for _, b in at.values())])
        M["x"] = sb("x", [P, T, D])
        M["gT"] = sb("gT", [P, 16, TOK])
        M["vec"], M["conv"] = sb("vectors", [P, 68]), sb("conv_taps", [P, 96])
        M["modT"], M["gate"] = sb("modT", [P, 2, 16, 2]), sb("gate", [2, 2, D])
        M["ps"] = [ctx.enter_context(nc.psum_tensor(f"bank{i}", [P, 512], F32)) for i in range(8)]
        setup(nc, M, IN, OUT)
        with ExitStack() as layer:
            for name in ("hT_high", "hT_low"):
                M[name] = layer.enter_context(nc.sbuf_tensor(name, [P, KT, TOK], F32R))
            for name, shape in (("negM", [P, EVEN_H, TOK]), ("ucol", [P, T, EVEN_H]), ("mcols", [P, 4, T, EVEN_H])):
                M[name] = layer.enter_context(nc.sbuf_tensor(name, shape, F32))
            even_gates(nc, M, IN, OUT)
            heads(nc, M, IN, OUT, "A")
            heads(nc, M, IN, OUT, "B")
        output(nc, M, IN, OUT, 0)
        with ExitStack() as layer:
            for name in ("hT_high", "hT_low"):
                M[name] = layer.enter_context(nc.sbuf_tensor(name + "1", [P, KT, TOK], F32R))
            for name, shape in (("a1T", [RANK, TOK]), ("grow", [GDN_H, 2, TOK]), ("Gcol", [P, T, GDN_H]), ("gcols", [P, 5, T, GDN_H]),
                                ("cacheT", [P, 72])):
                M[name] = layer.enter_context(nc.sbuf_tensor(name, shape, F32))
            odd_gates(nc, M, IN, OUT)
            heads(nc, M, IN, OUT, "C")
            gdn_heads(nc, M, IN, OUT)
        output(nc, M, IN, OUT, 1)


_OUTS = [("y_p", (1, SEQ, D)), ("y_s", (1, DEC, D))] + [
    (side + n, (1, 1) + shape) for side in "ps" for n, shape in (
        ("C", (4, 256, 256)), ("n", (4, 256)), ("m", (4,)), ("ret", (4, 256, 256)), ("gla", (4, 128, 256)),
        ("gdn", (8, 128, 128)), ("conv", (3, 3072)))]
_INS = ["x_prompt", "x_sample", "c_prompt", "c_sample", "state_mlstm_C", "state_mlstm_n", "state_mlstm_m", "state_ret",
        "state_gla", "state_gdn", "cache_gdn_conv", "w_ada", "b_ada", "g_pre", "g_post", "w_in_even", "b_if_even",
        "g_head_even", "w_out_even", "w_in_odd", "w_a2", "b_a2", "conv_w", "a_log", "dt_bias", "g_head_odd", "w_out_odd"]


def kernel(**inputs):
    import concourse.bacc as bacc
    from concourse.bass_utils import run_bass_kernel_spmd

    nc = bacc.Bacc("TRN2", target_bir_lowering=False, num_devices=1)
    const, at = shape_constants()
    arrays, IN, OUT = {"in_const": const}, {}, {}
    for name in _INS:
        arrays["in_" + name] = np.ascontiguousarray(inputs[name])
    for name, a in arrays.items():
        IN[name[3:]] = nc.dram_tensor(name, a.shape, F32, kind="ExternalInput").ap()
    for name, shape in _OUTS:
        OUT[name] = nc.dram_tensor("out_" + name, shape, F32, kind="ExternalOutput").ap()
    build(nc, IN, OUT, at)
    r = run_bass_kernel_spmd(nc, [arrays], core_ids=[0])
    return tuple(r.results[0]["out_" + name] for name, _ in _OUTS)
```
